# Optimizing a Trainium2 kernel written in Bass

```python
import math
import jax, jax.numpy as jnp
from jax import lax
import numpy as np

D_MODEL = 1024
BATCH = 1
SEQ = 256
DEPTH = 2

HEAD_DIM = 64
DIFF_HEADS = 6
DIFF_QK_DIM = HEAD_DIM // 2
RWKV_HEADS = 6
FOX_HEADS = 4
DIFF_WIDTH = DIFF_HEADS * HEAD_DIM
RWKV_WIDTH = RWKV_HEADS * HEAD_DIM
FOX_WIDTH = FOX_HEADS * HEAD_DIM
MIX_WIDTH = DIFF_WIDTH + RWKV_WIDTH + FOX_WIDTH
DECAY_LORA = 64
AAA_LORA = 64
GATE_LORA = 128
DIFF_COLS = 3 * DIFF_WIDTH
RWKV_COLS = 3 * RWKV_WIDTH + DECAY_LORA + AAA_LORA + GATE_LORA
FOX_COLS = 3 * FOX_WIDTH + FOX_HEADS
IN_COLS = DIFF_COLS + RWKV_COLS + FOX_COLS
QB = 128

PEER_HEADS = 8
PEER_NKEYS = 128
PEER_EXPERTS = PEER_NKEYS * PEER_NKEYS
PEER_TOPK = 16
PEER_QDIM = 256
PEER_HALF = PEER_QDIM // 2
PEER_CHUNK = 128

RMS_EPS = 1e-6
RWKV_LN_EPS = 64e-5

kernel_name = 'hymba_diff_rwkv7_fox_peer_adaln'

def _rmsnorm(x, g):
    xf = x.astype(jnp.float32)
    y = xf * lax.rsqrt(jnp.mean(xf * xf, axis=-1, keepdims=True) + RMS_EPS)
    return (y * g.astype(jnp.float32)).astype(x.dtype)

def _heads(t, n_heads):
    B, S, _ = t.shape
    return t.reshape(B, S, n_heads, -1).transpose(0, 2, 1, 3)

def _merge_blocks(o):
    nb, B, H, qb, d = o.shape
    return o.transpose(1, 0, 3, 2, 4).reshape(B, nb * qb, H * d)

def _causal_mask(q0, S):
    qpos = q0 + jnp.arange(QB)
    kpos = jnp.arange(S)
    return qpos[:, None] >= kpos[None, :]

def diff_attention(cols, lam_params, subln_g, layer_idx):
    B, S, _ = cols.shape
    q = cols[..., :DIFF_WIDTH].reshape(B, S, DIFF_HEADS, 2, DIFF_QK_DIM)
    k = cols[..., DIFF_WIDTH:2 * DIFF_WIDTH].reshape(B, S, DIFF_HEADS, 2, DIFF_QK_DIM)
    v = _heads(cols[..., 2 * DIFF_WIDTH:], DIFF_HEADS)
    q1 = q[:, :, :, 0].transpose(0, 2, 1, 3)
    q2 = q[:, :, :, 1].transpose(0, 2, 1, 3)
    k1 = k[:, :, :, 0].transpose(0, 2, 1, 3)
    k2 = k[:, :, :, 1].transpose(0, 2, 1, 3)
    lam_init = 0.8 - 0.6 * math.exp(-0.3 * layer_idx)
    lp = lam_params.astype(jnp.float32)
    lam = jnp.exp(jnp.dot(lp[0], lp[1])) - jnp.exp(jnp.dot(lp[2], lp[3])) + lam_init
    scale = DIFF_QK_DIM ** -0.5

    def block(i):
        q0 = i * QB
        qa = lax.dynamic_slice_in_dim(q1, q0, QB, axis=2)
        qb = lax.dynamic_slice_in_dim(q2, q0, QB, axis=2)
        mask = _causal_mask(q0, S)
        s1 = jnp.einsum('bhqd,bhkd->bhqk', qa, k1).astype(jnp.float32) * scale
        s2 = jnp.einsum('bhqd,bhkd->bhqk', qb, k2).astype(jnp.float32) * scale
        p = (jax.nn.softmax(jnp.where(mask, s1, -jnp.inf), axis=-1)
             - lam * jax.nn.softmax(jnp.where(mask, s2, -jnp.inf), axis=-1))
        return jnp.einsum('bhqk,bhkd->bhqd', p.astype(v.dtype), v)

    o = lax.map(block, jnp.arange(S // QB))
    o = _rmsnorm(o, subln_g) * (1.0 - lam_init)
    return _merge_blocks(o)

def rwkv7_time_mix(cols, mu, w0, w2, a0, a2, g2, k_k, k_a, r_k, ln_g, ln_b):
    B, S, _ = cols.shape
    W = RWKV_WIDTH
    prev = jnp.pad(cols, ((0, 0), (1, 0), (0, 0)))[:, :-1]
    cols = cols + (prev - cols) * mu
    o1 = 3 * W + DECAY_LORA
    o2 = o1 + AAA_LORA
    r = cols[..., :W]
    k = cols[..., W:2 * W]
    v = cols[..., 2 * W:3 * W]
    xw = cols[..., 3 * W:o1]
    xa = cols[..., o1:o2]
    xg = cols[..., o2:]
    w = -jax.nn.softplus(-(w0 + jnp.tanh(xw) @ w2)) - 0.5
    decay = jnp.exp(-jnp.exp(w.astype(jnp.float32)))
    a = jax.nn.sigmoid(a0 + xa @ a2)
    g = jax.nn.sigmoid(xg) @ g2

    def hs(t):
        return t.reshape(B, S, RWKV_HEADS, HEAD_DIM).astype(jnp.float32)

    kk = hs(k * k_k)
    kk = kk / jnp.maximum(jnp.sqrt(jnp.sum(kk * kk, axis=-1, keepdims=True)), 1e-12)
    k = k * (1.0 + (a - 1.0) * k_a)
    r_h, k_h, v_h, w_h, a_h = hs(r), hs(k), hs(v), hs(decay), hs(a)
    a_vec = -kk
    b_vec = kk * a_h

    def step(state, inp):
        r_t, w_t, k_t, v_t, av, bv = inp
        sa = jnp.einsum('bhvk,bhk->bhv', state, av)
        state = (state * w_t[:, :, None, :] + sa[..., None] * bv[:, :, None, :]
                 + v_t[..., None] * k_t[:, :, None, :])
        y = jnp.einsum('bhvk,bhk->bhv', state, r_t)
        return state, y

    tm = lambda t: jnp.moveaxis(t, 1, 0)
    s0 = jnp.zeros((B, RWKV_HEADS, HEAD_DIM, HEAD_DIM), jnp.float32)
    _, y = lax.scan(step, s0, (tm(r_h), tm(w_h), tm(k_h), tm(v_h), tm(a_vec), tm(b_vec)))
    y = jnp.moveaxis(y, 0, 1)
    mean = jnp.mean(y, axis=-1, keepdims=True)
    var = jnp.mean((y - mean) ** 2, axis=-1, keepdims=True)
    y = ((y - mean) * lax.rsqrt(var + RWKV_LN_EPS)).reshape(B, S, W)
    y = y * ln_g.astype(jnp.float32) + ln_b.astype(jnp.float32)
    bonus = jnp.sum(r_h * k_h * r_k.astype(jnp.float32), axis=-1, keepdims=True) * v_h
    y = (y + bonus.reshape(B, S, W)) * g.astype(jnp.float32)
    return y.astype(cols.dtype)

def forgetting_attention(cols, b_f):
    B, S, _ = cols.shape
    q = _heads(cols[..., :FOX_WIDTH], FOX_HEADS)
    k = _heads(cols[..., FOX_WIDTH:2 * FOX_WIDTH], FOX_HEADS)
    v = _heads(cols[..., 2 * FOX_WIDTH:3 * FOX_WIDTH], FOX_HEADS)
    f_logit = cols[..., 3 * FOX_WIDTH:]
    logf = jax.nn.log_sigmoid(f_logit.astype(jnp.float32) + b_f.astype(jnp.float32))
    cum = jnp.cumsum(logf, axis=1).transpose(0, 2, 1)
    scale = HEAD_DIM ** -0.5

    def block(i):
        q0 = i * QB
        qb = lax.dynamic_slice_in_dim(q, q0, QB, axis=2)
        cq = lax.dynamic_slice_in_dim(cum, q0, QB, axis=2)
        mask = _causal_mask(q0, S)
        logits = (jnp.einsum('bhqd,bhkd->bhqk', qb, k).astype(jnp.float32) * scale
                  + cq[..., :, None] - cum[..., None, :])
        p = jax.nn.softmax(jnp.where(mask, logits, -jnp.inf), axis=-1)
        return jnp.einsum('bhqk,bhkd->bhqd', p.astype(v.dtype), v)

    return _merge_blocks(lax.map(block, jnp.arange(S // QB)))

def peer_ffn(h, wq, subkeys, u_tab, v_tab):
    B, S, D = h.shape
    h_chunks = h.reshape(B * S // PEER_CHUNK, PEER_CHUNK, D)
    kk2 = PEER_TOPK * PEER_TOPK

    def chunk(hc):
        q = (hc @ wq).reshape(PEER_CHUNK, PEER_HEADS, 2, PEER_HALF)
        s = jnp.einsum('thcd,hcnd->thcn', q, subkeys).astype(jnp.float32)
        sv, si = lax.top_k(s, PEER_TOPK)
        cand = (sv[:, :, 0, :, None] + sv[:, :, 1, None, :]).reshape(PEER_CHUNK, PEER_HEADS, kk2)
        cidx = (si[:, :, 0, :, None] * PEER_NKEYS + si[:, :, 1, None, :]).reshape(PEER_CHUNK, PEER_HEADS, kk2)
        fv, fpos = lax.top_k(cand, PEER_TOPK)
        eidx = jnp.take_along_axis(cidx, fpos, axis=-1)
        gate = jax.nn.softmax(fv, axis=-1)
        u = jnp.take(u_tab, eidx, axis=0)
        act = jnp.einsum('thkd,td->thk', u, hc).astype(jnp.float32)
        coef = (gate * jax.nn.gelu(act, approximate=False)).astype(hc.dtype)
        vsel = jnp.take(v_tab, eidx, axis=0)
        return jnp.einsum('thk,thkd->td', coef, vsel)

    return lax.map(chunk, h_chunks).reshape(B, S, D)

def setup_inputs(seed: int = 0) -> dict:
    key = jax.random.key(seed)
    ks = jax.random.split(key, 32)
    L, D = DEPTH, D_MODEL
    f32 = jnp.float32

    def nrm(k, shape, s):
        return jax.random.normal(k, shape, f32) * s

    return {
        'x': nrm(ks[0], (BATCH, SEQ, D), 1.0),
        'c': nrm(ks[1], (BATCH, D), 1.0),
        'norm_mix_g': 1.0 + nrm(ks[2], (L, D), 0.02),
        'norm_ffn_g': 1.0 + nrm(ks[3], (L, D), 0.02),
        'final_norm_g': 1.0 + nrm(ks[4], (D,), 0.02),
        'ada_w': nrm(ks[5], (L, D, 6 * D), 0.5 * D ** -0.5),
        'ada_b': nrm(ks[6], (L, 6 * D), 0.02),
        'w_in': nrm(ks[7], (L, D, IN_COLS), D ** -0.5),
        'w_out': nrm(ks[8], (L, MIX_WIDTH, D), MIX_WIDTH ** -0.5),
        'dif_lam': nrm(ks[9], (L, 4, DIFF_QK_DIM), 0.1),
        'dif_subln_g': 1.0 + nrm(ks[10], (L, 2 * DIFF_QK_DIM), 0.02),
        'rw_mu': jax.random.uniform(ks[11], (L, RWKV_COLS), f32, 0.0, 1.0),
        'rw_w0': jax.random.uniform(ks[12], (L, RWKV_WIDTH), f32, -6.5, -1.5),
        'rw_w2': nrm(ks[13], (L, DECAY_LORA, RWKV_WIDTH), 0.1),
        'rw_a0': nrm(ks[14], (L, RWKV_WIDTH), 0.1),
        'rw_a2': nrm(ks[15], (L, AAA_LORA, RWKV_WIDTH), 0.1),
        'rw_g2': nrm(ks[16], (L, GATE_LORA, RWKV_WIDTH), GATE_LORA ** -0.5),
        'rw_kk': 1.0 + nrm(ks[17], (L, RWKV_WIDTH), 0.1),
        'rw_ka': 1.0 + nrm(ks[18], (L, RWKV_WIDTH), 0.1),
        'rw_rk': nrm(ks[19], (L, RWKV_HEADS, HEAD_DIM), 0.1),
        'rw_ln_g': 1.0 + nrm(ks[20], (L, RWKV_WIDTH), 0.02),
        'rw_ln_b': nrm(ks[21], (L, RWKV_WIDTH), 0.02),
        'fox_bf': 1.0 + nrm(ks[22], (L, FOX_HEADS), 0.5),
        'peer_wq': nrm(ks[23], (L, D, PEER_HEADS * PEER_QDIM), D ** -0.5),
        'peer_subkeys': nrm(ks[24], (L, PEER_HEADS, 2, PEER_NKEYS, PEER_HALF), PEER_HALF ** -0.5),
        'peer_u': nrm(ks[25], (L, PEER_EXPERTS, D), D ** -0.5),
        'peer_v': nrm(ks[26], (L, PEER_EXPERTS, D), 1.0),
    }

def reference(x, c, norm_mix_g, norm_ffn_g, final_norm_g, ada_w, ada_b, w_in, w_out,
              dif_lam, dif_subln_g, rw_mu, rw_w0, rw_w2, rw_a0, rw_a2, rw_g2, rw_kk, rw_ka,
              rw_rk, rw_ln_g, rw_ln_b, fox_bf, peer_wq, peer_subkeys, peer_u, peer_v):
    c_act = jax.nn.silu(c)
    for l in range(DEPTH):
        mod = c_act @ ada_w[l] + ada_b[l]
        sh_m, sc_m, g_m, sh_f, sc_f, g_f = jnp.split(mod, 6, axis=-1)
        h = _rmsnorm(x, norm_mix_g[l]) * (1.0 + sc_m[:, None]) + sh_m[:, None]
        cols = h @ w_in[l]
        y_a = diff_attention(cols[..., :DIFF_COLS], dif_lam[l], dif_subln_g[l], l)
        y_b = rwkv7_time_mix(cols[..., DIFF_COLS:DIFF_COLS + RWKV_COLS], rw_mu[l], rw_w0[l],
                             rw_w2[l], rw_a0[l], rw_a2[l], rw_g2[l], rw_kk[l], rw_ka[l],
                             rw_rk[l], rw_ln_g[l], rw_ln_b[l])
        y_c = forgetting_attention(cols[..., DIFF_COLS + RWKV_COLS:], fox_bf[l])
        mix = jnp.concatenate([y_a, y_b, y_c], axis=-1) @ w_out[l]
        x = x + g_m[:, None] * mix
        h = _rmsnorm(x, norm_ffn_g[l]) * (1.0 + sc_f[:, None]) + sh_f[:, None]
        x = x + g_f[:, None] * peer_ffn(h, peer_wq[l], peer_subkeys[l], peer_u[l], peer_v[l])
    return _rmsnorm(x, final_norm_g)


_drawn_inputs = setup_inputs


def setup_inputs(seed=0):
    import zlib

    import numpy as np

    out = dict(_drawn_inputs(seed))
    spreads = {}
    factors = {'final_norm_g': 2.878,
     'dif_subln_g': 2.869,
     'rw_a0': 2.749,
     'rw_ln_g': 3.733,
     'rw_ln_b': 3.861}
    for name, (base, spread) in spreads.items():
        noise = np.random.default_rng([zlib.crc32(name.encode()), seed]).standard_normal(out[name].shape)
        drawn = base * np.exp(spread * noise) if base else spread * noise
        out[name] = __import__('jax').numpy.asarray(drawn.astype(out[name].dtype))
    for name, factor in factors.items():
        out[name] = (out[name] * factor).astype(out[name].dtype)
    return out
```

```python
import math
from contextlib import ExitStack

import concourse.bass as bass
from concourse import mybir

ALU = mybir.AluOpType
ACT = mybir.ActivationFunctionType
F32 = mybir.dt.float32
I32 = mybir.dt.int32
U32 = mybir.dt.uint32
AX_X = mybir.AxisListType.X

P = 128
D = 1024
S = 256
NT = S // P
KD = D // P
DEPTH = 2
HD = 64
DIFF_H, RW_H, FOX_H = 6, 6, 4
W6 = DIFF_H * HD
WF = FOX_H * HD
NPAIR = RW_H // 2
C = 64
NC = S // C
LEVELS = int(math.log2(C))
IN_COLS = 3 * W6 + (3 * W6 + 256) + (3 * WF + FOX_H)
RMS_EPS = 1e-6
LN_EPS = 64e-5
DIFF_SCALE = 32 ** -0.5
FOX_SCALE = 64 ** -0.5
PH, NK, TOPK = 8, 128, 16
EXPERTS = NK * NK
SEL = PH * TOPK
RING = 16
WS = 4
BIG = -1e30

_off = {}
_n = 0
for _name, _w in (("ident", P), ("amask", 4 * P), ("xmask", LEVELS * P), ("xtmask", LEVELS * P), ("pairones", P),
                  ("headsel", 2), ("cumsel", NT * S), ("reset", NPAIR * S), ("causal", S), ("foxsel", FOX_H * P),
                  ("iota", TOPK)):
    _off[_name] = (_n, _n + _w)
    _n += _w
CONSTS = _n

DIFF0, RW0, FOX0 = 0, 3 * W6, 6 * W6 + 256
GROUPS = [("r", RW0, W6, "f"), ("k", RW0 + W6, W6, "f"), ("v", RW0 + 2 * W6, W6, "f"), ("x", RW0 + 3 * W6, 256, "f"),
          ("dq", DIFF0, W6, "f"), ("dk", DIFF0 + W6, W6, "f"), ("dv", DIFF0 + 2 * W6, W6, "t"),
          ("fqk", FOX0, 2 * WF, "f"), ("fv", FOX0 + 2 * WF, WF + FOX_H, "t")]
OUTS_OF = [(w // P if kind == "f" else NT) for _, _, w, kind in GROUPS]
COLS = {g[0]: sum(OUTS_OF[:n + 1]) for n, g in enumerate(GROUPS)}


def trunk(nc, x, c, norm_mix_g, norm_ffn_g, final_norm_g, ada_w, ada_b, w_in, w_out, dif_lam, dif_subln_g, rw_mu,
          rw_w0, rw_w2, rw_a0, rw_a2, rw_g2, rw_kk, rw_ka, rw_rk, rw_ln_g, rw_ln_b, fox_bf, peer_wq, peer_subkeys,
          peer_u, peer_v, consts, lam_consts, out):
    gelu, exp, sig = ACT.Gelu, ACT.Exp, ACT.Sigmoid

    with ExitStack() as ctx:
        def sb(name, shape, dt=F32, where=ctx):
            return where.enter_context(nc.sbuf_tensor(name, shape, dt))

        def sem(name):
            return ctx.enter_context(nc.semaphore(name))

        bank = [ctx.enter_context(nc.psum_tensor(f"bank{i}", [P, 512], F32)) for i in range(8)]

        row_landed = [sem(f"row_landed{i}") for i in range(RING)]
        names = ("const_in", "params_in", "bias_in", "gain_in", "wout_in", "small_in",
                 "w_in0", "w_in1", "w_in2", "w_in3",
                 "c_ready", "cT", "crep", "pe_out", "mod_ready", "cols_ready", "dve_step", "act_step", "h_ready",
                 "h_turned", "hT_ready", "ss_ready", "var_ready", "sd_ready", "prow_turned", "params_ready",
                 "lora_in", "lora_out", "lora_act", "kk_sq", "kk_sum", "kk_var", "kk_sd", "decay", "decay_exp",
                 "rw_ops", "bonus_out", "tm_turned", "tm_ready", "apair", "apair_sb", "z_out", "z_sb", "xz_out",
                 "x_sb", "av_out", "av_sb", "uw_out", "uw_sb", "sa_out", "sa_sb", "st_out", "st_sb", "y_out",
                 "y_taken", "y_copied", "gate_out", "gate_sb", "s_out", "s_masked", "s_exp", "p_ready", "p_turned", "pT_ready",
                 "pv_out", "o_taken", "f_exp", "f_in", "f_ln", "cum_in", "cum_out", "cum_sb", "lam_in", "lam_exp",
                 "o_var", "o_sd", "y_var", "y_sd", "mix_ready", "mix_turned", "mixT_ready", "mix_out", "x_done",
                 "reset_free", "rpad", "stored", "sk_turned", "sk_ready", "q_out", "q_ready", "score_out",
                 "score_taken", "gate_max", "gate_exp", "idx_ready", "row_used", "idx_step", "pool_pass",
                 "act_in", "gelu_out", "slots_open")
        s = {n: sem(n) for n in names}
        clearable = range(min(q.num for q in s.values()), max(q.num for q in s.values()) + 1)
        assert len(clearable) == len(names) and all(q.num not in clearable for q in row_landed)

        class Steps:

            def __init__(self, eng, own):
                self.eng, self.own, self.count = eng, own, {}

            def __call__(self, ins, tell=None):
                q = self.own if tell is None else tell
                self.count[q] = self.count.get(q, 0) + 1
                ins.then_inc(s[q], 1)
                self.eng.wait_ge(s[q], self.count[q])

        K = sb("K", [P, CONSTS])
        const = {n: K[:, a:b] for n, (a, b) in _off.items()}
        ident, pairones = const["ident"], const["pairones"]
        xs = sb("xs", [P, NT, D])
        hm = sb("hm", [P, NT, D])
        hT = sb("hT", [P, KD, S])
        mod = sb("mod", [P, 3, D])
        crep = sb("crep", [P, KD, P])
        ringmem = sb("ringmem", [P, RING, D])
        ringf = ringmem[:].rearrange("p a b -> p (a b)")
        wslot = [ringf[:, i * 4096:(i + 1) * 4096].rearrange("p (k n) -> p k n", k=KD) for i in range(WS)]
        stat = sb("stat", [P, 16])
        ones_c = sb("ones_c", [P, P])
        ebase = sb("ebase", [P, 1])

        def load_weights(sp, plan):
            for n, (view, width, free_at) in enumerate(plan):
                if free_at is not None:
                    sp.wait_ge(s["pe_out"], free_at)
                sp.dma_start(wslot[n % WS][:, :, 0:width], view).then_inc(s[f"w_in{n % WS}"], 16)

        def weight_landed(pe, n):
            pe.wait_ge(s[f"w_in{n % WS}"], 16 * (n // WS + 1))

        with ExitStack() as setup, nc.Block() as block:
            c8 = sb("c8", [KD, P], where=setup)
            c8a = sb("c8a", [KD, P], where=setup)
            cT = sb("cT_sb", [P, KD], where=setup)

            @block.sync
            def _(sp):
                sp.dma_start(K[:], consts).then_inc(s["const_in"], 16)
                sp.dma_start(c8[:], c.rearrange("o (k p) -> (o k) p", p=P)).then_inc(s["small_in"], 16)
                sp.dma_start(xs[:], x.rearrange("o (t p) d -> p (o t) d", p=P)).then_inc(s["params_in"], 16)
                sp.wait_ge(s["params_in"], 16)

            @block.scalar
            def _(act):
                act.wait_ge(s["small_in"], 16)
                nc.scalar.activation(c8a[:], c8[:], ACT.Silu).then_inc(s["c_ready"], 1)

            @block.tensor
            def _(pe):
                pe.wait_ge(s["const_in"], 16)
                pe.wait_ge(s["c_ready"], 1)
                nc.tensor.transpose(bank[0][:, 0:KD], c8a[:], ident[0:KD, 0:KD]).then_inc(s["cT"], 1)

            @block.vector
            def _(dve):
                step = Steps(dve, "dve_step")
                step(nc.vector.memset(ones_c[:], 1.0))
                step(nc.vector.memset(ebase[:], 0.0))
                dve.wait_ge(s["cT"], 1)
                step(nc.vector.tensor_copy(cT[:], bank[0][:, 0:KD]))
                for k in range(KD):
                    nc.vector.tensor_scalar(crep[:, k, :], ones_c[:], cT[:, k:k + 1], None,
                                            ALU.mult).then_inc(s["crep"], 1)

        nc.all_engine_barrier(sems_to_clear=clearable)

        def ada_plan(l, half):
            view = ada_w[bass.ds(l, 1)].rearrange("o (k p) n -> p (o k) n", p=P)
            return [(view[:, :, half * 3 * D + 512 * n:half * 3 * D + 512 * (n + 1)], 512,
                     None if n < WS else n - WS + 1) for n in range(6)]

        def load_mod(sp, l, half, gain, gains):
            b = ada_b[bass.ds(l, 1), half * 3 * D:(half + 1) * 3 * D]
            sp.dma_start(mod[:].rearrange("p a d -> p (a d)"), b.broadcast_to([P, 3 * D])).then_inc(s["bias_in"], 16)
            sp.dma_start(gain, gains[bass.ds(l, 1), :].broadcast_to([P, D])).then_inc(s["gain_in"], 16)

        def ada_pe(pe):
            for n in range(6):
                weight_landed(pe, n)
                if n >= 2:
                    pe.wait_ge(s["mod_ready"], n - 1)
                for k in range(KD):
                    mm = nc.tensor.matmul(bank[n % 2][:, :], crep[:, k, :], wslot[n % WS][:, k, :],
                                          start=(k == 0), stop=(k == KD - 1))
                mm.then_inc(s["pe_out"], 1)

        def norm_dve(dve, step, gain):
            for t in range(NT):
                dve.wait_ge(s["ss_ready"], t + 1)
                step(nc.vector.tensor_scalar(stat[:, 2 + t:3 + t], stat[:, t:t + 1], 1.0 / D, RMS_EPS,
                                             ALU.mult, ALU.add), "var_ready")
            dve.wait_ge(s["bias_in"], 16)
            m = mod[:].rearrange("p a d -> p (a d)")
            for n in range(6):
                dve.wait_ge(s["pe_out"], n + 1)
                part = m[:, 512 * n:512 * (n + 1)]
                step(nc.vector.tensor_tensor(part, bank[n % 2][:, :], part, ALU.add), "mod_ready")
            dve.wait_ge(s["gain_in"], 16)
            step(nc.vector.scalar_tensor_tensor(out=mod[:, 1, :], in0=mod[:, 1, :], scalar=1.0, in1=gain,
                                                op0=ALU.add, op1=ALU.mult))
            for t in range(NT):
                dve.wait_ge(s["sd_ready"], t + 1)
                step(nc.vector.reciprocal(stat[:, 6 + t:7 + t], stat[:, 4 + t:5 + t]))
                step(nc.vector.scalar_tensor_tensor(out=hm[:, t, :], in0=xs[:, t, :], scalar=stat[:, 6 + t:7 + t],
                                                    in1=mod[:, 1, :], op0=ALU.mult, op1=ALU.mult))
                step(nc.vector.tensor_tensor(hm[:, t, :], hm[:, t, :], mod[:, 0, :], ALU.add), "h_ready")

        def norm_act(act, junk):
            for t in range(NT):
                nc.scalar.activation(junk, xs[:, t, :], ACT.Square,
                                     accum_out=stat[:, t:t + 1]).then_inc(s["ss_ready"], 1)
                act.wait_ge(s["ss_ready"], t + 1)
            for t in range(NT):
                act.wait_ge(s["var_ready"], t + 1)
                nc.scalar.activation(stat[:, 4 + t:5 + t], stat[:, 2 + t:3 + t], ACT.Sqrt).then_inc(s["sd_ready"], 1)

        def turn_pe(pe, src, ready, turned, taken, banks):
            for t in range(NT):
                pe.wait_ge(s[ready], t + 1)
                for b in range(2):
                    n = 2 * t + b
                    if n >= 2:
                        pe.wait_ge(s[taken], n - 1)
                    for j in range(4):
                        k = 4 * b + j
                        tr = nc.tensor.transpose(bank[banks + n % 2][:, j * P:(j + 1) * P],
                                                 src[:, t, k * P:(k + 1) * P], ident)
                    tr.then_inc(s[turned], 1)

        def turn_act(act, turned, taken, banks):
            for t in range(NT):
                for b in range(2):
                    n = 2 * t + b
                    act.wait_ge(s[turned], n + 1)
                    nc.scalar.activation(hT[:, 4 * b:4 * b + 4, t * P:(t + 1) * P],
                                         bank[banks + n % 2][:, :].rearrange("p (j c) -> p j c", j=4),
                                         ACT.Copy).then_inc(s[taken], 1)

        with nc.Fori(0, DEPTH) as l:
            with ExitStack() as mix, nc.Block() as block:
                gain = hm[:, 0, :]
                prow = sb("prow", [26, P], where=mix)
                pcol = sb("pcol", [P, 26], where=mix)
                MU, PW0, PA0, PKK, PKA, PRK = 0, 11, 14, 17, 20, 23
                colsT = sb("colsT", [P, 11, S + 1], where=mix)
                mixed = sb("mixed", [P, 11, S], where=mix)
                w2a2 = sb("w2a2", [P, W6], where=mix)
                g2 = sb("g2", [P, W6], where=mix)
                lnp = sb("lnp", [P, 2, W6], where=mix)
                subg = sb("subg", [P, HD], where=mix)
                lamp = sb("lamp", [P, 4, 32], where=mix)
                lamc = sb("lamc", [P, 2], where=mix)
                small = sb("small", [P, 24], where=mix)
                bfb = sb("bfb", [P, FOX_H], where=mix)
                sgx = sb("sgx", [P, S], where=mix)
                thx = sb("thx", [HD, S], where=mix)
                AL = sb("AL", [P, 2, NPAIR, S], where=mix)
                asig, lw = AL[:, 0], AL[:, 1]
                T12 = sb("T12", [P, 2, NPAIR, S], where=mix)
                T1, T2 = T12[:, 0], T12[:, 1]
                cold = colsT[:].rearrange("p a b -> p (a b)")

                def old(n):
                    return cold[:, 1 + n * NPAIR * S:1 + (n + 1) * NPAIR * S].rearrange("p (a b) -> p a b", a=NPAIR)

                E1, E2, E3 = (old(n) for n in range(3))
                bt, kt = (hT[:, 3 * n:3 * n + 3, :] for n in range(2))
                ar = sb("ar", [P, NPAIR, NT, 2, P], where=mix)
                rpad = sb("rpad_sb", [P, NPAIR, NT, 2, P], where=mix)
                bon = sb("bon", [P, NT, RW_H], where=mix)
                gate = sb("gate", [P, NT, W6], where=mix)
                ST = sb("ST", [P, NC, NPAIR, P], where=mix)
                alf, t12f = (a[:].rearrange("p a g c -> p (a g c)") for a in (AL, T12))
                stmp = alf[:, 896:1280].rearrange("p (g c) -> p g c", g=NPAIR)
                SA = sb("SA", [P, NT, NPAIR, P], where=mix)
                dq = sb("dq", [P, 3, S], where=mix)
                dk = sb("dk", [P, 3, S], where=mix)
                dv = sb("dv", [P, NT, W6], where=mix)
                fqk = sb("fqk", [P, 4, S], where=mix)
                fv = sb("fv", [P, NT, WF + FOX_H], where=mix)
                fl = sb("fl", [P, 4, NT, FOX_H], where=mix)
                cumT = sb("cumT", [FOX_H, S], where=mix)
                sc = t12f[:, 0:1024].rearrange("p (a b) -> p a b", a=2)
                pn = t12f[:, 1024:1536].rearrange("p (a b) -> p a b", a=2)
                pT = alf[:, 0:512].rearrange("p (a b) -> p a b", a=2)
                ast = sb("ast", [P, 2, 8], where=mix)
                ov = alf[:, 512:896]
                AT = [ringf[:, n * 512:(n + 1) * 512] for n in range(12)]
                X, XT, Z = (ringf[:, 6144 + n * 1536:6144 + (n + 1) * 1536].rearrange("p (g c) -> p g c", g=NPAIR)
                            for n in range(3))
                tm = ringf[:, 10752:10752 + 3072].rearrange("p (g t k c) -> p g t k c", g=NPAIR, t=NT, k=4)
                AV, U, WT = (ringf[:, 13824 + n * 768:13824 + (n + 1) * 768].rearrange("p (t g c) -> p t g c", t=NT, g=NPAIR)
                             for n in range(3))
                wout = ringf[:, 0:8192].rearrange("p (k n) -> p k n", k=KD)
                BTK, KTK, ATK, VTK = range(4)
                proj0 = 6
                nproj = COLS["fv"]

                units = [("d", h, t) for t in range(NT) for h in range(DIFF_H)] + \
                        [("f", h, t) for t in range(NT) for h in range(FOX_H)]

                @block.sync
                def _(sp):
                    load_mod(sp, l, 0, gain, norm_mix_g)
                    plan = ada_plan(l, 0)
                    for n, (view, width, free_at) in enumerate(plan):
                        if free_at is not None:
                            sp.wait_ge(s["pe_out"], free_at)
                        sp.dma_start(wslot[n % WS][:, :, 0:width], view).then_inc(s[f"w_in{n % WS}"], 16)
                        if n == 0:
                            for row, src, cnt in ((MU, rw_mu, 11), (PW0, rw_w0, 3), (PA0, rw_a0, 3), (PKK, rw_kk, 3),
                                                  (PKA, rw_ka, 3)):
                                sp.dma_start(prow[row:row + cnt, :], src[bass.ds(l, 1), :].rearrange(
                                    "o (c p) -> (o c) p", p=P)).then_inc(s["params_in"], 16)
                            sp.dma_start(prow[PRK:PRK + 3, :], rw_rk[bass.ds(l, 1)].rearrange(
                                "o (c a) d -> (o c) (a d)", a=2)).then_inc(s["params_in"], 16)
                            sp.dma_start(w2a2[0:64, :], rw_w2[bass.ds(l, 1)].rearrange("o p n -> (o p) n")).then_inc(s["lora_in"], 16)
                            sp.dma_start(w2a2[64:128, :], rw_a2[bass.ds(l, 1)].rearrange("o p n -> (o p) n")).then_inc(s["lora_in"], 16)
                            sp.dma_start(g2[:], rw_g2[bass.ds(l, 1)].rearrange("o p n -> (o p) n")).then_inc(s["lora_in"], 16)
                            sp.dma_start(lnp[:, 0, :], rw_ln_g[bass.ds(l, 1), :].broadcast_to([P, W6])).then_inc(s["small_in"], 16)
                            sp.dma_start(lnp[:, 1, :], rw_ln_b[bass.ds(l, 1), :].broadcast_to([P, W6])).then_inc(s["small_in"], 16)
                            sp.dma_start(subg[:], dif_subln_g[bass.ds(l, 1), :].broadcast_to([P, HD])).then_inc(s["small_in"], 16)
                            sp.dma_start(lamp[:].rearrange("p a b -> p (a b)"), dif_lam[bass.ds(l, 1)].rearrange(
                                "o a b -> o (a b)").broadcast_to([P, 128])).then_inc(s["small_in"], 16)
                            sp.dma_start(lamc[:], lam_consts[bass.ds(l, 1), :].broadcast_to([P, 2])).then_inc(s["small_in"], 16)
                            sp.dma_start(bfb[:], fox_bf[bass.ds(l, 1), :].broadcast_to([P, FOX_H])).then_inc(s["small_in"], 16)
                    win = w_in[bass.ds(l, 1)].rearrange("o (k p) n -> p (o k) n", p=P)
                    last_out = [n + 1 for n in range(6)] + [proj0 + COLS[g[0]] for g in GROUPS]
                    for g, (_, c0, w, _) in enumerate(GROUPS):
                        n = 6 + g
                        sp.wait_ge(s["pe_out"], last_out[n - WS])
                        sp.dma_start(wslot[n % WS][:, :, 0:w], win[:, :, c0:c0 + w]).then_inc(s[f"w_in{n % WS}"], 16)
                    sp.wait_ge(s["y_out"], NT)
                    sp.dma_start(wout, w_out[bass.ds(l, 1)].rearrange("o (k p) n -> p (o k) n", p=P)).then_inc(s["wout_in"], 16)

                @block.gpsimd
                def _(pool):
                    nc.gpsimd.memset(rpad[:], 0.0).then_inc(s["reset_free"], 1)
                    nc.gpsimd.memset(colsT[:, :, 0:1], 0.0).then_inc(s["reset_free"], 1)
                    nc.gpsimd.memset(ST[:, 0], 0.0).then_inc(s["reset_free"], 1)
                    pool.wait_ge(s["pe_out"], proj0 + nproj)
                    for a in (X, XT):
                        nc.gpsimd.tensor_copy(a.rearrange("p g (i c) -> p (g i) c", c=P),
                                              ident.rearrange("p (o c) -> p o c", o=1).broadcast_to([P, 12, P])).then_inc(s["reset_free"], 1)
                    pool.wait_ge(s["rw_ops"], 2)
                    pool.wait_ge(s["reset_free"], 1)
                    for cc in range(2):
                        nc.gpsimd.tensor_copy(rpad[:, :, :, cc, cc * C:(cc + 1) * C].rearrange("p g t c -> p (g t) c"),
                                              ar[:, :, :, 1, cc * C:(cc + 1) * C].rearrange("p g t c -> p (g t) c")
                                              ).then_inc(s["rpad"], 1)

                @block.tensor
                def _(pe):
                    pe.wait_ge(s["params_in"], 6 * 16)
                    nc.tensor.transpose(bank[7][:, 0:26], prow[:], ident[0:26, 0:26]).then_inc(s["prow_turned"], 1)
                    ada_pe(pe)
                    turn_pe(pe, hm, "h_ready", "h_turned", "hT_ready", 2)
                    pe.wait_ge(s["hT_ready"], 4)
                    m = 0
                    for g, (name, c0, w, kind) in enumerate(GROUPS):
                        n = 6 + g
                        weight_landed(pe, n)
                        wt = wslot[n % WS]
                        for j in range(w // P if kind == "f" else NT):
                            if m >= 2:
                                pe.wait_ge(s["cols_ready"], m - 1)
                            for k in range(KD):
                                if kind == "f":
                                    mm = nc.tensor.matmul(bank[m % 2][:, 0:S], wt[:, k, j * P:(j + 1) * P], hT[:, k, :],
                                                          start=(k == 0), stop=(k == KD - 1))
                                else:
                                    mm = nc.tensor.matmul(bank[m % 2][:, 0:w], hT[:, k, j * P:(j + 1) * P], wt[:, k, 0:w],
                                                          start=(k == 0), stop=(k == KD - 1))
                            mm.then_inc(s["pe_out"], 1)
                            m += 1
                    pe.wait_ge(s["lora_in"], 48)
                    pe.wait_ge(s["act_step"], 2)
                    pe.wait_ge(s["rw_ops"], 1)
                    for j in range(6):
                        r0 = 0 if j < 3 else 64
                        rhs = thx[:, :] if j < 3 else mixed[64:128, 9, :]
                        if j >= 2:
                            pe.wait_ge(s["lora_act"], j - 1)
                        nc.tensor.matmul(bank[2 + j % 2][:, 0:S], w2a2[r0:r0 + 64, (j % 3) * P:(j % 3 + 1) * P], rhs,
                                         start=True, stop=True).then_inc(s["lora_out"], 1)
                    for t in range(NT):
                        nc.tensor.matmul(bank[4 + t][:, 0:W6], sgx[:, t * P:(t + 1) * P], g2[:, :],
                                         start=True, stop=True).then_inc(s["gate_out"], 1)
                    pe.wait_ge(s["kk_sq"], 1)
                    for p in range(NPAIR):
                        mm = nc.tensor.matmul(bank[6 + p // 2][:, (p % 2) * S:(p % 2 + 1) * S], pairones, T1[:, p, :],
                                              start=True, stop=True)
                    mm.then_inc(s["kk_sum"], 1)

                    pe.wait_ge(s["cum_in"], 1)
                    for t in range(NT):
                        mm = nc.tensor.matmul(bank[0][0:FOX_H, 0:S], fl[:, 3, t, :],
                                              const["cumsel"][:, t * S:(t + 1) * S], start=(t == 0), stop=(t == NT - 1))
                    mm.then_inc(s["cum_out"], 1)

                    pe.wait_ge(s["rw_ops"], 3)
                    pe.wait_ge(s["lora_act"], 6)
                    pe.wait_ge(s["kk_var"], 1)
                    for n in range(6):
                        p, t = n // 2, n % 2
                        if n >= 2:
                            pe.wait_ge(s["tm_ready"], n - 1)
                        for kind, src in ((BTK, bt[:, p, t * P:(t + 1) * P]), (KTK, kt[:, p, t * P:(t + 1) * P]),
                                          (ATK, ar[:, p, t, 0, :]), (VTK, mixed[:, 6 + p, t * P:(t + 1) * P])):
                            tr = nc.tensor.transpose(bank[2 + n % 2][:, kind * P:(kind + 1) * P], src, ident)
                        tr.then_inc(s["tm_turned"], 1)
                    pe.wait_ge(s["gate_sb"], NT)
                    for n in range(12):
                        p, t, par = n // 4, (n // 2) % 2, n % 2
                        if n >= 2:
                            pe.wait_ge(s["apair_sb"], n - 1)
                        q = slice(64 * par, 64 * par + 64)
                        rhs = ar[q, p, t, :, :].rearrange("p a c -> p (a c)")
                        for o, left in ((0, bt), (256, kt)):
                            mm = nc.tensor.matmul(bank[4 + n % 2][:, o:o + 256], left[q, p, t * P:(t + 1) * P], rhs,
                                                  start=True, stop=True)
                        mm.then_inc(s["apair"], 1)
                    pe.wait_ge(s["rw_ops"], 4)
                    for t in range(NT):
                        for p in range(NPAIR):
                            mm = nc.tensor.matmul(bank[6][:, t * 8 + 2 * p:t * 8 + 2 * p + 2], T2[:, p, t * P:(t + 1) * P],
                                                  const["headsel"], start=True, stop=True)
                    mm.then_inc(s["bonus_out"], 1)

                    pe.wait_ge(s["apair_sb"], 12)
                    pe.wait_ge(s["reset_free"], 5)
                    pe.wait_ge(s["y_taken"], 1)
                    pe.wait_ge(s["cum_sb"], 1)
                    for lev in range(LEVELS):
                        for p in range(NPAIR):
                            pe.wait_ge(s["tm_ready"], 6)
                            if lev:
                                pe.wait_ge(s["x_sb"], (lev - 1) * 6 + 2 * p + 2)
                            for j in range(4):
                                mm = nc.tensor.matmul(bank[p][:, j * P:(j + 1) * P], AT[4 * p + j][:, 0:P],
                                                      X[:, p, j * P:(j + 1) * P], start=True, stop=True)
                            mm.then_inc(s["z_out"], 1)
                        for p in range(NPAIR):
                            pe.wait_ge(s["z_sb"], lev * 3 + p + 1)
                            b2 = 3 + 2 * (p % 2)
                            before = lev * NPAIR + p - (1, 3, 2)[p]
                            if before >= 0:
                                pe.wait_ge(s["x_sb"], 2 * before + 2)
                            if lev < LEVELS - 1:
                                for j in range(4):
                                    mm = nc.tensor.matmul(bank[b2][:, j * P:(j + 1) * P], XT[:, p, j * P:(j + 1) * P],
                                                          Z[:, p, j * P:(j + 1) * P], start=True, stop=True)
                            for j in range(4):
                                mm = nc.tensor.matmul(bank[b2 + 1][:, j * P:(j + 1) * P], Z[:, p, j * P:(j + 1) * P],
                                                      XT[:, p, j * P:(j + 1) * P], start=True, stop=True)
                            mm.then_inc(s["xz_out"], 1)
                    pe.wait_ge(s["x_sb"], LEVELS * 6)
                    for t in range(NT):
                        for p in range(NPAIR):
                            for par in range(2):
                                mm = nc.tensor.matmul(bank[3 + t][:, p * P + par * 64:p * P + par * 64 + 64],
                                                      AT[4 * p + 2 * t + par][:, 256:384],
                                                      tm[:, p, t, VTK, par * 64:par * 64 + 64], start=True, stop=True)
                        mm.then_inc(s["av_out"], 1)
                    for t in range(NT):
                        pe.wait_ge(s["av_sb"], t + 1)
                        if t:
                            pe.wait_ge(s["uw_sb"], 1)
                        for p in range(NPAIR):
                            for par in range(2):
                                xt = XT[:, p, (2 * t + par) * P:(2 * t + par + 1) * P]
                                nc.tensor.matmul(bank[5][:, p * P + par * 64:p * P + par * 64 + 64], xt,
                                                 AV[:, t, p, par * 64:par * 64 + 64], start=True, stop=True)
                                mm = nc.tensor.matmul(bank[6 + par][:, p * P:(p + 1) * P], tm[:, p, t, ATK, :], xt,
                                                      start=True, stop=True)
                        mm.then_inc(s["uw_out"], 1)
                    pe.wait_ge(s["uw_sb"], NT)
                    for cc in range(NC):
                        t, o = cc // 2, slice(64 * (cc % 2), 64 * (cc % 2) + 64)
                        if cc:
                            pe.wait_ge(s["st_sb"], cc)
                        for p in range(NPAIR):
                            mm = nc.tensor.matmul(bank[3][:, p * P:(p + 1) * P], WT[:, t, p, :], ST[:, cc, p, :],
                                                  start=True, stop=True)
                        mm.then_inc(s["sa_out"], 1)
                        if cc < NC - 1:
                            pe.wait_ge(s["sa_sb"], cc + 1)
                            for p in range(NPAIR):
                                nc.tensor.matmul(bank[4][:, p * P:(p + 1) * P], tm[o, p, t, KTK, :], tm[o, p, t, VTK, :],
                                                 start=True, stop=False)
                                mm = nc.tensor.matmul(bank[4][:, p * P:(p + 1) * P], tm[o, p, t, BTK, :],
                                                      SA[o, t, p, :], start=False, stop=True)
                            mm.then_inc(s["st_out"], 1)
                    pe.wait_ge(s["rpad"], 2)
                    pe.wait_ge(s["sa_sb"], NC)
                    for t in range(NT):
                        for p in range(NPAIR):
                            whole = bank[5 + t][:, p * P:(p + 1) * P]
                            for cc in range(2):
                                nc.tensor.matmul(whole, rpad[:, p, t, cc, :], ST[:, 2 * t + cc, p, :],
                                                 start=(cc == 0), stop=False, skip_group_check=True)
                            for par in range(2):
                                half = bank[5 + t][:, p * P + 64 * par:p * P + 64 * par + 64]
                                a = AT[4 * p + 2 * t + par]
                                nc.tensor.matmul(half, a[:, 128:256], SA[:, t, p, 64 * par:64 * par + 64],
                                                 start=False, stop=False, skip_group_check=True)
                                mm = nc.tensor.matmul(half, a[:, 384:512], tm[:, p, t, VTK, 64 * par:64 * par + 64],
                                                      start=False, stop=True, skip_group_check=True)
                        mm.then_inc(s["y_out"], 1)

                    pe.wait_ge(s["cum_sb"], 1)
                    pe.wait_ge(s["z_sb"], LEVELS * NPAIR)
                    pe.wait_ge(s["y_copied"], NT)

                    def scores(n):
                        kind, h, t = units[n]
                        nk = (t + 1) * P
                        ps = bank[n % 2]
                        if n >= 2:
                            pe.wait_ge(s["s_masked"], n - 1)
                        o = 64 * (h % 2)
                        if kind == "d":
                            for a in range(2):
                                q = slice(o + 32 * a, o + 32 * a + 32)
                                mm = nc.tensor.matmul(bank[n % 2 + 5 * a][:, 0:nk], dq[q, h // 2, t * P:(t + 1) * P],
                                                      dk[q, h // 2, 0:nk], start=True, stop=True)
                        else:
                            q = slice(o, o + 64)
                            nc.tensor.matmul(ps[:, 0:nk], fqk[q, h // 2, t * P:(t + 1) * P], fqk[q, 2 + h // 2, 0:nk],
                                             start=True, stop=False)
                            mm = nc.tensor.matmul(ps[:, 0:nk], const["foxsel"][0:FOX_H, h * P:(h + 1) * P],
                                                  cumT[:, 0:nk], start=False, stop=True)
                        mm.then_inc(s["s_out"], 1)

                    def values(n):
                        kind, h, t = units[n]
                        pe.wait_ge(s["p_ready"], n + 1)
                        if n >= 1:
                            pe.wait_ge(s["pT_ready"], n)
                        for j in range(t + 1):
                            tr = nc.tensor.transpose(bank[2][:, j * P:(j + 1) * P], pn[:, n % 2, j * P:(j + 1) * P], ident)
                        tr.then_inc(s["p_turned"], 1)
                        pe.wait_ge(s["pT_ready"], n + 1)
                        base = 0 if kind == "d" else W6
                        o = 0 if kind == "d" else 0
                        if kind == "d":
                            dst = bank[3 if t == 0 else 4][:, h * HD:(h + 1) * HD]
                        else:
                            if t == 0 and h == 0:
                                pe.wait_ge(s["o_taken"], 1)
                            if t == 1 and h == 0:
                                pe.wait_ge(s["o_taken"], 2)
                            dst = bank[3 if t == 0 else 4][:, h * HD:(h + 1) * HD]
                        for j in range(t + 1):
                            v = dv[:, j, h * HD:(h + 1) * HD] if kind == "d" else fv[:, j, h * HD:(h + 1) * HD]
                            mm = nc.tensor.matmul(dst, pT[:, n % 2, j * P:(j + 1) * P], v,
                                                  start=(j == 0), stop=(j == t))
                        mm.then_inc(s["pv_out"], 1)

                    for n in range(len(units) + 1):
                        if n < len(units):
                            scores(n)
                        if n >= 1:
                            values(n - 1)

                    turn_pe(pe, hm, "mix_ready", "mix_turned", "mixT_ready", 0)
                    pe.wait_ge(s["mixT_ready"], 4)
                    pe.wait_ge(s["wout_in"], 16)
                    for t in range(NT):
                        for b in range(2):
                            for k in range(KD):
                                mm = nc.tensor.matmul(bank[4 + 2 * t + b][:, :], hT[:, k, t * P:(t + 1) * P],
                                                      wout[:, k, b * 512:(b + 1) * 512],
                                                      start=(k == 0), stop=(k == KD - 1))
                            mm.then_inc(s["mix_out"], 1)

                @block.scalar
                def _(act):
                    junk = t12f[:, 0:1024]
                    norm_act(act, junk)
                    turn_act(act, "h_turned", "hT_ready", 2)
                    dest = {"r": colsT[:, 0:3, 1:], "k": colsT[:, 3:6, 1:], "v": colsT[:, 6:9, 1:], "x": colsT[:, 9:11, 1:],
                            "dq": dq, "dk": dk, "dv": dv, "fqk": fqk, "fv": fv}

                    def take(name):
                        g = [q[0] for q in GROUPS].index(name)
                        w, kind = GROUPS[g][2], GROUPS[g][3]
                        first = COLS[name] - OUTS_OF[g]
                        for j in range(OUTS_OF[g]):
                            m = first + j
                            act.wait_ge(s["pe_out"], proj0 + m + 1)
                            nc.scalar.activation(dest[name][:, j, 0:(S if kind == "f" else w)],
                                                 bank[m % 2][:, 0:(S if kind == "f" else w)],
                                                 ACT.Copy).then_inc(s["cols_ready"], 1)

                    for name in ("r", "k", "v", "x", "dq"):
                        take(name)
                    act.wait_ge(s["rw_ops"], 1)
                    nc.scalar.activation(thx[:], mixed[0:64, 9, :], ACT.Tanh).then_inc(s["act_step"], 1)
                    nc.scalar.activation(sgx[:], mixed[:, 10, :], sig).then_inc(s["act_step"], 1)
                    act.wait_ge(s["kk_sq"], 1)
                    for name in ("dk", "dv", "fqk", "fv"):
                        take(name)
                    for j in range(6):
                        act.wait_ge(s["lora_out"], j + 1)
                        dst = lw[:, j, :] if j < 3 else asig[:, j - 3, :]
                        nc.scalar.activation(dst, bank[2 + j % 2][:, 0:S], sig, bias=pcol[:, PW0 + j:PW0 + j + 1]
                                             ).then_inc(s["lora_act"], 1)
                    for t in range(NT):
                        act.wait_ge(s["gate_out"], t + 1)
                        nc.scalar.activation(gate[:, t, :], bank[4 + t][:, 0:W6], ACT.Copy).then_inc(s["gate_sb"], 1)
                    act.wait_ge(s["decay"], 1)
                    nc.scalar.activation(E2, E1, exp).then_inc(s["decay_exp"], 1)
                    nc.scalar.activation(E3, E1, exp, scale=-1.0).then_inc(s["decay_exp"], 1)
                    act.wait_ge(s["decay"], 2)
                    nc.scalar.activation(lw, lw, exp).then_inc(s["decay_exp"], 1)
                    act.wait_ge(s["f_in"], 1)
                    nc.scalar.activation(fl[:, 2], fl[:, 1], exp, scale=-1.0).then_inc(s["f_exp"], 1)
                    act.wait_ge(s["lam_in"], 1)
                    nc.scalar.activation(small[:, 2:4], small[:, 0:2], exp).then_inc(s["lam_exp"], 1)
                    act.wait_ge(s["f_exp"], 1)
                    nc.scalar.activation(fl[:, 1], fl[:, 2], ACT.Ln, bias=1.0).then_inc(s["f_ln"], 1)
                    act.wait_ge(s["kk_var"], 1)
                    nc.scalar.activation(T1, T1, ACT.Sqrt).then_inc(s["kk_sd"], 1)
                    for n in range(6):
                        act.wait_ge(s["tm_turned"], n + 1)
                        nc.scalar.activation(tm[:, n // 2, n % 2].rearrange("p k c -> p (k c)"), bank[2 + n % 2][:, :],
                                             ACT.Copy).then_inc(s["tm_ready"], 1)
                    act.wait_ge(s["cum_out"], 1)
                    nc.scalar.activation(cumT[:], bank[0][0:FOX_H, 0:S], ACT.Copy).then_inc(s["cum_sb"], 1)
                    for lev in range(LEVELS):
                        for p in range(NPAIR):
                            act.wait_ge(s["z_out"], lev * 3 + p + 1)
                            nc.scalar.activation(Z[:, p, :], bank[p][:, :], ACT.Copy).then_inc(s["z_sb"], 1)
                    for n, (kind, h, t) in enumerate(units):
                        nk = (t + 1) * P
                        act.wait_ge(s["s_masked"], n + 1)
                        for a in range(2 if kind == "d" else 1):
                            ins = nc.scalar.activation(sc[:, n % 2, a * S:a * S + nk], sc[:, n % 2, a * S:a * S + nk], exp,
                                                       bias=ast[:, n % 2, a:a + 1],
                                                       scale=DIFF_SCALE if kind == "d" else FOX_SCALE,
                                                       accum_out=ast[:, n % 2, 2 + a:3 + a])
                        ins.then_inc(s["s_exp"], 1)
                    for t in range(NT):
                        act.wait_ge(s["o_var"], t + 1)
                        nc.scalar.activation(small[:, 12:18] if t == 0 else small[:, 18:24], small[:, 6:12], ACT.Sqrt
                                             ).then_inc(s["o_sd"], 1)
                    for t in range(NT):
                        act.wait_ge(s["y_var"], t + 1)
                        nc.scalar.activation(small[:, 12:18] if t == 0 else small[:, 18:24], small[:, 6:12], ACT.Sqrt
                                             ).then_inc(s["y_sd"], 1)
                    turn_act(act, "mix_turned", "mixT_ready", 0)

                @block.vector
                def _(dve):
                    v = nc.vector
                    step = Steps(dve, "dve_step")
                    dve.wait_ge(s["prow_turned"], 1)
                    step(v.tensor_copy(pcol[:], bank[7][:, 0:26]), "params_ready")
                    norm_dve(dve, step, gain)
                    dve.wait_ge(s["small_in"], 6 * 16)
                    lprod = ov[:, 0:64].rearrange("p (a b) -> p a b", a=2)
                    step(v.tensor_tensor(lprod, lamp[:, 0:4:2, :], lamp[:, 1:4:2, :], ALU.mult))
                    step(v.tensor_reduce(small[:, 0:2], lprod, AX_X, ALU.add), "lam_in")

                    dve.wait_ge(s["reset_free"], 3)
                    for name, a, b in (("r", 0, 3), ("k", 3, 6), ("v", 6, 9), ("x", 9, 11)):
                        dve.wait_ge(s["cols_ready"], COLS[name])
                        step(v.tensor_tensor(mixed[:, a:b, :], colsT[:, a:b, 0:S], colsT[:, a:b, 1:S + 1], ALU.subtract))
                        for q in range(a, b):
                            ins = v.scalar_tensor_tensor(out=mixed[:, q, :], in0=mixed[:, q, :],
                                                         scalar=pcol[:, MU + q:MU + q + 1], in1=colsT[:, q, 1:S + 1],
                                                         op0=ALU.mult, op1=ALU.add)
                            if q == 10:
                                step(ins, "rw_ops")
                            else:
                                step(ins)

                    def bc(o):
                        return pcol[:, o:o + 3].rearrange("p (a b) -> p a b", b=1).broadcast_to([P, NPAIR, S])

                    r_, k_, v_ = mixed[:, 0:3, :], mixed[:, 3:6, :], mixed[:, 6:9, :]
                    step(v.tensor_tensor(T2, k_, bc(PKK), ALU.mult))
                    step(v.tensor_tensor(T1, T2, T2, ALU.mult), "kk_sq")
                    dve.wait_ge(s["cols_ready"], nproj)
                    z = fl[:, 0]
                    step(v.tensor_tensor(z, fv[:, :, WF:], bfb[:].rearrange("p (a b) -> p a b", a=1).broadcast_to([P, NT, FOX_H]), ALU.add))
                    step(v.tensor_scalar(fl[:, 1], z, -1.0, None, ALU.mult))
                    step(v.tensor_tensor(fl[:, 1], fl[:, 1], z, ALU.max), "f_in")
                    dve.wait_ge(s["kk_sum"], 1)
                    step(v.tensor_scalar(T1[:, 0:2, :].rearrange("p a b -> p (a b)"), bank[6][:, :], 1e-24, None, ALU.max))
                    step(v.tensor_scalar(T1[:, 2, :], bank[7][:, 0:S], 1e-24, None, ALU.max), "kk_var")
                    dve.wait_ge(s["lora_act"], 6)
                    step(v.tensor_scalar(lw, lw, -math.exp(-0.5), None, ALU.mult))
                    step(v.tensor_tensor_scan(E1.rearrange("p a b -> p (a b)"), const["reset"],
                                              lw.rearrange("p a b -> p (a b)"), 0.0, ALU.mult, ALU.add), "decay")
                    step(v.tensor_tensor(lw, E1, lw, ALU.subtract), "decay")
                    dve.wait_ge(s["f_ln"], 1)
                    step(v.scalar_tensor_tensor(out=fl[:, 3], in0=z, scalar=0.0, in1=fl[:, 1],
                                                op0=ALU.min, op1=ALU.subtract), "cum_in")
                    dve.wait_ge(s["decay_exp"], 3)
                    step(v.tensor_tensor(ar[:, :, :, 1, :], r_.rearrange("p g (t c) -> p g t c", t=NT),
                                         E2.rearrange("p g (t c) -> p g t c", t=NT), ALU.mult), "rw_ops")
                    step(v.scalar_tensor_tensor(out=E1, in0=asig, scalar=-1.0, in1=bc(PKA), op0=ALU.add, op1=ALU.mult))
                    step(v.scalar_tensor_tensor(out=E1, in0=E1, scalar=1.0, in1=k_, op0=ALU.add, op1=ALU.mult))
                    step(v.tensor_tensor(kt, E1, E3, ALU.mult))
                    dve.wait_ge(s["kk_sd"], 1)
                    step(v.reciprocal(T1, T1))
                    step(v.scalar_tensor_tensor(out=T2, in0=T2, scalar=-1.0, in1=T1, op0=ALU.mult, op1=ALU.mult))
                    step(v.tensor_tensor(ar[:, :, :, 0, :], T2.rearrange("p g (t c) -> p g t c", t=NT),
                                         lw.rearrange("p g (t c) -> p g t c", t=NT), ALU.mult))
                    step(v.scalar_tensor_tensor(out=asig, in0=T2, scalar=-1.0, in1=asig, op0=ALU.mult, op1=ALU.mult))
                    step(v.tensor_tensor(bt, asig, E3, ALU.mult), "rw_ops")
                    step(v.tensor_tensor(T2, r_, E1, ALU.mult))
                    step(v.tensor_tensor(T2, T2, bc(PRK), ALU.mult), "rw_ops")
                    for n in range(12):
                        dve.wait_ge(s["apair"], n + 1)
                        step(v.tensor_tensor(AT[n], bank[4 + n % 2][:, :], const["amask"], ALU.mult), "apair_sb")
                    dve.wait_ge(s["bonus_out"], 1)
                    step(v.tensor_copy(bon[:], bank[6][:, 0:16].rearrange("p (t h) -> p t h", t=NT)[:, :, 0:RW_H]), "y_taken")
                    dve.wait_ge(s["lam_exp"], 1)
                    step(v.tensor_tensor(small[:, 4:5], small[:, 3:4], small[:, 2:3], ALU.subtract))
                    step(v.tensor_tensor(small[:, 4:5], small[:, 4:5], lamc[:, 0:1], ALU.subtract))
                    step(v.tensor_scalar(subg[:], subg[:], lamc[:, 1:2], None, ALU.mult))

                    def mask4(name, lev):
                        a = const[name][:, lev * P:(lev + 1) * P].rearrange("p (o c) -> p o c", o=1)
                        return a.broadcast_to([P, 4, P]).bitcast(I32)

                    def four(a):
                        return a.rearrange("p (j c) -> p j c", j=4)

                    for lev in range(LEVELS):
                        for p in range(NPAIR):
                            dve.wait_ge(s["xz_out"], lev * 3 + p + 1)
                            b2 = 3 + 2 * (p % 2)
                            if lev < LEVELS - 1:
                                step(v.copy_predicated(four(X[:, p, :]), mask4("xmask", lev), four(bank[b2][:, :])), "x_sb")
                            else:
                                step(v.tensor_copy(stat[:, 8:9], stat[:, 6:7]), "x_sb")
                            step(v.copy_predicated(four(XT[:, p, :]), mask4("xtmask", lev), four(bank[b2 + 1][:, :])), "x_sb")
                    for t in range(NT):
                        dve.wait_ge(s["av_out"], t + 1)
                        step(v.tensor_copy(AV[:, t].rearrange("p g c -> p (g c)"), bank[3 + t][:, 0:W6]), "av_sb")
                    for t in range(NT):
                        dve.wait_ge(s["uw_out"], t + 1)
                        step(v.tensor_copy(U[:, t].rearrange("p g c -> p (g c)"), bank[5][:, 0:W6]))
                        for par in range(2):
                            q = slice(64 * par, 64 * par + 64)
                            ins = v.tensor_copy(WT[q, t].rearrange("p g c -> p (g c)"), bank[6 + par][q, 0:W6])
                            step(ins, "uw_sb") if par else step(ins)
                    for cc in range(NC):
                        t, o = cc // 2, slice(64 * (cc % 2), 64 * (cc % 2) + 64)
                        dve.wait_ge(s["sa_out"], cc + 1)
                        step(v.tensor_tensor(SA[o, t].rearrange("p g c -> p (g c)"), bank[3][o, 0:W6],
                                             U[o, t].rearrange("p g c -> p (g c)"), ALU.add), "sa_sb")
                        if cc < NC - 1:
                            dve.wait_ge(s["st_out"], cc + 1)
                            step(v.tensor_tensor(stmp, bank[4][:, 0:W6].rearrange("p (g c) -> p g c", g=NPAIR),
                                                 ST[:, cc], ALU.add))
                            last = E2[:, :, cc * C + C - 1:cc * C + C]
                            step(v.tensor_tensor(stmp, stmp, last.broadcast_to([P, NPAIR, P]), ALU.mult))
                            step(v.tensor_tensor(ST[:, cc + 1], stmp, pairones.rearrange("p (o c) -> p o c", o=1)
                                                 .broadcast_to([P, NPAIR, P]), ALU.mult), "st_sb")

                    def head6(a):
                        return a.rearrange("p (h d) -> p h d", h=6)

                    def col6(a):
                        return a.rearrange("p (h o) -> p h o", o=1).broadcast_to([P, 6, HD])

                    for t in range(NT):
                        dve.wait_ge(s["y_out"], t + 1)
                        step(v.tensor_copy(hm[:, t, W6:2 * W6], bank[5 + t][:, 0:W6]), "y_copied")

                    for n, (kind, h, t) in enumerate(units):
                        nk = (t + 1) * P
                        na = 2 if kind == "d" else 1
                        scale = DIFF_SCALE if kind == "d" else FOX_SCALE
                        a_ = sc[:, n % 2, :].rearrange("p (a c) -> p a c", a=2)[:, 0:na, 0:nk]
                        st = ast[:, n % 2, :]
                        dve.wait_ge(s["s_out"], n + 1)
                        for a in range(na):
                            step(v.tensor_tensor(a_[:, a, :], bank[n % 2 + 5 * a][:, 0:nk], const["causal"][:, S - nk:S],
                                                 ALU.add))
                        step(v.tensor_reduce(st[:, 0:na], a_, AX_X, ALU.max))
                        step(v.tensor_scalar(st[:, 0:na], st[:, 0:na], -scale, None, ALU.mult), "s_masked")
                        dve.wait_ge(s["s_exp"], n + 1)
                        step(v.reciprocal(st[:, 4:4 + na], st[:, 2:2 + na]))
                        if kind == "d":
                            step(v.tensor_tensor(st[:, 5:6], st[:, 5:6], small[:, 4:5], ALU.mult))
                            step(v.tensor_scalar(sc[:, n % 2, 0:nk], sc[:, n % 2, 0:nk], st[:, 4:5], None, ALU.mult))
                            step(v.scalar_tensor_tensor(out=pn[:, n % 2, 0:nk], in0=sc[:, n % 2, S:S + nk], scalar=st[:, 5:6],
                                                        in1=sc[:, n % 2, 0:nk], op0=ALU.mult, op1=ALU.add), "p_ready")
                        else:
                            step(v.tensor_scalar(pn[:, n % 2, 0:nk], sc[:, n % 2, 0:nk], st[:, 4:5], None, ALU.mult), "p_ready")
                        dve.wait_ge(s["p_turned"], n + 1)
                        step(v.tensor_copy(pT[:, n % 2, 0:nk], bank[2][:, 0:nk]), "pT_ready")
                        if kind == "d" and h == DIFF_H - 1:
                            dve.wait_ge(s["pv_out"], n + 1)
                            step(v.tensor_copy(hm[:, t, 0:W6], bank[3 + t][:, 0:W6]), "o_taken")
                        if kind == "f" and h == FOX_H - 1:
                            dve.wait_ge(s["pv_out"], n + 1)
                            step(v.tensor_copy(hm[:, t, 2 * W6:D], bank[3 + t][:, 0:WF]), "o_taken")
                    for t in range(NT):
                        o = hm[:, t, 0:W6]
                        step(v.tensor_tensor(ov, o, o, ALU.mult))
                        step(v.tensor_reduce(small[:, 6:12], head6(ov), AX_X, ALU.add))
                        step(v.tensor_scalar(small[:, 6:12], small[:, 6:12], 1.0 / HD, RMS_EPS, ALU.mult, ALU.add), "o_var")
                        dve.wait_ge(s["o_sd"], t + 1)
                        sd = small[:, 12:18] if t == 0 else small[:, 18:24]
                        step(v.reciprocal(sd, sd))
                        step(v.tensor_tensor(head6(o), head6(o), col6(sd), ALU.mult))
                        step(v.tensor_tensor(head6(o), head6(o), subg[:].rearrange("p (o d) -> p o d", o=1)
                                             .broadcast_to([P, 6, HD]), ALU.mult))
                    dve.wait_ge(s["gate_sb"], NT)
                    for t in range(NT):
                        y = hm[:, t, W6:2 * W6]
                        step(v.tensor_reduce(small[:, 6:12], head6(y), AX_X, ALU.add))
                        step(v.tensor_scalar(small[:, 6:12], small[:, 6:12], 1.0 / HD, None, ALU.mult))
                        step(v.tensor_tensor(head6(y), head6(y), col6(small[:, 6:12]), ALU.subtract))
                        step(v.tensor_tensor(ov, y, y, ALU.mult))
                        step(v.tensor_reduce(small[:, 6:12], head6(ov), AX_X, ALU.add))
                        step(v.tensor_scalar(small[:, 6:12], small[:, 6:12], 1.0 / HD, LN_EPS, ALU.mult, ALU.add), "y_var")
                        dve.wait_ge(s["y_sd"], t + 1)
                        sd = small[:, 12:18] if t == 0 else small[:, 18:24]
                        step(v.reciprocal(sd, sd))
                        step(v.tensor_tensor(head6(y), head6(y), col6(sd), ALU.mult))
                        step(v.tensor_tensor(y, y, lnp[:, 0, :], ALU.mult))
                        step(v.tensor_tensor(y, y, lnp[:, 1, :], ALU.add))
                        step(v.tensor_tensor(ov.rearrange("p (g c) -> p g c", g=NPAIR).rearrange("p g (a d) -> p g a d", a=2),
                                             tm[:, :, t, VTK, :].rearrange("p g (a d) -> p g a d", a=2),
                                             bon[:, t, :].rearrange("p (g a o) -> p g a o", g=NPAIR, o=1).broadcast_to([P, NPAIR, 2, HD]),
                                             ALU.mult))
                        step(v.tensor_tensor(y, y, ov, ALU.add))
                        step(v.tensor_tensor(y, y, gate[:, t, :], ALU.mult), "mix_ready")
                    for t in range(NT):
                        for b in range(2):
                            dve.wait_ge(s["mix_out"], 2 * t + b + 1)
                            q = slice(b * 512, (b + 1) * 512)
                            step(v.tensor_tensor(mod[:, 0, q], bank[4 + 2 * t + b][:, :], mod[:, 2, q], ALU.mult))
                            step(v.tensor_tensor(xs[:, t, q], xs[:, t, q], mod[:, 0, q], ALU.add))

            nc.all_engine_barrier(sems_to_clear=clearable)

            with ExitStack() as peer, nc.Block() as block:
                gain = hm[:, 0, :]
                qT = sb("qT", [P, 2 * PH, S], where=peer)
                sk = sb("sk", [P, 2 * PH, P], where=peer)
                skT = sb("skT", [P, 2 * PH, P], where=peer)
                score = sb("score", [P, 2 * PH, NK], where=peer)
                top = sb("top", [P, 2 * PH, TOPK], where=peer)
                topi = sb("topi", [P, 2 * PH, TOPK], U32, where=peer)
                topf = sb("topf", [P, 2 * PH, TOPK], where=peer)
                cand = sb("cand", [P, PH, TOPK * TOPK], where=peer)
                fval = sb("fval", [P, NT, PH, TOPK], where=peer)
                fpos = sb("fpos", [P, PH, TOPK], U32, where=peer)
                fhi = sb("fhi", [P, PH, TOPK], U32, where=peer)
                ff = sb("ff", [P, PH, TOPK], where=peer)
                eid = sb("eid", [P, PH, TOPK], where=peer)
                eidx = sb("eidx", [P, NT, SEL], I32, where=peer)
                zidx = sb("zidx", [P, RING], I32, where=peer)
                islot = sb("islot", [P, 2, RING], I32, where=peer)
                gsum = sb("gsum", [P, NT, 2, PH], where=peer)
                dots = sb("dots", [P, NT, SEL], where=peer)
                coef = sb("coef", [P, NT, SEL], where=peer)
                accv = sb("accv", [P, NT, D], where=peer)
                proj0 = 6

                @block.sync
                def _(sp):
                    load_mod(sp, l, 1, gain, norm_ffn_g)
                    load_weights(sp, ada_plan(l, 1))
                    keys = peer_subkeys[bass.ds(l, 1)].rearrange("o h c n d -> (o h c) n d")
                    for hc in range(2 * PH):
                        sp.dma_start(sk[:, hc, :], keys[hc]).then_inc(s["small_in"], 16)
                    wq = peer_wq[bass.ds(l, 1)].rearrange("o (k p) n -> p (o k) n", p=P)
                    for g in range(4):
                        n = 6 + g
                        sp.wait_ge(s["pe_out"], n - WS + 1)
                        sp.dma_start(wslot[n % WS][:, :, :], wq[:, :, g * 512:(g + 1) * 512]).then_inc(s[f"w_in{n % WS}"], 16)

                @block.tensor
                def _(pe):
                    ada_pe(pe)
                    pe.wait_ge(s["small_in"], 2 * PH * 16)
                    for b in range(4):
                        if b >= 2:
                            pe.wait_ge(s["sk_ready"], b - 1)
                        for j in range(4):
                            tr = nc.tensor.transpose(bank[4 + b % 2][:, j * P:(j + 1) * P], sk[:, 4 * b + j, :], ident)
                        tr.then_inc(s["sk_turned"], 1)
                    turn_pe(pe, hm, "h_ready", "h_turned", "hT_ready", 2)
                    pe.wait_ge(s["hT_ready"], 4)
                    for m in range(16):
                        if m % 4 == 0:
                            weight_landed(pe, 6 + m // 4)
                        if m >= 2:
                            pe.wait_ge(s["q_ready"], m - 1)
                        wt = wslot[(6 + m // 4) % WS]
                        for k in range(KD):
                            mm = nc.tensor.matmul(bank[m % 2][:, 0:S], wt[:, k, (m % 4) * P:(m % 4 + 1) * P], hT[:, k, :],
                                                  start=(k == 0), stop=(k == KD - 1))
                        mm.then_inc(s["q_out"], 1)
                    pe.wait_ge(s["q_ready"], 16)
                    pe.wait_ge(s["sk_ready"], 4)
                    for t in range(NT):
                        for b in range(4):
                            for j in range(4):
                                hc = 4 * b + j
                                mm = nc.tensor.matmul(bank[4 * t + b][:, j * P:(j + 1) * P], qT[:, hc, t * P:(t + 1) * P],
                                                      skT[:, hc, :], start=True, stop=True)
                            mm.then_inc(s["score_out"], 1)

                @block.scalar
                def _(act):
                    norm_act(act, score[:, 0:8, :].rearrange("p a b -> p (a b)"))
                    for b in range(4):
                        act.wait_ge(s["sk_turned"], b + 1)
                        nc.scalar.activation(skT[:, 4 * b:4 * b + 4, :].rearrange("p a b -> p (a b)"), bank[4 + b % 2][:, :],
                                             ACT.Copy).then_inc(s["sk_ready"], 1)
                    turn_act(act, "h_turned", "hT_ready", 2)
                    for m in range(16):
                        act.wait_ge(s["q_out"], m + 1)
                        nc.scalar.activation(qT[:, m, :], bank[m % 2][:, 0:S], ACT.Copy).then_inc(s["q_ready"], 1)
                    for t in range(NT):
                        act.wait_ge(s["gate_max"], t + 1)
                        nc.scalar.activation(coef[:, t, :], coef[:, t, :], exp).then_inc(s["gate_exp"], 1)
                        act.wait_ge(s["act_in"], t + 1)
                        nc.scalar.activation(dots[:, t, :], dots[:, t, :], gelu).then_inc(s["gelu_out"], 1)

                ROUNDS = SEL // RING

                @block.gpsimd
                def _(pool):
                    for ph in range(2 * NT):
                        t, table = ph // 2, (peer_u, peer_v)[ph % 2]
                        rows = table.rearrange("a e d -> (a e) d")
                        if ph % 2 == 0:
                            pool.wait_ge(s["idx_ready"], t + 1)
                        with pool.Fori(0, ROUNDS // 2) as rr:
                            for half in range(2):
                                first = rr * (2 * RING) + (half * RING + ph * SEL)
                                pool.wait_ge(s["row_used"], first + 1)
                                nc.gpsimd.tensor_tensor(islot[:, half, :], eidx[:, t, bass.ds(rr * (2 * RING) + half * RING, RING)],
                                                        zidx[:], ALU.add).then_inc(s["idx_step"], 1)
                                pool.wait_ge(s["idx_step"], rr * 2 + (half + ph * ROUNDS + 1))
                                pool.sem_inc(s["pool_pass"], 1)
                                for j in range(RING):
                                    if j:
                                        pool.wait_ge(s["row_used"], first + j + 1)
                                        pool.sem_inc(s["pool_pass"], 1)
                                    nc.gpsimd.indirect_dma_start(ringmem[:, j, :], None, rows,
                                                                 bass.IndirectOffsetOnAxis(ap=islot[:, half, j:j + 1], axis=0)
                                                                 ).then_inc(row_landed[j], 16)

                @block.vector
                def _(dve):
                    v = nc.vector
                    step = Steps(dve, "dve_step")
                    step(v.memset(zidx[:], 0))
                    norm_dve(dve, step, gain)

                    def top16(vals, idxs, src):
                        step(v.max(vals[:, 0:8], src))
                        step(v.max_index(idxs[:, 0:8], vals[:, 0:8], src))
                        step(v.match_replace(src, vals[:, 0:8], src, BIG * 1e8))
                        step(v.max(vals[:, 8:16], src))
                        step(v.max_index(idxs[:, 8:16], vals[:, 8:16], src))

                    def retrieve(t):
                        for b in range(4):
                            dve.wait_ge(s["score_out"], 4 * t + b + 1)
                            step(v.tensor_copy(score[:, 4 * b:4 * b + 4, :].rearrange("p a b -> p (a b)"),
                                               bank[4 * t + b][:, :]))
                        for hc in range(2 * PH):
                            top16(top[:, hc, :], topi[:, hc, :], score[:, hc, :])
                        step(v.tensor_copy(topf[:], topi[:]))
                        for h in range(PH):
                            a = top[:, 2 * h, :].rearrange("p (i o) -> p i o", o=1).broadcast_to([P, TOPK, TOPK])
                            b = top[:, 2 * h + 1, :].rearrange("p (o j) -> p o j", o=1).broadcast_to([P, TOPK, TOPK])
                            step(v.tensor_tensor(cand[:, h, :].rearrange("p (i j) -> p i j", i=TOPK), a, b, ALU.add))
                            top16(fval[:, t, h, :], fpos[:, h, :], cand[:, h, :])
                        oh = cand[:].rearrange("p h (k i) -> p h k i", k=TOPK)
                        io = const["iota"].rearrange("p (a b i) -> p a b i", a=1, b=1).broadcast_to([P, PH, TOPK, TOPK])
                        for half in range(2):
                            if half == 0:
                                step(v.tensor_scalar(fhi[:], fpos[:], 4, None, ALU.logical_shift_right))
                            else:
                                step(v.tensor_scalar(fhi[:], fpos[:], 15, None, ALU.bitwise_and))
                            step(v.tensor_copy(ff[:], fhi[:]))
                            f4 = ff[:].rearrange("p h (k o) -> p h k o", o=1).broadcast_to([P, PH, TOPK, TOPK])
                            step(v.tensor_tensor(oh, f4, io, ALU.is_equal))
                            for h in range(PH):
                                ix = topf[:, 2 * h + half, :].rearrange("p (o i) -> p o i", o=1).broadcast_to([P, TOPK, TOPK])
                                step(v.tensor_tensor(oh[:, h], oh[:, h], ix, ALU.mult))
                            dst = eid if half == 0 else ff
                            step(v.tensor_reduce(dst[:], oh, AX_X, ALU.add))
                        step(v.scalar_tensor_tensor(out=eid[:], in0=eid[:], scalar=float(NK), in1=ff[:],
                                                    op0=ALU.mult, op1=ALU.add))
                        step(v.tensor_scalar(eid[:], eid[:], ebase[:, 0:1], None, ALU.add))
                        step(v.tensor_copy(eidx[:, t, :], eid[:].rearrange("p h k -> p (h k)")), "idx_ready")
                        c3 = coef[:, t, :].rearrange("p (h k) -> p h k", h=PH)
                        step(v.tensor_tensor(c3, fval[:, t], fval[:, t, :, 0:1].broadcast_to([P, PH, TOPK]),
                                             ALU.subtract), "gate_max")
                        dve.wait_ge(s["gate_exp"], t + 1)
                        step(v.tensor_reduce(gsum[:, t, 0, :], c3, AX_X, ALU.add))
                        step(v.reciprocal(gsum[:, t, 1, :], gsum[:, t, 0, :]))
                        step(v.tensor_tensor(c3, c3, gsum[:, t, 1, :].rearrange("p (h o) -> p h o", o=1)
                                             .broadcast_to([P, PH, TOPK]), ALU.mult))

                    def rows(ph):
                        t = ph // 2
                        with dve.Fori(0, ROUNDS) as r:
                            for j in range(RING):
                                dve.wait_ge(row_landed[j], l * (2 * NT * ROUNDS * 16) + r * 16 + ph * ROUNDS * 16 + 16)
                                dve.wait_ge(s["row_used"], r * RING + ph * SEL + j + RING)
                                if ph % 2 == 0:
                                    ins = v.scalar_tensor_tensor(out=ringmem[:, j, :], in0=ringmem[:, j, :], scalar=1.0,
                                                                 in1=hm[:, t, :], op0=ALU.mult, op1=ALU.mult,
                                                                 accum_out=dots[:, t, bass.ds(r * RING + j, 1)])
                                else:
                                    ins = v.scalar_tensor_tensor(out=accv[:, t, :], in0=ringmem[:, j, :],
                                                                 scalar=coef[:, t, bass.ds(r * RING + j, 1)],
                                                                 in1=accv[:, t, :], op0=ALU.mult, op1=ALU.add)
                                ins.then_inc(s["row_used"], 1)

                    def coefficients(t):
                        dve.wait_ge(s["row_used"], (2 * t + 1) * SEL + RING)
                        step(v.memset(stat[:, 9:10], 0.0), "act_in")
                        dve.wait_ge(s["gelu_out"], t + 1)
                        step(v.tensor_tensor(coef[:, t, :], coef[:, t, :], dots[:, t, :], ALU.mult))

                    v.memset(accv[:], 0.0).then_inc(s["row_used"], RING)
                    dve.wait_ge(s["row_used"], RING)
                    retrieve(0)
                    rows(0)
                    coefficients(0)
                    retrieve(1)
                    rows(1)
                    rows(2)
                    coefficients(1)
                    rows(3)
                    dve.wait_ge(s["row_used"], 4 * SEL + RING)
                    for t in range(NT):
                        step(v.tensor_tensor(accv[:, t, :], accv[:, t, :], mod[:, 2, :], ALU.mult))
                        step(v.tensor_tensor(xs[:, t, :], xs[:, t, :], accv[:, t, :], ALU.add))
                    step(v.tensor_scalar(ebase[:], ebase[:], float(EXPERTS), None, ALU.add))

            nc.all_engine_barrier(sems_to_clear=clearable)

        with ExitStack() as end, nc.Block() as block:
            fg = sb("fg", [P, D], where=end)

            @block.sync
            def _(sp):
                sp.dma_start(fg[:], final_norm_g.rearrange("(o d) -> o d", o=1).broadcast_to([P, D])).then_inc(s["gain_in"], 16)
                for t in range(NT):
                    sp.wait_ge(s["h_ready"], t + 1)
                    sp.dma_start(out.rearrange("o (t p) d -> p (o t) d", p=P)[:, t, :], hm[:, t, :]).then_inc(s["stored"], 16)
                sp.wait_ge(s["stored"], 16 * NT)

            @block.scalar
            def _(act):
                norm_act(act, hm[:, 0, :])

            @block.vector
            def _(dve):
                step = Steps(dve, "dve_step")
                for t in range(NT):
                    dve.wait_ge(s["ss_ready"], t + 1)
                    step(nc.vector.tensor_scalar(stat[:, 2 + t:3 + t], stat[:, t:t + 1], 1.0 / D, RMS_EPS,
                                                 ALU.mult, ALU.add), "var_ready")
                dve.wait_ge(s["gain_in"], 16)
                for t in range(NT):
                    dve.wait_ge(s["sd_ready"], t + 1)
                    step(nc.vector.reciprocal(stat[:, 6 + t:7 + t], stat[:, 4 + t:5 + t]))
                    step(nc.vector.scalar_tensor_tensor(out=hm[:, t, :], in0=xs[:, t, :], scalar=stat[:, 6 + t:7 + t],
                                                        in1=fg[:], op0=ALU.mult, op1=ALU.mult), "h_ready")


def shape_constants():
    import numpy as np
    a = np.zeros((P, CONSTS), np.float32)

    def put(name, value):
        lo, hi = _off[name]
        a[:, lo:hi] = np.asarray(value, np.float32).reshape(P, hi - lo)

    i = np.arange(P)
    row, col = i[:, None], i[None, :]
    put("ident", row == col)
    same = row // C == col // C
    strict, upto = same & (row < col), same & (row <= col)
    put("amask", np.stack([strict, upto, strict, upto], 1))
    lower = []
    for lev in range(LEVELS):
        b = 1 << lev
        lower.append((row // (2 * b) == col // (2 * b)) & (row // b % 2 == 1) & (col // b % 2 == 0))
    put("xmask", np.stack(lower, 1))
    put("xtmask", np.stack([m.T for m in lower], 1))
    put("pairones", row // HD == col // HD)
    put("headsel", row // HD == np.arange(2)[None, :])
    tok = np.arange(S)[None, :]
    put("cumsel", np.stack([row + P * t <= tok for t in range(NT)], 1))
    put("reset", np.broadcast_to(np.arange(NPAIR * S) % C != 0, (P, NPAIR * S)))
    put("causal", np.concatenate([np.zeros((P, P)), np.where(col > row, BIG, 0.0)], 1))
    fs = np.zeros((P, FOX_H, P))
    for h in range(FOX_H):
        fs[h, h, :] = -1.0 / FOX_SCALE
    put("foxsel", fs)
    put("iota", np.broadcast_to(np.arange(TOPK), (P, TOPK)))
    lam = np.array([0.8 - 0.6 * math.exp(-0.3 * d) for d in range(DEPTH)])
    return a, np.stack([lam, 1.0 - lam], 1).astype(np.float32)


_INS = ["x", "c", "norm_mix_g", "norm_ffn_g", "final_norm_g", "ada_w", "ada_b", "w_in", "w_out", "dif_lam",
        "dif_subln_g", "rw_mu", "rw_w0", "rw_w2", "rw_a0", "rw_a2", "rw_g2", "rw_kk", "rw_ka", "rw_rk", "rw_ln_g",
        "rw_ln_b", "fox_bf", "peer_wq", "peer_subkeys", "peer_u", "peer_v"]


def kernel(**inputs):
    import numpy as _np
    import concourse.bacc as _bacc
    from concourse import mybir as _mybir
    from concourse.bass_utils import run_bass_kernel_spmd as _run

    nc = _bacc.Bacc("TRN2", target_bir_lowering=False, num_devices=1)
    arrays, args = {}, []
    consts, lam_consts = shape_constants()
    for name, a in [(n, _np.ascontiguousarray(inputs[n])) for n in _INS] + [("consts", consts), ("lam_consts", lam_consts)]:
        arrays[f"in_{name}_dram"] = a
        args.append(nc.dram_tensor(f"in_{name}_dram", a.shape, _mybir.dt.from_np(a.dtype), kind="ExternalInput").ap())
    args.append(nc.dram_tensor("out_0_dram", (1, S, D), _mybir.dt.float32, kind="ExternalOutput").ap())
    trunk(nc, *args)
    r = _run(nc, [arrays], core_ids=[0])
    return r.results[0]["out_0_dram"]
```

```python
import math
from contextlib import ExitStack

import concourse.bass as bass
from concourse import mybir

ALU = mybir.AluOpType
ACT = mybir.ActivationFunctionType
F32 = mybir.dt.float32
I32 = mybir.dt.int32
U32 = mybir.dt.uint32
AX_X = mybir.AxisListType.X

P = 128
D = 1024
S = 256
NT = S // P
KD = D // P
DEPTH = 2
HD = 64
DIFF_H, RW_H, FOX_H = 6, 6, 4
W6 = DIFF_H * HD
WF = FOX_H * HD
NPAIR = RW_H // 2
C = 64
NC = S // C
LEVELS = int(math.log2(C))
IN_COLS = 3 * W6 + (3 * W6 + 256) + (3 * WF + FOX_H)
RMS_EPS = 1e-6
LN_EPS = 64e-5
DIFF_SCALE = 32 ** -0.5
FOX_SCALE = 64 ** -0.5
PH, NK, TOPK = 8, 128, 16
EXPERTS = NK * NK
SEL = PH * TOPK
RING = 16
PE_ROWS = (1, 4, 6, 9, 12, 14)
DVE_ROWS = tuple(j for j in range(RING) if j not in PE_ROWS)
WS = 4
BIG = -1e30

_off = {}
_n = 0
for _name, _w in (("ident", P), ("amask", 4 * P), ("xmask", LEVELS * P), ("xtmask", LEVELS * P), ("pairones", P),
                  ("headsel", 2), ("cumsel", NT * S), ("reset", NPAIR * S), ("causal", S), ("foxsel", FOX_H * P),
                  ("iota", TOPK)):
    _off[_name] = (_n, _n + _w)
    _n += _w
CONSTS = _n

DIFF0, RW0, FOX0 = 0, 3 * W6, 6 * W6 + 256
GROUPS = [("r", RW0, W6, "f"), ("k", RW0 + W6, W6, "f"), ("v", RW0 + 2 * W6, W6, "f"), ("x", RW0 + 3 * W6, 256, "f"),
          ("dq", DIFF0, W6, "f"), ("dk", DIFF0 + W6, W6, "f"), ("dv", DIFF0 + 2 * W6, W6, "t"),
          ("fqk", FOX0, 2 * WF, "f"), ("fv", FOX0 + 2 * WF, WF + FOX_H, "t")]
OUTS_OF = [(w // P if kind == "f" else NT) for _, _, w, kind in GROUPS]
COLS = {g[0]: sum(OUTS_OF[:n + 1]) for n, g in enumerate(GROUPS)}


def trunk(nc, x, c, norm_mix_g, norm_ffn_g, final_norm_g, ada_w, ada_b, w_in, w_out, dif_lam, dif_subln_g, rw_mu,
          rw_w0, rw_w2, rw_a0, rw_a2, rw_g2, rw_kk, rw_ka, rw_rk, rw_ln_g, rw_ln_b, fox_bf, peer_wq, peer_subkeys,
          peer_u, peer_v, consts, lam_consts, out):
    gelu, exp, sig = ACT.Gelu, ACT.Exp, ACT.Sigmoid

    with ExitStack() as ctx:
        def sb(name, shape, dt=F32, where=ctx):
            return where.enter_context(nc.sbuf_tensor(name, shape, dt))

        def sem(name):
            return ctx.enter_context(nc.semaphore(name))

        bank = [ctx.enter_context(nc.psum_tensor(f"bank{i}", [P, 512], F32)) for i in range(8)]

        row_landed = [sem(f"row_landed{i}") for i in range(RING)]
        names = ("zero_diag", "gf_out", "gf_taken", "pe_sum_taken", "diag_ready", "coef_ready", "act_pass",
                 "const_in", "params_in", "bias_in", "gain_in", "wout_in", "small_in",
                 "w_in0", "w_in1", "w_in2", "w_in3",
                 "c_ready", "cT", "crep", "pe_out", "mod_ready", "cols_ready", "dve_step", "act_step", "h_ready",
                 "h_turned", "hT_ready", "ss_ready", "var_ready", "sd_ready", "prow_turned", "params_ready",
                 "lora_in", "lora_out", "lora_act", "kk_sq", "kk_sum", "kk_var", "kk_sd", "decay", "decay_exp",
                 "rw_ops", "bonus_out", "tm_turned", "tm_ready", "apair", "apair_sb", "z_out", "z_sb", "xz_out",
                 "x_sb", "av_out", "av_sb", "uw_out", "uw_sb", "sa_out", "sa_sb", "st_out", "st_sb", "y_out",
                 "y_taken", "y_copied", "gate_out", "gate_sb", "s_out", "s_masked", "s_exp", "p_ready", "p_turned", "pT_ready",
                 "pv_out", "o_taken", "f_exp", "f_in", "f_ln", "cum_in", "cum_out", "cum_sb", "lam_in", "lam_exp",
                 "o_var", "o_sd", "y_var", "y_sd", "mix_ready", "mix_turned", "mixT_ready", "mix_out", "x_done",
                 "reset_free", "rpad", "stored", "sk_turned", "sk_ready", "q_out", "q_ready", "score_out",
                 "score_taken", "gate_max", "gate_exp", "idx_ready", "row_used", "idx_step", "pool_pass",
                 "act_in", "gelu_out", "slots_open")
        s = {n: sem(n) for n in names}
        slot_free = [sem(f"slot_free{i}") for i in range(RING)]
        clearable = range(min(q.num for q in s.values()), max(q.num for q in slot_free) + 1)
        assert RING == TOPK and len(clearable) == len(names) + RING and all(q.num not in clearable for q in row_landed)

        class Steps:

            def __init__(self, eng, own):
                self.eng, self.own, self.count = eng, own, {}

            def __call__(self, ins, tell=None):
                q = self.own if tell is None else tell
                self.count[q] = self.count.get(q, 0) + 1
                ins.then_inc(s[q], 1)
                self.eng.wait_ge(s[q], self.count[q])

        K = sb("K", [P, CONSTS])
        const = {n: K[:, a:b] for n, (a, b) in _off.items()}
        ident, pairones = const["ident"], const["pairones"]
        xs = sb("xs", [P, NT, D])
        hm = sb("hm", [P, NT, D])
        hT = sb("hT", [P, KD, S])
        mod = sb("mod", [P, 3, D])
        crep = sb("crep", [P, KD, P])
        ringmem = sb("ringmem", [P, RING, D])
        ringf = ringmem[:].rearrange("p a b -> p (a b)")
        wslot = [ringf[:, i * 4096:(i + 1) * 4096].rearrange("p (k n) -> p k n", k=KD) for i in range(WS)]
        stat = sb("stat", [P, 16])
        ones_c = sb("ones_c", [P, P])
        ebase = sb("ebase", [P, 1])

        def weight_landed(pe, n):
            pe.wait_ge(s[f"w_in{n % WS}"], 16 * (n // WS + 1))

        with ExitStack() as setup, nc.Block() as block:
            c8 = sb("c8", [KD, P], where=setup)
            c8a = sb("c8a", [KD, P], where=setup)
            cT = sb("cT_sb", [P, KD], where=setup)

            @block.sync
            def _(sp):
                sp.dma_start(K[:], consts).then_inc(s["const_in"], 16)
                sp.dma_start(c8[:], c.rearrange("o (k p) -> (o k) p", p=P)).then_inc(s["small_in"], 16)
                sp.dma_start(xs[:], x.rearrange("o (t p) d -> p (o t) d", p=P)).then_inc(s["params_in"], 16)
                sp.wait_ge(s["params_in"], 16)

            @block.scalar
            def _(act):
                act.wait_ge(s["small_in"], 16)
                nc.scalar.activation(c8a[:], c8[:], ACT.Silu).then_inc(s["c_ready"], 1)

            @block.tensor
            def _(pe):
                pe.wait_ge(s["const_in"], 16)
                pe.wait_ge(s["c_ready"], 1)
                nc.tensor.transpose(bank[0][:, 0:KD], c8a[:], ident[0:KD, 0:KD]).then_inc(s["cT"], 1)

            @block.vector
            def _(dve):
                step = Steps(dve, "dve_step")
                step(nc.vector.memset(ones_c[:], 1.0))
                step(nc.vector.memset(ebase[:], 0.0))
                dve.wait_ge(s["cT"], 1)
                step(nc.vector.tensor_copy(cT[:], bank[0][:, 0:KD]))
                for k in range(KD):
                    nc.vector.tensor_scalar(crep[:, k, :], ones_c[:], cT[:, k:k + 1], None,
                                            ALU.mult).then_inc(s["crep"], 1)

        nc.all_engine_barrier(sems_to_clear=clearable)

        def ada_plan(l, half):
            view = ada_w[bass.ds(l, 1)].rearrange("o (k p) n -> p (o k) n", p=P)
            return [(view[:, :, half * 3 * D + 512 * n:half * 3 * D + 512 * (n + 1)], 512,
                     None if n < WS else n - WS + 1) for n in range(6)]

        def load_bias(sp, l, half, rows):
            b = ada_b[bass.ds(l, 1), (half * 3 + rows.start) * D:(half * 3 + rows.stop) * D]
            sp.dma_start(mod[:, rows, :].rearrange("p a d -> p (a d)"),
                         b.broadcast_to([P, (rows.stop - rows.start) * D])).then_inc(s["bias_in"], 16)

        def load_gain(sp, l, gain, gains):
            sp.dma_start(gain, gains[bass.ds(l, 1), :].broadcast_to([P, D])).then_inc(s["gain_in"], 16)

        def ada_pe(pe):
            for n in range(6):
                weight_landed(pe, n)
                if n >= 2:
                    pe.wait_ge(s["mod_ready"], n - 1)
                for k in range(KD):
                    mm = nc.tensor.matmul(bank[n % 2][:, :], crep[:, k, :], wslot[n % WS][:, k, :],
                                          start=(k == 0), stop=(k == KD - 1))
                mm.then_inc(s["pe_out"], 1)

        def take_mod(dve, step, n, out_n, bk):
            dve.wait_ge(s["pe_out"], out_n)
            part = mod[:].rearrange("p a d -> p (a d)")[:, 512 * n:512 * (n + 1)]
            step(nc.vector.tensor_tensor(part, bank[bk][:, :], part, ALU.add), "mod_ready")

        def norm_dve(dve, step, gain, take_mods):
            for t in range(NT):
                dve.wait_ge(s["ss_ready"], t + 1)
                step(nc.vector.tensor_scalar(stat[:, 2 + t:3 + t], stat[:, t:t + 1], 1.0 / D, RMS_EPS,
                                             ALU.mult, ALU.add), "var_ready")
            take_mods()
            dve.wait_ge(s["gain_in"], 16)
            step(nc.vector.scalar_tensor_tensor(out=mod[:, 1, :], in0=mod[:, 1, :], scalar=1.0, in1=gain,
                                                op0=ALU.add, op1=ALU.mult))
            for t in range(NT):
                dve.wait_ge(s["sd_ready"], t + 1)
                step(nc.vector.reciprocal(stat[:, 6 + t:7 + t], stat[:, 4 + t:5 + t]))
                step(nc.vector.scalar_tensor_tensor(out=hm[:, t, :], in0=xs[:, t, :], scalar=stat[:, 6 + t:7 + t],
                                                    in1=mod[:, 1, :], op0=ALU.mult, op1=ALU.mult))
                step(nc.vector.tensor_tensor(hm[:, t, :], hm[:, t, :], mod[:, 0, :], ALU.add), "h_ready")

        def norm_act(act, junk):
            for t in range(NT):
                nc.scalar.activation(junk, xs[:, t, :], ACT.Square,
                                     accum_out=stat[:, t:t + 1]).then_inc(s["ss_ready"], 1)
                act.wait_ge(s["ss_ready"], t + 1)
            for t in range(NT):
                act.wait_ge(s["var_ready"], t + 1)
                nc.scalar.activation(stat[:, 4 + t:5 + t], stat[:, 2 + t:3 + t], ACT.Sqrt).then_inc(s["sd_ready"], 1)

        def turn_pe(pe, src, ready, turned, taken, banks):
            for t in range(NT):
                pe.wait_ge(s[ready], t + 1)
                for b in range(2):
                    n = 2 * t + b
                    if n >= 2:
                        pe.wait_ge(s[taken], n - 1)
                    for j in range(4):
                        k = 4 * b + j
                        tr = nc.tensor.transpose(bank[banks + n % 2][:, j * P:(j + 1) * P],
                                                 src[:, t, k * P:(k + 1) * P], ident)
                    tr.then_inc(s[turned], 1)

        def turn_act(act, turned, taken, banks):
            for t in range(NT):
                for b in range(2):
                    n = 2 * t + b
                    act.wait_ge(s[turned], n + 1)
                    nc.scalar.activation(hT[:, 4 * b:4 * b + 4, t * P:(t + 1) * P],
                                         bank[banks + n % 2][:, :].rearrange("p (j c) -> p j c", j=4),
                                         ACT.Copy).then_inc(s[taken], 1)

        with nc.Fori(0, DEPTH) as l:
            with ExitStack() as mix, nc.Block() as block:
                gain = hm[:, 0, :]
                prow = sb("prow", [26, P], where=mix)
                pcol = sb("pcol", [P, 26], where=mix)
                MU, PW0, PA0, PKK, PKA, PRK = 0, 11, 14, 17, 20, 23
                colsT = sb("colsT", [P, 11, S + 1], where=mix)
                mixed = sb("mixed", [P, 11, S], where=mix)
                w2a2 = sb("w2a2", [P, W6], where=mix)
                g2 = sb("g2", [P, W6], where=mix)
                lnp = sb("lnp", [P, 2, W6], where=mix)
                subg = sb("subg", [P, HD], where=mix)
                lamp = sb("lamp", [P, 4, 32], where=mix)
                lamc = sb("lamc", [P, 2], where=mix)
                small = sb("small", [P, 24], where=mix)
                bfb = sb("bfb", [P, FOX_H], where=mix)
                sgx = sb("sgx", [P, S], where=mix)
                thx = sb("thx", [HD, S], where=mix)
                AL = sb("AL", [P, 2, NPAIR, S], where=mix)
                asig, lw = AL[:, 0], AL[:, 1]
                T12 = sb("T12", [P, 2, NPAIR, S], where=mix)
                T1, T2 = T12[:, 0], T12[:, 1]
                cold = colsT[:].rearrange("p a b -> p (a b)")

                def old(n):
                    return cold[:, 1 + n * NPAIR * S:1 + (n + 1) * NPAIR * S].rearrange("p (a b) -> p a b", a=NPAIR)

                E1, E2, E3 = (old(n) for n in range(3))
                bt, kt = (hT[:, 3 * n:3 * n + 3, :] for n in range(2))
                ar = sb("ar", [P, NPAIR, NT, 2, P], where=mix)
                rpad = sb("rpad_sb", [P, NPAIR, NT, 2, P], where=mix)
                bon = sb("bon", [P, NT, RW_H], where=mix)
                gate = sb("gate", [P, NT, W6], where=mix)
                ST = sb("ST", [P, NC, NPAIR, P], where=mix)
                bv = mixed[:, 0:3, :].rearrange("p a c -> p (a c)").rearrange("p (t c) -> p t c", t=NT)
                alf, t12f = (a[:].rearrange("p a g c -> p (a g c)") for a in (AL, T12))
                stmp = alf[:, 896:1280].rearrange("p (g c) -> p g c", g=NPAIR)
                SA = sb("SA", [P, NT, NPAIR, P], where=mix)
                dq = sb("dq", [P, 3, S], where=mix)
                dk = sb("dk", [P, 3, S], where=mix)
                dv = sb("dv", [P, NT, W6], where=mix)
                fqk = sb("fqk", [P, 4, S], where=mix)
                fv = sb("fv", [P, NT, WF + FOX_H], where=mix)
                fl = sb("fl", [P, 4, NT, FOX_H], where=mix)
                cumT = sb("cumT", [FOX_H, S], where=mix)
                sc = t12f[:, 0:1024].rearrange("p (a b) -> p a b", a=2)
                pn = t12f[:, 1024:1536].rearrange("p (a b) -> p a b", a=2)
                pT = alf[:, 0:512].rearrange("p (a b) -> p a b", a=2)
                ast = sb("ast", [P, 2, 8], where=mix)
                ov = alf[:, 512:896]
                AT = [ringf[:, n * 512:(n + 1) * 512] for n in range(12)]
                X, XT, Z = (ringf[:, 6144 + n * 1536:6144 + (n + 1) * 1536].rearrange("p (g c) -> p g c", g=NPAIR)
                            for n in range(3))
                tm = ringf[:, 10752:10752 + 3072].rearrange("p (g t k c) -> p g t k c", g=NPAIR, t=NT, k=4)
                AV, U, WT = (ringf[:, 13824 + n * 768:13824 + (n + 1) * 768].rearrange("p (t g c) -> p t g c", t=NT, g=NPAIR)
                             for n in range(3))
                wout = ringf[:, 0:8192].rearrange("p (k n) -> p k n", k=KD)
                BTK, KTK, ATK, VTK = range(4)
                proj0 = 6
                nproj = COLS["fv"]

                units = [("d", h, t) for t in range(NT) for h in range(DIFF_H)] + \
                        [("f", h, t) for t in range(NT) for h in range(FOX_H)]
                assert len(units) == 2 * LEVELS + 2 * NC

                @block.sync
                def _(sp):
                    load_bias(sp, l, 0, slice(0, 3))
                    load_gain(sp, l, gain, norm_mix_g)
                    plan = ada_plan(l, 0)
                    for n, (view, width, free_at) in enumerate(plan):
                        if free_at is not None:
                            sp.wait_ge(s["pe_out"], free_at)
                        sp.dma_start(wslot[n % WS][:, :, 0:width], view).then_inc(s[f"w_in{n % WS}"], 16)
                        if n == 0:
                            for row, src, cnt in ((MU, rw_mu, 11), (PW0, rw_w0, 3), (PA0, rw_a0, 3), (PKK, rw_kk, 3),
                                                  (PKA, rw_ka, 3)):
                                sp.dma_start(prow[row:row + cnt, :], src[bass.ds(l, 1), :].rearrange(
                                    "o (c p) -> (o c) p", p=P)).then_inc(s["params_in"], 16)
                            sp.dma_start(prow[PRK:PRK + 3, :], rw_rk[bass.ds(l, 1)].rearrange(
                                "o (c a) d -> (o c) (a d)", a=2)).then_inc(s["params_in"], 16)
                            sp.dma_start(w2a2[0:64, :], rw_w2[bass.ds(l, 1)].rearrange("o p n -> (o p) n")).then_inc(s["lora_in"], 16)
                            sp.dma_start(w2a2[64:128, :], rw_a2[bass.ds(l, 1)].rearrange("o p n -> (o p) n")).then_inc(s["lora_in"], 16)
                            sp.dma_start(g2[:], rw_g2[bass.ds(l, 1)].rearrange("o p n -> (o p) n")).then_inc(s["lora_in"], 16)
                            sp.dma_start(lnp[:, 0, :], rw_ln_g[bass.ds(l, 1), :].broadcast_to([P, W6])).then_inc(s["small_in"], 16)
                            sp.dma_start(lnp[:, 1, :], rw_ln_b[bass.ds(l, 1), :].broadcast_to([P, W6])).then_inc(s["small_in"], 16)
                            sp.dma_start(subg[:], dif_subln_g[bass.ds(l, 1), :].broadcast_to([P, HD])).then_inc(s["small_in"], 16)
                            sp.dma_start(lamp[:].rearrange("p a b -> p (a b)"), dif_lam[bass.ds(l, 1)].rearrange(
                                "o a b -> o (a b)").broadcast_to([P, 128])).then_inc(s["small_in"], 16)
                            sp.dma_start(lamc[:], lam_consts[bass.ds(l, 1), :].broadcast_to([P, 2])).then_inc(s["small_in"], 16)
                            sp.dma_start(bfb[:], fox_bf[bass.ds(l, 1), :].broadcast_to([P, FOX_H])).then_inc(s["small_in"], 16)
                    win = w_in[bass.ds(l, 1)].rearrange("o (k p) n -> p (o k) n", p=P)
                    last_out = [n + 1 for n in range(6)] + [proj0 + COLS[g[0]] for g in GROUPS]
                    for g, (_, c0, w, _) in enumerate(GROUPS):
                        n = 6 + g
                        sp.wait_ge(s["pe_out"], last_out[n - WS])
                        sp.dma_start(wslot[n % WS][:, :, 0:w], win[:, :, c0:c0 + w]).then_inc(s[f"w_in{n % WS}"], 16)
                    sp.wait_ge(s["h_ready"], NT)
                    load_bias(sp, l, 1, slice(0, 2))
                    sp.wait_ge(s["y_out"], NT)
                    for n in range(4):
                        if n == 2:
                            sp.dma_start(wout, w_out[bass.ds(l, 1)].rearrange("o (k p) n -> p (o k) n", p=P)
                                         ).then_inc(s["wout_in"], 16)
                        if n >= 2:
                            sp.wait_ge(s["pe_out"], proj0 + nproj + n - 1)
                        sp.dma_start(wslot[2 + n % 2][:, :, :], ada_plan(l, 1)[n][0]).then_inc(s[f"w_in{2 + n % 2}"], 16)

                @block.gpsimd
                def _(pool):
                    nc.gpsimd.memset(rpad[:], 0.0).then_inc(s["reset_free"], 1)
                    nc.gpsimd.memset(colsT[:, :, 0:1], 0.0).then_inc(s["reset_free"], 1)
                    nc.gpsimd.memset(ST[:, 0], 0.0).then_inc(s["reset_free"], 1)
                    pool.wait_ge(s["pe_out"], proj0 + nproj)
                    for a in (X, XT):
                        nc.gpsimd.tensor_copy(a.rearrange("p g (i c) -> p (g i) c", c=P),
                                              ident.rearrange("p (o c) -> p o c", o=1).broadcast_to([P, 12, P])).then_inc(s["reset_free"], 1)
                    pool.wait_ge(s["rw_ops"], 2)
                    pool.wait_ge(s["reset_free"], 1)
                    for cc in range(2):
                        nc.gpsimd.tensor_copy(rpad[:, :, :, cc, cc * C:(cc + 1) * C].rearrange("p g t c -> p (g t) c"),
                                              ar[:, :, :, 1, cc * C:(cc + 1) * C].rearrange("p g t c -> p (g t) c")
                                              ).then_inc(s["rpad"], 1)

                @block.tensor
                def _(pe):
                    def blocks_z(u):
                        p = u % NPAIR
                        if u >= 2:
                            pe.wait_ge(s["z_sb"], u - 1)
                        if u >= NPAIR:
                            pe.wait_ge(s["x_sb"], 2 * (u - NPAIR) + 2)
                        for j in range(4):
                            mm = nc.tensor.matmul(bank[u % 2][:, j * P:(j + 1) * P], AT[4 * p + j][:, 0:P],
                                                  X[:, p, j * P:(j + 1) * P], start=True, stop=True)
                        mm.then_inc(s["z_out"], 1)

                    def blocks_x(u):
                        p = u % NPAIR
                        pe.wait_ge(s["z_sb"], u + 1)
                        if u:
                            pe.wait_ge(s["x_sb"], 2 * u)
                        if u < (LEVELS - 1) * NPAIR:
                            for j in range(4):
                                nc.tensor.matmul(bank[2][:, j * P:(j + 1) * P], XT[:, p, j * P:(j + 1) * P],
                                                 Z[:, p, j * P:(j + 1) * P], start=True, stop=True)
                        for j in range(4):
                            mm = nc.tensor.matmul(bank[3][:, j * P:(j + 1) * P], Z[:, p, j * P:(j + 1) * P],
                                                  XT[:, p, j * P:(j + 1) * P], start=True, stop=True)
                        mm.then_inc(s["xz_out"], 1)

                    def att_scores(n):
                        kind, h, t = units[n]
                        nk = (t + 1) * P
                        if n:
                            pe.wait_ge(s["s_masked"], n)
                        o = 64 * (h % 2)
                        if kind == "d":
                            for a in range(2):
                                q = slice(o + 32 * a, o + 32 * a + 32)
                                mm = nc.tensor.matmul(bank[4 + a][:, 0:nk], dq[q, h // 2, t * P:(t + 1) * P],
                                                      dk[q, h // 2, 0:nk], start=True, stop=True)
                        else:
                            q = slice(o, o + 64)
                            nc.tensor.matmul(bank[4][:, 0:nk], fqk[q, h // 2, t * P:(t + 1) * P], fqk[q, 2 + h // 2, 0:nk],
                                             start=True, stop=False)
                            mm = nc.tensor.matmul(bank[4][:, 0:nk], const["foxsel"][0:FOX_H, h * P:(h + 1) * P],
                                                  cumT[:, 0:nk], start=False, stop=True)
                        mm.then_inc(s["s_out"], 1)

                    def att_turn(n):
                        kind, h, t = units[n]
                        pe.wait_ge(s["p_ready"], n + 1)
                        if n:
                            pe.wait_ge(s["pT_ready"], n)
                        for j in range(t + 1):
                            tr = nc.tensor.transpose(bank[6][:, j * P:(j + 1) * P], pn[:, n % 2, j * P:(j + 1) * P], ident)
                        tr.then_inc(s["p_turned"], 1)

                    def att_values(n):
                        kind, h, t = units[n]
                        pe.wait_ge(s["pT_ready"], n + 1)
                        if n:
                            pe.wait_ge(s["o_taken"], n)
                        for j in range(t + 1):
                            vals = (dv if kind == "d" else fv)[:, j, h * HD:(h + 1) * HD]
                            mm = nc.tensor.matmul(bank[7][:, 0:HD], pT[:, n % 2, j * P:(j + 1) * P], vals,
                                                  start=(j == 0), stop=(j == t))
                        mm.then_inc(s["pv_out"], 1)

                    def attention(n):
                        if n < len(units):
                            att_scores(n)
                        if 1 <= n <= len(units):
                            att_turn(n - 1)
                        if n >= 2:
                            att_values(n - 2)

                    pe.wait_ge(s["params_in"], 6 * 16)
                    nc.tensor.transpose(bank[7][:, 0:26], prow[:], ident[0:26, 0:26]).then_inc(s["prow_turned"], 1)
                    ada_pe(pe)
                    turn_pe(pe, hm, "h_ready", "h_turned", "hT_ready", 2)
                    pe.wait_ge(s["hT_ready"], 4)
                    m = 0
                    for g, (name, c0, w, kind) in enumerate(GROUPS):
                        n = 6 + g
                        weight_landed(pe, n)
                        wt = wslot[n % WS]
                        for j in range(w // P if kind == "f" else NT):
                            if m >= 2:
                                pe.wait_ge(s["cols_ready"], m - 1)
                            for k in range(KD):
                                if kind == "f":
                                    mm = nc.tensor.matmul(bank[m % 2][:, 0:S], wt[:, k, j * P:(j + 1) * P], hT[:, k, :],
                                                          start=(k == 0), stop=(k == KD - 1))
                                else:
                                    mm = nc.tensor.matmul(bank[m % 2][:, 0:w], hT[:, k, j * P:(j + 1) * P], wt[:, k, 0:w],
                                                          start=(k == 0), stop=(k == KD - 1))
                            mm.then_inc(s["pe_out"], 1)
                            m += 1
                    pe.wait_ge(s["lora_in"], 48)
                    pe.wait_ge(s["act_step"], 2)
                    pe.wait_ge(s["rw_ops"], 1)
                    for j in range(6):
                        r0 = 0 if j < 3 else 64
                        rhs = thx[:, :] if j < 3 else mixed[64:128, 9, :]
                        if j >= 2:
                            pe.wait_ge(s["lora_act"], j - 1)
                        nc.tensor.matmul(bank[2 + j % 2][:, 0:S], w2a2[r0:r0 + 64, (j % 3) * P:(j % 3 + 1) * P], rhs,
                                         start=True, stop=True).then_inc(s["lora_out"], 1)
                    for t in range(NT):
                        nc.tensor.matmul(bank[4 + t][:, 0:W6], sgx[:, t * P:(t + 1) * P], g2[:, :],
                                         start=True, stop=True).then_inc(s["gate_out"], 1)
                    pe.wait_ge(s["kk_sq"], 1)
                    for p in range(NPAIR):
                        mm = nc.tensor.matmul(bank[6 + p // 2][:, (p % 2) * S:(p % 2 + 1) * S], pairones, T1[:, p, :],
                                              start=True, stop=True)
                    mm.then_inc(s["kk_sum"], 1)

                    pe.wait_ge(s["cum_in"], 1)
                    for t in range(NT):
                        mm = nc.tensor.matmul(bank[0][0:FOX_H, 0:S], fl[:, 3, t, :],
                                              const["cumsel"][:, t * S:(t + 1) * S], start=(t == 0), stop=(t == NT - 1))
                    mm.then_inc(s["cum_out"], 1)

                    pe.wait_ge(s["rw_ops"], 3)
                    pe.wait_ge(s["lora_act"], 6)
                    pe.wait_ge(s["kk_var"], 1)
                    for n in range(6):
                        p, t = n // 2, n % 2
                        if n >= 2:
                            pe.wait_ge(s["tm_ready"], n - 1)
                        for kind, src in ((BTK, bt[:, p, t * P:(t + 1) * P]), (KTK, kt[:, p, t * P:(t + 1) * P]),
                                          (ATK, ar[:, p, t, 0, :]), (VTK, mixed[:, 6 + p, t * P:(t + 1) * P])):
                            tr = nc.tensor.transpose(bank[2 + n % 2][:, kind * P:(kind + 1) * P], src, ident)
                        tr.then_inc(s["tm_turned"], 1)
                    pe.wait_ge(s["gate_sb"], NT)
                    for n in range(12):
                        p, t, par = n // 4, (n // 2) % 2, n % 2
                        if n >= 2:
                            pe.wait_ge(s["apair_sb"], n - 1)
                        q = slice(64 * par, 64 * par + 64)
                        rhs = ar[q, p, t, :, :].rearrange("p a c -> p (a c)")
                        for o, left in ((0, bt), (256, kt)):
                            mm = nc.tensor.matmul(bank[4 + n % 2][:, o:o + 256], left[q, p, t * P:(t + 1) * P], rhs,
                                                  start=True, stop=True)
                        mm.then_inc(s["apair"], 1)
                    pe.wait_ge(s["rw_ops"], 4)
                    for t in range(NT):
                        for p in range(NPAIR):
                            mm = nc.tensor.matmul(bank[6][:, t * 8 + 2 * p:t * 8 + 2 * p + 2], T2[:, p, t * P:(t + 1) * P],
                                                  const["headsel"], start=True, stop=True)
                    mm.then_inc(s["bonus_out"], 1)

                    pe.wait_ge(s["apair_sb"], 12)
                    pe.wait_ge(s["reset_free"], 5)
                    pe.wait_ge(s["tm_ready"], 6)
                    pe.wait_ge(s["y_taken"], 1)
                    pe.wait_ge(s["cum_sb"], 1)
                    for lev in range(LEVELS):
                        first = lev * NPAIR
                        blocks_z(first)
                        blocks_z(first + 1)
                        attention(2 * lev)
                        blocks_x(first)
                        blocks_z(first + 2)
                        blocks_x(first + 1)
                        attention(2 * lev + 1)
                        blocks_x(first + 2)
                    pe.wait_ge(s["x_sb"], LEVELS * 6)
                    for t in range(NT):
                        for p in range(NPAIR):
                            for par in range(2):
                                mm = nc.tensor.matmul(bank[t][:, p * P + par * 64:p * P + par * 64 + 64],
                                                      AT[4 * p + 2 * t + par][:, 256:384],
                                                      tm[:, p, t, VTK, par * 64:par * 64 + 64], start=True, stop=True)
                        mm.then_inc(s["av_out"], 1)
                    pe.wait_ge(s["av_sb"], NT)
                    for t in range(NT):
                        if t:
                            pe.wait_ge(s["uw_sb"], 1)
                        for p in range(NPAIR):
                            for par in range(2):
                                xt = XT[:, p, (2 * t + par) * P:(2 * t + par + 1) * P]
                                nc.tensor.matmul(bank[2][:, p * P + par * 64:p * P + par * 64 + 64], xt,
                                                 AV[:, t, p, par * 64:par * 64 + 64], start=True, stop=True)
                                mm = nc.tensor.matmul(bank[par][:, p * P:(p + 1) * P], tm[:, p, t, ATK, :], xt,
                                                      start=True, stop=True)
                        mm.then_inc(s["uw_out"], 1)
                    pe.wait_ge(s["uw_sb"], NT)
                    for cc in range(NC):
                        t, o = cc // 2, slice(64 * (cc % 2), 64 * (cc % 2) + 64)
                        if cc:
                            pe.wait_ge(s["st_sb"], cc)
                        for p in range(NPAIR):
                            mm = nc.tensor.matmul(bank[2][:, p * P:(p + 1) * P], WT[:, t, p, :], ST[:, cc, p, :],
                                                  start=True, stop=True)
                        mm.then_inc(s["sa_out"], 1)
                        attention(2 * LEVELS + 2 * cc)
                        if cc < NC - 1:
                            pe.wait_ge(s["sa_sb"], cc + 1)
                            for p in range(NPAIR):
                                nc.tensor.matmul(bank[3][:, p * P:(p + 1) * P], tm[o, p, t, KTK, :], tm[o, p, t, VTK, :],
                                                 start=True, stop=False)
                                mm = nc.tensor.matmul(bank[3][:, p * P:(p + 1) * P], tm[o, p, t, BTK, :],
                                                      SA[o, t, p, :], start=False, stop=True)
                            mm.then_inc(s["st_out"], 1)
                        attention(2 * LEVELS + 2 * cc + 1)
                    pe.wait_ge(s["rpad"], 2)
                    pe.wait_ge(s["sa_sb"], NC)
                    for t in range(NT):
                        for p in range(NPAIR):
                            whole = bank[t][:, p * P:(p + 1) * P]
                            for cc in range(2):
                                nc.tensor.matmul(whole, rpad[:, p, t, cc, :], ST[:, 2 * t + cc, p, :],
                                                 start=(cc == 0), stop=False, skip_group_check=True)
                            for par in range(2):
                                half = bank[t][:, p * P + 64 * par:p * P + 64 * par + 64]
                                a = AT[4 * p + 2 * t + par]
                                nc.tensor.matmul(half, a[:, 128:256], SA[:, t, p, 64 * par:64 * par + 64],
                                                 start=False, stop=False, skip_group_check=True)
                                mm = nc.tensor.matmul(half, a[:, 384:512], tm[:, p, t, VTK, 64 * par:64 * par + 64],
                                                      start=False, stop=True, skip_group_check=True)
                        mm.then_inc(s["y_out"], 1)
                    attention(len(units))
                    attention(len(units) + 1)

                    def next_mod(n):
                        had = sum(q % WS == 2 + n % 2 for q in range(6 + len(GROUPS)))
                        pe.wait_ge(s[f"w_in{2 + n % 2}"], 16 * (had + n // 2 + 1))
                        if n >= 2:
                            pe.wait_ge(s["mod_ready"], 6 + n - 1)
                        for k in range(KD):
                            mm = nc.tensor.matmul(bank[2 + n % 2][:, :], crep[:, k, :], wslot[2 + n % 2][:, k, :],
                                                  start=(k == 0), stop=(k == KD - 1))
                        mm.then_inc(s["pe_out"], 1)

                    next_mod(0)
                    next_mod(1)
                    turn_pe(pe, hm, "mix_ready", "mix_turned", "mixT_ready", 0)
                    pe.wait_ge(s["mixT_ready"], 4)
                    pe.wait_ge(s["wout_in"], 16)
                    for t in range(NT):
                        for b in range(2):
                            for k in range(KD):
                                mm = nc.tensor.matmul(bank[4 + 2 * t + b][:, :], hT[:, k, t * P:(t + 1) * P],
                                                      wout[:, k, b * 512:(b + 1) * 512],
                                                      start=(k == 0), stop=(k == KD - 1))
                            mm.then_inc(s["mix_out"], 1)
                    next_mod(2)
                    next_mod(3)

                @block.scalar
                def _(act):
                    junk = t12f[:, 0:1024]
                    norm_act(act, junk)
                    turn_act(act, "h_turned", "hT_ready", 2)
                    dest = {"r": colsT[:, 0:3, 1:], "k": colsT[:, 3:6, 1:], "v": colsT[:, 6:9, 1:], "x": colsT[:, 9:11, 1:],
                            "dq": dq, "dk": dk, "dv": dv, "fqk": fqk, "fv": fv}

                    def take(name):
                        g = [q[0] for q in GROUPS].index(name)
                        w, kind = GROUPS[g][2], GROUPS[g][3]
                        first = COLS[name] - OUTS_OF[g]
                        for j in range(OUTS_OF[g]):
                            m = first + j
                            act.wait_ge(s["pe_out"], proj0 + m + 1)
                            nc.scalar.activation(dest[name][:, j, 0:(S if kind == "f" else w)],
                                                 bank[m % 2][:, 0:(S if kind == "f" else w)],
                                                 ACT.Copy).then_inc(s["cols_ready"], 1)

                    for name in ("r", "k", "v", "x", "dq"):
                        take(name)
                    act.wait_ge(s["rw_ops"], 1)
                    nc.scalar.activation(thx[:], mixed[0:64, 9, :], ACT.Tanh).then_inc(s["act_step"], 1)
                    nc.scalar.activation(sgx[:], mixed[:, 10, :], sig).then_inc(s["act_step"], 1)
                    act.wait_ge(s["kk_sq"], 1)
                    for name in ("dk", "dv", "fqk", "fv"):
                        take(name)
                    for j in range(6):
                        act.wait_ge(s["lora_out"], j + 1)
                        dst = lw[:, j, :] if j < 3 else asig[:, j - 3, :]
                        nc.scalar.activation(dst, bank[2 + j % 2][:, 0:S], sig, bias=pcol[:, PW0 + j:PW0 + j + 1]
                                             ).then_inc(s["lora_act"], 1)
                    for t in range(NT):
                        act.wait_ge(s["gate_out"], t + 1)
                        nc.scalar.activation(gate[:, t, :], bank[4 + t][:, 0:W6], ACT.Copy).then_inc(s["gate_sb"], 1)
                    act.wait_ge(s["decay"], 1)
                    nc.scalar.activation(E2, E1, exp).then_inc(s["decay_exp"], 1)
                    nc.scalar.activation(E3, E1, exp, scale=-1.0).then_inc(s["decay_exp"], 1)
                    act.wait_ge(s["decay"], 2)
                    nc.scalar.activation(lw, lw, exp).then_inc(s["decay_exp"], 1)
                    act.wait_ge(s["f_in"], 1)
                    nc.scalar.activation(fl[:, 2], fl[:, 1], exp, scale=-1.0).then_inc(s["f_exp"], 1)
                    act.wait_ge(s["lam_in"], 1)
                    nc.scalar.activation(small[:, 2:4], small[:, 0:2], exp).then_inc(s["lam_exp"], 1)
                    act.wait_ge(s["f_exp"], 1)
                    nc.scalar.activation(fl[:, 1], fl[:, 2], ACT.Ln, bias=1.0).then_inc(s["f_ln"], 1)
                    act.wait_ge(s["kk_var"], 1)
                    nc.scalar.activation(T1, T1, ACT.Sqrt).then_inc(s["kk_sd"], 1)
                    for n in range(6):
                        act.wait_ge(s["tm_turned"], n + 1)
                        nc.scalar.activation(tm[:, n // 2, n % 2].rearrange("p k c -> p (k c)"), bank[2 + n % 2][:, :],
                                             ACT.Copy).then_inc(s["tm_ready"], 1)
                    act.wait_ge(s["cum_out"], 1)
                    nc.scalar.activation(cumT[:], bank[0][0:FOX_H, 0:S], ACT.Copy).then_inc(s["cum_sb"], 1)
                    def take_z(u):
                        act.wait_ge(s["z_out"], u + 1)
                        nc.scalar.activation(Z[:, u % NPAIR, :], bank[u % 2][:, :], ACT.Copy).then_inc(s["z_sb"], 1)

                    def attention(n):
                        if n < len(units):
                            kind, h, t = units[n]
                            nk = (t + 1) * P
                            act.wait_ge(s["s_masked"], n + 1)
                            for a in range(2 if kind == "d" else 1):
                                ins = nc.scalar.activation(sc[:, n % 2, a * S:a * S + nk], sc[:, n % 2, a * S:a * S + nk],
                                                           exp, bias=ast[:, n % 2, a:a + 1],
                                                           scale=DIFF_SCALE if kind == "d" else FOX_SCALE,
                                                           accum_out=ast[:, n % 2, 2 + a:3 + a])
                            ins.then_inc(s["s_exp"], 1)
                        if 1 <= n <= len(units):
                            m = n - 1
                            nk = (units[m][2] + 1) * P
                            act.wait_ge(s["p_turned"], m + 1)
                            nc.scalar.activation(pT[:, m % 2, 0:nk], bank[6][:, 0:nk], ACT.Copy).then_inc(s["pT_ready"], 1)
                        if n >= 2:
                            kind, h, t = units[n - 2]
                            c0 = h * HD + (0 if kind == "d" else 2 * W6)
                            act.wait_ge(s["pv_out"], n - 1)
                            nc.scalar.activation(hm[:, t, c0:c0 + HD], bank[7][:, 0:HD], ACT.Copy).then_inc(s["o_taken"], 1)

                    for lev in range(LEVELS):
                        take_z(lev * NPAIR)
                        take_z(lev * NPAIR + 1)
                        attention(2 * lev)
                        take_z(lev * NPAIR + 2)
                        attention(2 * lev + 1)
                    for n in range(2 * LEVELS, len(units) + 2):
                        attention(n)
                    for t in range(NT):
                        act.wait_ge(s["o_var"], t + 1)
                        nc.scalar.activation(small[:, 12:18] if t == 0 else small[:, 18:24], small[:, 6:12], ACT.Sqrt
                                             ).then_inc(s["o_sd"], 1)
                    for t in range(NT):
                        act.wait_ge(s["y_var"], t + 1)
                        nc.scalar.activation(small[:, 12:18] if t == 0 else small[:, 18:24], small[:, 6:12], ACT.Sqrt
                                             ).then_inc(s["y_sd"], 1)
                    turn_act(act, "mix_turned", "mixT_ready", 0)

                @block.vector
                def _(dve):
                    v = nc.vector
                    step = Steps(dve, "dve_step")
                    dve.wait_ge(s["prow_turned"], 1)
                    step(v.tensor_copy(pcol[:], bank[7][:, 0:26]), "params_ready")

                    def take_mods():
                        dve.wait_ge(s["bias_in"], 16)
                        for n in range(6):
                            take_mod(dve, step, n, n + 1, n % 2)

                    norm_dve(dve, step, gain, take_mods)
                    dve.wait_ge(s["small_in"], 6 * 16)
                    lprod = ov[:, 0:64].rearrange("p (a b) -> p a b", a=2)
                    step(v.tensor_tensor(lprod, lamp[:, 0:4:2, :], lamp[:, 1:4:2, :], ALU.mult))
                    step(v.tensor_reduce(small[:, 0:2], lprod, AX_X, ALU.add), "lam_in")

                    dve.wait_ge(s["reset_free"], 3)
                    for name, a, b in (("r", 0, 3), ("k", 3, 6), ("v", 6, 9), ("x", 9, 11)):
                        dve.wait_ge(s["cols_ready"], COLS[name])
                        step(v.tensor_tensor(mixed[:, a:b, :], colsT[:, a:b, 0:S], colsT[:, a:b, 1:S + 1], ALU.subtract))
                        for q in range(a, b):
                            ins = v.scalar_tensor_tensor(out=mixed[:, q, :], in0=mixed[:, q, :],
                                                         scalar=pcol[:, MU + q:MU + q + 1], in1=colsT[:, q, 1:S + 1],
                                                         op0=ALU.mult, op1=ALU.add)
                            if q == 10:
                                step(ins, "rw_ops")
                            else:
                                step(ins)

                    def bc(o):
                        return pcol[:, o:o + 3].rearrange("p (a b) -> p a b", b=1).broadcast_to([P, NPAIR, S])

                    r_, k_, v_ = mixed[:, 0:3, :], mixed[:, 3:6, :], mixed[:, 6:9, :]
                    step(v.tensor_tensor(T2, k_, bc(PKK), ALU.mult))
                    step(v.tensor_tensor(T1, T2, T2, ALU.mult), "kk_sq")
                    dve.wait_ge(s["cols_ready"], nproj)
                    z = fl[:, 0]
                    step(v.tensor_tensor(z, fv[:, :, WF:], bfb[:].rearrange("p (a b) -> p a b", a=1).broadcast_to([P, NT, FOX_H]), ALU.add))
                    step(v.tensor_scalar(fl[:, 1], z, -1.0, None, ALU.mult))
                    step(v.tensor_tensor(fl[:, 1], fl[:, 1], z, ALU.max), "f_in")
                    dve.wait_ge(s["kk_sum"], 1)
                    step(v.tensor_scalar(T1[:, 0:2, :].rearrange("p a b -> p (a b)"), bank[6][:, :], 1e-24, None, ALU.max))
                    step(v.tensor_scalar(T1[:, 2, :], bank[7][:, 0:S], 1e-24, None, ALU.max), "kk_var")
                    dve.wait_ge(s["lora_act"], 6)
                    step(v.tensor_scalar(lw, lw, -math.exp(-0.5), None, ALU.mult))
                    step(v.tensor_tensor_scan(E1.rearrange("p a b -> p (a b)"), const["reset"],
                                              lw.rearrange("p a b -> p (a b)"), 0.0, ALU.mult, ALU.add), "decay")
                    step(v.tensor_tensor(lw, E1, lw, ALU.subtract), "decay")
                    dve.wait_ge(s["f_ln"], 1)
                    step(v.scalar_tensor_tensor(out=fl[:, 3], in0=z, scalar=0.0, in1=fl[:, 1],
                                                op0=ALU.min, op1=ALU.subtract), "cum_in")
                    dve.wait_ge(s["decay_exp"], 3)
                    step(v.tensor_tensor(ar[:, :, :, 1, :], r_.rearrange("p g (t c) -> p g t c", t=NT),
                                         E2.rearrange("p g (t c) -> p g t c", t=NT), ALU.mult), "rw_ops")
                    step(v.scalar_tensor_tensor(out=E1, in0=asig, scalar=-1.0, in1=bc(PKA), op0=ALU.add, op1=ALU.mult))
                    step(v.scalar_tensor_tensor(out=E1, in0=E1, scalar=1.0, in1=k_, op0=ALU.add, op1=ALU.mult))
                    step(v.tensor_tensor(kt, E1, E3, ALU.mult))
                    dve.wait_ge(s["kk_sd"], 1)
                    step(v.reciprocal(T1, T1))
                    step(v.scalar_tensor_tensor(out=T2, in0=T2, scalar=-1.0, in1=T1, op0=ALU.mult, op1=ALU.mult))
                    step(v.tensor_tensor(ar[:, :, :, 0, :], T2.rearrange("p g (t c) -> p g t c", t=NT),
                                         lw.rearrange("p g (t c) -> p g t c", t=NT), ALU.mult))
                    step(v.scalar_tensor_tensor(out=asig, in0=T2, scalar=-1.0, in1=asig, op0=ALU.mult, op1=ALU.mult))
                    step(v.tensor_tensor(bt, asig, E3, ALU.mult), "rw_ops")
                    step(v.tensor_tensor(T2, r_, E1, ALU.mult))
                    step(v.tensor_tensor(T2, T2, bc(PRK), ALU.mult), "rw_ops")
                    for n in range(12):
                        dve.wait_ge(s["apair"], n + 1)
                        step(v.tensor_tensor(AT[n], bank[4 + n % 2][:, :], const["amask"], ALU.mult), "apair_sb")
                    dve.wait_ge(s["bonus_out"], 1)
                    dve.wait_ge(s["tm_ready"], 6)
                    step(v.tensor_copy(bon[:], bank[6][:, 0:16].rearrange("p (t h) -> p t h", t=NT)[:, :, 0:RW_H]), "y_taken")
                    for t in range(NT):
                        step(v.tensor_tensor(bv[:, t, :].rearrange("p (g a d) -> p g a d", g=NPAIR, a=2),
                                             tm[:, :, t, VTK, :].rearrange("p g (a d) -> p g a d", a=2),
                                             bon[:, t, :].rearrange("p (g a o) -> p g a o", g=NPAIR, o=1).broadcast_to([P, NPAIR, 2, HD]),
                                             ALU.mult), "y_taken")
                    dve.wait_ge(s["lam_exp"], 1)
                    step(v.tensor_tensor(small[:, 4:5], small[:, 3:4], small[:, 2:3], ALU.subtract))
                    step(v.tensor_tensor(small[:, 4:5], small[:, 4:5], lamc[:, 0:1], ALU.subtract))
                    step(v.tensor_scalar(subg[:], subg[:], lamc[:, 1:2], None, ALU.mult))

                    def mask4(name, lev):
                        a = const[name][:, lev * P:(lev + 1) * P].rearrange("p (o c) -> p o c", o=1)
                        return a.broadcast_to([P, 4, P]).bitcast(I32)

                    def four(a):
                        return a.rearrange("p (j c) -> p j c", j=4)

                    def take_x(u):
                        lev, p = u // NPAIR, u % NPAIR
                        dve.wait_ge(s["xz_out"], u + 1)
                        if lev < LEVELS - 1:
                            step(v.copy_predicated(four(X[:, p, :]), mask4("xmask", lev), four(bank[2][:, :])), "x_sb")
                        else:
                            step(v.tensor_copy(stat[:, 8:9], stat[:, 6:7]), "x_sb")
                        step(v.copy_predicated(four(XT[:, p, :]), mask4("xtmask", lev), four(bank[3][:, :])), "x_sb")

                    def attention(n):
                        if 1 <= n <= len(units):
                            m = n - 1
                            kind, h, t = units[m]
                            nk = (t + 1) * P
                            st = ast[:, m % 2, :]
                            na = 2 if kind == "d" else 1
                            dve.wait_ge(s["s_exp"], m + 1)
                            step(v.reciprocal(st[:, 4:4 + na], st[:, 2:2 + na]))
                            if kind == "d":
                                step(v.tensor_tensor(st[:, 5:6], st[:, 5:6], small[:, 4:5], ALU.mult))
                                step(v.tensor_scalar(sc[:, m % 2, 0:nk], sc[:, m % 2, 0:nk], st[:, 4:5], None, ALU.mult))
                                step(v.scalar_tensor_tensor(out=pn[:, m % 2, 0:nk], in0=sc[:, m % 2, S:S + nk],
                                                            scalar=st[:, 5:6], in1=sc[:, m % 2, 0:nk],
                                                            op0=ALU.mult, op1=ALU.add), "p_ready")
                            else:
                                step(v.tensor_scalar(pn[:, m % 2, 0:nk], sc[:, m % 2, 0:nk], st[:, 4:5], None, ALU.mult),
                                     "p_ready")
                        if n < len(units):
                            kind, h, t = units[n]
                            nk = (t + 1) * P
                            na = 2 if kind == "d" else 1
                            a_ = sc[:, n % 2, :].rearrange("p (a c) -> p a c", a=2)[:, 0:na, 0:nk]
                            st = ast[:, n % 2, :]
                            dve.wait_ge(s["s_out"], n + 1)
                            for a in range(na):
                                step(v.tensor_tensor(a_[:, a, :], bank[4 + a][:, 0:nk], const["causal"][:, S - nk:S], ALU.add))
                            step(v.tensor_reduce(st[:, 0:na], a_, AX_X, ALU.max))
                            step(v.tensor_scalar(st[:, 0:na], st[:, 0:na], -(DIFF_SCALE if kind == "d" else FOX_SCALE), None,
                                                 ALU.mult), "s_masked")

                    for lev in range(LEVELS):
                        attention(2 * lev)
                        take_x(lev * NPAIR)
                        take_x(lev * NPAIR + 1)
                        attention(2 * lev + 1)
                        take_x(lev * NPAIR + 2)
                    for t in range(NT):
                        dve.wait_ge(s["av_out"], t + 1)
                        step(v.tensor_copy(AV[:, t].rearrange("p g c -> p (g c)"), bank[t][:, 0:W6]), "av_sb")
                    for t in range(NT):
                        dve.wait_ge(s["uw_out"], t + 1)
                        step(v.tensor_copy(U[:, t].rearrange("p g c -> p (g c)"), bank[2][:, 0:W6]))
                        for par in range(2):
                            q = slice(64 * par, 64 * par + 64)
                            ins = v.tensor_copy(WT[q, t].rearrange("p g c -> p (g c)"), bank[par][q, 0:W6])
                            step(ins, "uw_sb") if par else step(ins)
                    for cc in range(NC):
                        t, o = cc // 2, slice(64 * (cc % 2), 64 * (cc % 2) + 64)
                        dve.wait_ge(s["sa_out"], cc + 1)
                        step(v.tensor_tensor(SA[o, t].rearrange("p g c -> p (g c)"), bank[2][o, 0:W6],
                                             U[o, t].rearrange("p g c -> p (g c)"), ALU.add), "sa_sb")
                        attention(2 * LEVELS + 2 * cc)
                        if cc < NC - 1:
                            dve.wait_ge(s["st_out"], cc + 1)
                            step(v.tensor_tensor(stmp, bank[3][:, 0:W6].rearrange("p (g c) -> p g c", g=NPAIR),
                                                 ST[:, cc], ALU.add))
                            last = E2[:, :, cc * C + C - 1:cc * C + C]
                            step(v.tensor_tensor(stmp, stmp, last.broadcast_to([P, NPAIR, P]), ALU.mult))
                            step(v.tensor_tensor(ST[:, cc + 1], stmp, pairones.rearrange("p (o c) -> p o c", o=1)
                                                 .broadcast_to([P, NPAIR, P]), ALU.mult), "st_sb")
                        attention(2 * LEVELS + 2 * cc + 1)
                    attention(len(units))

                    def head6(a):
                        return a.rearrange("p (h d) -> p h d", h=6)

                    def col6(a):
                        return a.rearrange("p (h o) -> p h o", o=1).broadcast_to([P, 6, HD])

                    for t in range(NT):
                        dve.wait_ge(s["y_out"], t + 1)
                        step(v.tensor_copy(hm[:, t, W6:2 * W6], bank[t][:, 0:W6]), "y_copied")
                    dve.wait_ge(s["o_taken"], len(units))
                    for t in range(NT):
                        o = hm[:, t, 0:W6]
                        step(v.tensor_tensor(ov, o, o, ALU.mult))
                        step(v.tensor_reduce(small[:, 6:12], head6(ov), AX_X, ALU.add))
                        step(v.tensor_scalar(small[:, 6:12], small[:, 6:12], 1.0 / HD, RMS_EPS, ALU.mult, ALU.add), "o_var")
                        dve.wait_ge(s["o_sd"], t + 1)
                        sd = small[:, 12:18] if t == 0 else small[:, 18:24]
                        step(v.reciprocal(sd, sd))
                        step(v.tensor_tensor(head6(o), head6(o), col6(sd), ALU.mult))
                        step(v.tensor_tensor(head6(o), head6(o), subg[:].rearrange("p (o d) -> p o d", o=1)
                                             .broadcast_to([P, 6, HD]), ALU.mult))
                    dve.wait_ge(s["gate_sb"], NT)
                    for t in range(NT):
                        y = hm[:, t, W6:2 * W6]
                        step(v.tensor_reduce(small[:, 6:12], head6(y), AX_X, ALU.add))
                        step(v.tensor_scalar(small[:, 6:12], small[:, 6:12], 1.0 / HD, None, ALU.mult))
                        step(v.tensor_tensor(head6(y), head6(y), col6(small[:, 6:12]), ALU.subtract))
                        step(v.tensor_tensor(ov, y, y, ALU.mult))
                        step(v.tensor_reduce(small[:, 6:12], head6(ov), AX_X, ALU.add))
                        step(v.tensor_scalar(small[:, 6:12], small[:, 6:12], 1.0 / HD, LN_EPS, ALU.mult, ALU.add), "y_var")
                        dve.wait_ge(s["y_sd"], t + 1)
                        sd = small[:, 12:18] if t == 0 else small[:, 18:24]
                        step(v.reciprocal(sd, sd))
                        step(v.tensor_tensor(head6(y), head6(y), col6(sd), ALU.mult))
                        step(v.tensor_tensor(y, y, lnp[:, 0, :], ALU.mult))
                        step(v.tensor_tensor(y, y, lnp[:, 1, :], ALU.add))
                        step(v.tensor_tensor(y, y, bv[:, t, :], ALU.add))
                        step(v.tensor_tensor(y, y, gate[:, t, :], ALU.mult), "mix_ready")
                        if t == 0:
                            dve.wait_ge(s["bias_in"], 32)
                        take_mod(dve, step, t, proj0 + nproj + t + 1, 2 + t)
                    for t in range(NT):
                        for b in range(2):
                            dve.wait_ge(s["mix_out"], 2 * t + b + 1)
                            q = slice(b * 512, (b + 1) * 512)
                            step(v.tensor_tensor(hm[:, t, q], bank[4 + 2 * t + b][:, :], mod[:, 2, q], ALU.mult))
                            step(v.tensor_tensor(xs[:, t, q], xs[:, t, q], hm[:, t, q], ALU.add))
                    for n in (2, 3):
                        take_mod(dve, step, n, proj0 + nproj + n + 1, 2 + n % 2)

            nc.all_engine_barrier(sems_to_clear=clearable)

            with ExitStack() as peer, nc.Block() as block:
                gain = hm[:, 0, :]
                whead = sb("whead", [P, 2, KD, 256], where=peer)
                qh = sb("qh", [P, 2, 2, S], where=peer)
                diag = sb("diag", [P, len(PE_ROWS), P], where=peer)
                sk = sb("sk", [P, 2 * PH, P], where=peer)
                skT = sb("skT", [P, 2 * PH, P], where=peer)
                score = sb("score", [P, NT, 2 * PH, NK], where=peer)
                top = sb("top", [P, 2 * PH, TOPK], where=peer)
                topi = sb("topi", [P, 2 * PH, TOPK], U32, where=peer)
                topf = sb("topf", [P, 2 * PH, TOPK], where=peer)
                cand = sb("cand", [P, 4, TOPK * TOPK], where=peer)
                fval = sb("fval", [P, NT, PH, TOPK], where=peer)
                fpos = sb("fpos", [P, PH, TOPK], U32, where=peer)
                fhi = sb("fhi", [P, PH, TOPK], U32, where=peer)
                ff = sb("ff", [P, PH, TOPK], where=peer)
                eid = sb("eid", [P, PH, TOPK], where=peer)
                eidx = sb("eidx", [P, NT, SEL], I32, where=peer)
                zidx = sb("zidx", [P, RING], I32, where=peer)
                islot = sb("islot", [P, 2, RING], I32, where=peer)
                gsum = sb("gsum", [P, NT, 2, PH], where=peer)
                dots = sb("dots", [P, NT, SEL], where=peer)
                coef = sb("coef", [P, NT, SEL], where=peer)
                accv = sb("accv", [P, NT, D], where=peer)
                zdiag = sb("zdiag", [P, P], where=peer)
                ROUNDS = SEL // RING

                @block.sync
                def _(sp):
                    load_gain(sp, l, gain, norm_ffn_g)
                    load_bias(sp, l, 1, slice(2, 3))
                    keys = peer_subkeys[bass.ds(l, 1)].rearrange("o h c n d -> (o h c) n d")
                    wq = peer_wq[bass.ds(l, 1)].rearrange("o (k p) n -> p (o k) n", p=P)
                    ada = ada_w[bass.ds(l, 1)].rearrange("o (k p) n -> p (o k) n", p=P)
                    for n in range(PH + 4):
                        if 2 <= n < PH + 2:
                            sp.wait_ge(s["q_out"], 2 * (n - 1))
                        elif n >= PH + 2:
                            sp.wait_ge(s["gf_out"], n - PH - 1)
                        src = wq[:, :, n * 256:(n + 1) * 256] if n < PH else \
                            ada[:, :, 5 * D + (n - PH) * 256:5 * D + (n - PH + 1) * 256]
                        sp.dma_start(whead[:, n % 2], src).then_inc(s[f"w_in{n % 2}"], 16)
                        if n == 1:
                            for hc in range(2 * PH):
                                sp.dma_start(sk[:, hc, :], keys[hc]).then_inc(s["small_in"], 16)

                @block.tensor
                def _(pe):
                    pe.wait_ge(s["small_in"], 2 * PH * 16)
                    for b in range(4):
                        if b >= 2:
                            pe.wait_ge(s["sk_ready"], b - 1)
                        for j in range(4):
                            tr = nc.tensor.transpose(bank[4 + b % 2][:, j * P:(j + 1) * P], sk[:, 4 * b + j, :], ident)
                        tr.then_inc(s["sk_turned"], 1)
                    turn_pe(pe, hm, "h_ready", "h_turned", "hT_ready", 2)
                    pe.wait_ge(s["hT_ready"], 4)
                    pe.wait_ge(s["sk_ready"], 4)
                    for h in range(PH):
                        pe.wait_ge(s[f"w_in{h % 2}"], 16 * (h // 2 + 1))
                        for cc in range(2):
                            m = 2 * h + cc
                            if m >= 2:
                                pe.wait_ge(s["q_ready"], m - 1)
                            for k in range(KD):
                                mm = nc.tensor.matmul(bank[cc][:, 0:S], whead[:, h % 2, k, cc * P:(cc + 1) * P], hT[:, k, :],
                                                      start=(k == 0), stop=(k == KD - 1))
                            mm.then_inc(s["q_out"], 1)
                        pe.wait_ge(s["q_ready"], 2 * h + 2)
                        if h >= 2:
                            pe.wait_ge(s["score_taken"], h - 1)
                        for t in range(NT):
                            for cc in range(2):
                                mm = nc.tensor.matmul(bank[4 + h % 2][:, (2 * t + cc) * P:(2 * t + cc + 1) * P],
                                                      qh[:, h % 2, cc, t * P:(t + 1) * P], skT[:, 2 * h + cc, :],
                                                      start=True, stop=True)
                        mm.then_inc(s["score_out"], 1)
                    for n in range(4):
                        pe.wait_ge(s[f"w_in{n % 2}"], 16 * (PH // 2 + n // 2 + 1))
                        if n >= 2:
                            pe.wait_ge(s["gf_taken"], n - 1)
                        for k in range(KD):
                            mm = nc.tensor.matmul(bank[2 + n % 2][:, 0:256], crep[:, k, :], whead[:, n % 2, k, :],
                                                  start=(k == 0), stop=(k == KD - 1))
                        mm.then_inc(s["gf_out"], 1)
                    pe.wait_ge(s["zero_diag"], 1)
                    for t in range(NT):
                        if t:
                            pe.wait_ge(s["pe_sum_taken"], t)
                        for b in range(2):
                            nc.tensor.matmul(bank[6 + b][:, :], zdiag[:], hT[:, 0:2, :].rearrange("p a c -> p (a c)"),
                                             start=True, stop=False, skip_group_check=True)
                        with pe.Fori(0, ROUNDS) as r:
                            pe.wait_ge(s["diag_ready"], r + (t * ROUNDS + 1))
                            for i, j in enumerate(PE_ROWS):
                                pe.wait_ge(row_landed[j], l * (2 * NT * ROUNDS * 16) + r * 16 + ((2 * t + 1) * ROUNDS * 16 + 16))
                                for b in range(2):
                                    mm = nc.tensor.matmul(bank[6 + b][:, :], diag[:, i, :], ringmem[:, j, b * 512:(b + 1) * 512],
                                                          start=False, stop=False, skip_group_check=True)
                                mm.then_inc(slot_free[j], 1)

                @block.scalar
                def _(act):
                    norm_act(act, score[:, 0, 0:8, :].rearrange("p a b -> p (a b)"))
                    for b in range(4):
                        act.wait_ge(s["sk_turned"], b + 1)
                        nc.scalar.activation(skT[:, 4 * b:4 * b + 4, :].rearrange("p a b -> p (a b)"), bank[4 + b % 2][:, :],
                                             ACT.Copy).then_inc(s["sk_ready"], 1)
                    turn_act(act, "h_turned", "hT_ready", 2)
                    for m in range(2 * PH):
                        act.wait_ge(s["q_out"], m + 1)
                        if m >= 4:
                            act.wait_ge(s["score_out"], m // 2 - 1)
                        nc.scalar.activation(qh[:, m // 2 % 2, m % 2, :], bank[m % 2][:, 0:S], ACT.Copy).then_inc(s["q_ready"], 1)
                    for t in range(NT):
                        act.wait_ge(s["gate_max"], t + 1)
                        nc.scalar.activation(coef[:, t, :], coef[:, t, :], exp).then_inc(s["gate_exp"], 1)
                        act.wait_ge(s["act_in"], t + 1)
                        nc.scalar.activation(dots[:, t, :], dots[:, t, :], gelu).then_inc(s["gelu_out"], 1)
                        act.wait_ge(s["coef_ready"], t + 1)
                        with act.Fori(0, ROUNDS) as r:
                            for j in PE_ROWS[-1:]:
                                act.wait_ge(slot_free[j], r + ((2 * t + 1) * ROUNDS + 1))
                                act.sem_inc(s["act_pass"], 1)
                            for i, j in enumerate(PE_ROWS):
                                ins = nc.scalar.activation(diag[:, i, :], ident, ACT.Copy,
                                                           scale=coef[:, t, bass.ds(r * RING + j, 1)])
                            ins.then_inc(s["diag_ready"], 1)

                @block.gpsimd
                def _(pool):
                    for ph in range(2 * NT):
                        t, table = ph // 2, (peer_u, peer_v)[ph % 2]
                        rows = table.rearrange("a e d -> (a e) d")
                        with pool.Fori(0, ROUNDS // 2) as rr:
                            for half in range(2):
                                rnd = rr * 2 + (half + ph * ROUNDS)
                                if ph % 2 == 0:
                                    pool.wait_ge(s["idx_ready"], rr * 2 + (half + t * PH + 1))
                                    pool.sem_inc(s["pool_pass"], 1)
                                pool.wait_ge(slot_free[0], rnd + 1)
                                nc.gpsimd.tensor_tensor(islot[:, half, :], eidx[:, t, bass.ds(rr * (2 * RING) + half * RING, RING)],
                                                        zidx[:], ALU.add).then_inc(s["idx_step"], 1)
                                pool.wait_ge(s["idx_step"], rr * 2 + (half + ph * ROUNDS + 1))
                                pool.sem_inc(s["pool_pass"], 1)
                                for j in range(RING):
                                    if j:
                                        pool.wait_ge(slot_free[j], rnd + 1)
                                        pool.sem_inc(s["pool_pass"], 1)
                                    nc.gpsimd.indirect_dma_start(ringmem[:, j, :], None, rows,
                                                                 bass.IndirectOffsetOnAxis(ap=islot[:, half, j:j + 1], axis=0)
                                                                 ).then_inc(row_landed[j], 16)

                @block.vector
                def _(dve):
                    v = nc.vector
                    step = Steps(dve, "dve_step")
                    step(v.memset(zidx[:], 0))
                    step(v.memset(zdiag[:], 0.0), "zero_diag")
                    norm_dve(dve, step, gain, lambda: None)

                    def top16(vals, idxs, src):
                        step(v.max(vals[:, 0:8], src))
                        step(v.max_index(idxs[:, 0:8], vals[:, 0:8], src))
                        step(v.match_replace(src, vals[:, 0:8], src, BIG * 1e8))
                        step(v.max(vals[:, 8:16], src))
                        step(v.max_index(idxs[:, 8:16], vals[:, 8:16], src))

                    def take_scores(h):
                        dve.wait_ge(s["score_out"], h + 1)
                        step(v.tensor_copy(score[:, :, 2 * h:2 * h + 2, :],
                                           bank[4 + h % 2][:, :].rearrange("p (t a n) -> p t a n", t=NT, a=2)), "score_taken")

                    def retrieve(t, h):
                        for hc in (2 * h, 2 * h + 1):
                            top16(top[:, hc, :], topi[:, hc, :], score[:, t, hc, :])
                        step(v.tensor_copy(topf[:, 2 * h:2 * h + 2, :], topi[:, 2 * h:2 * h + 2, :]))
                        a = top[:, 2 * h, :].rearrange("p (i o) -> p i o", o=1).broadcast_to([P, TOPK, TOPK])
                        b = top[:, 2 * h + 1, :].rearrange("p (o j) -> p o j", o=1).broadcast_to([P, TOPK, TOPK])
                        step(v.tensor_tensor(cand[:, 0, :].rearrange("p (i j) -> p i j", i=TOPK), a, b, ALU.add))
                        top16(fval[:, t, h, :], fpos[:, 0, :], cand[:, 0, :])
                        step(v.tensor_scalar(fhi[:, 0, :], fpos[:, 0, :], 4, None, ALU.logical_shift_right))
                        step(v.tensor_scalar(fhi[:, 1, :], fpos[:, 0, :], 15, None, ALU.bitwise_and))
                        step(v.tensor_copy(ff[:, 0:2, :], fhi[:, 0:2, :]))
                        oh = cand[:, 2:4, :].rearrange("p a (k i) -> p a k i", k=TOPK)
                        f4 = ff[:, 0:2, :].rearrange("p a (k o) -> p a k o", o=1).broadcast_to([P, 2, TOPK, TOPK])
                        io = const["iota"].rearrange("p (a b i) -> p a b i", a=1, b=1).broadcast_to([P, 2, TOPK, TOPK])
                        step(v.tensor_tensor(oh, f4, io, ALU.is_equal))
                        ix = topf[:, 2 * h:2 * h + 2, :].rearrange("p a (o i) -> p a o i", o=1).broadcast_to([P, 2, TOPK, TOPK])
                        step(v.tensor_tensor(oh, oh, ix, ALU.mult))
                        step(v.tensor_reduce(eid[:, 0:2, :], oh, AX_X, ALU.add))
                        step(v.scalar_tensor_tensor(out=eid[:, 2, :], in0=eid[:, 0, :], scalar=float(NK), in1=eid[:, 1, :],
                                                    op0=ALU.mult, op1=ALU.add))
                        step(v.tensor_scalar(eidx[:, t, h * TOPK:(h + 1) * TOPK], eid[:, 2, :], ebase[:, 0:1], None,
                                             ALU.add), "idx_ready")

                    def gates(t):
                        c3 = coef[:, t, :].rearrange("p (h k) -> p h k", h=PH)
                        step(v.tensor_tensor(c3, fval[:, t], fval[:, t, :, 0:1].broadcast_to([P, PH, TOPK]),
                                             ALU.subtract), "gate_max")
                        dve.wait_ge(s["gate_exp"], t + 1)
                        step(v.tensor_reduce(gsum[:, t, 0, :], c3, AX_X, ALU.add))
                        step(v.reciprocal(gsum[:, t, 1, :], gsum[:, t, 0, :]))
                        step(v.tensor_tensor(c3, c3, gsum[:, t, 1, :].rearrange("p (h o) -> p h o", o=1)
                                             .broadcast_to([P, PH, TOPK]), ALU.mult))

                    def row(ph, r, j):
                        t = ph // 2
                        if ph % 2 and j in PE_ROWS:
                            return
                        dve.wait_ge(row_landed[j], l * (2 * NT * ROUNDS * 16) + r * 16 + (ph * ROUNDS * 16 + 16))
                        k = r * RING + j
                        col = slice(k, k + 1) if isinstance(r, int) else bass.ds(k, 1)
                        if ph % 2 == 0:
                            ins = v.scalar_tensor_tensor(out=ringmem[:, j, :], in0=ringmem[:, j, :], scalar=1.0,
                                                         in1=hm[:, t, :], op0=ALU.mult, op1=ALU.mult,
                                                         accum_out=dots[:, t, col])
                            ins.then_inc(slot_free[j], 1)
                            return
                        at = DVE_ROWS.index(j)
                        dve.wait_ge(slot_free[DVE_ROWS[at - 1]], r + (ph * ROUNDS + (2 if at else 1)))
                        ins = v.scalar_tensor_tensor(out=accv[:, t, :], in0=ringmem[:, j, :], scalar=coef[:, t, col],
                                                     in1=accv[:, t, :], op0=ALU.mult, op1=ALU.add)
                        ins.then_inc(slot_free[j], 1)

                    def rows(ph):
                        with dve.Fori(0, ROUNDS) as r:
                            for j in range(RING):
                                row(ph, r, j)

                    def coefficients(t):
                        for j in range(RING):
                            dve.wait_ge(slot_free[j], (2 * t + 1) * ROUNDS + 1)
                        step(v.memset(stat[:, 9:10], 0.0), "act_in")
                        dve.wait_ge(s["gelu_out"], t + 1)
                        step(v.tensor_tensor(coef[:, t, :], coef[:, t, :], dots[:, t, :], ALU.mult), "coef_ready")

                    def take_pe_sum(t):
                        for j in range(RING):
                            dve.wait_ge(slot_free[j], (2 * t + 2) * ROUNDS + 1)
                        for b in range(2):
                            q = slice(512 * b, 512 * (b + 1))
                            ins = v.tensor_tensor(accv[:, t, q], accv[:, t, q], bank[6 + b][:, :], ALU.add)
                            step(ins, "pe_sum_taken") if b else step(ins)

                    for j in range(RING):
                        dve.sem_inc(slot_free[j], 1)
                    step(v.memset(accv[:], 0.0))
                    take_scores(0)
                    retrieve(0, 0)
                    for h in range(PH):
                        if h + 1 < PH:
                            take_scores(h + 1)
                            retrieve(0, h + 1)
                        else:
                            gates(0)
                        for j in range(TOPK):
                            row(0, h, j)
                    coefficients(0)
                    dve.wait_ge(s["bias_in"], 16)
                    for n in range(4):
                        dve.wait_ge(s["gf_out"], n + 1)
                        part = mod[:, 2, 256 * n:256 * (n + 1)]
                        step(v.tensor_tensor(part, bank[2 + n % 2][:, 0:256], part, ALU.add), "gf_taken")
                    for h in range(PH):
                        retrieve(1, h)
                        for j in range(TOPK):
                            row(1, h, j)
                    gates(1)
                    take_pe_sum(0)
                    rows(2)
                    coefficients(1)
                    rows(3)
                    take_pe_sum(1)
                    for t in range(NT):
                        step(v.tensor_tensor(accv[:, t, :], accv[:, t, :], mod[:, 2, :], ALU.mult))
                        step(v.tensor_tensor(xs[:, t, :], xs[:, t, :], accv[:, t, :], ALU.add))
                    step(v.tensor_scalar(ebase[:], ebase[:], float(EXPERTS), None, ALU.add))

            nc.all_engine_barrier(sems_to_clear=clearable)

        with ExitStack() as end, nc.Block() as block:
            fg = sb("fg", [P, D], where=end)

            @block.sync
            def _(sp):
                sp.dma_start(fg[:], final_norm_g.rearrange("(o d) -> o d", o=1).broadcast_to([P, D])).then_inc(s["gain_in"], 16)
                for t in range(NT):
                    sp.wait_ge(s["h_ready"], t + 1)
                    sp.dma_start(out.rearrange("o (t p) d -> p (o t) d", p=P)[:, t, :], hm[:, t, :]).then_inc(s["stored"], 16)
                sp.wait_ge(s["stored"], 16 * NT)

            @block.scalar
            def _(act):
                norm_act(act, hm[:, 0, :])

            @block.vector
            def _(dve):
                step = Steps(dve, "dve_step")
                for t in range(NT):
                    dve.wait_ge(s["ss_ready"], t + 1)
                    step(nc.vector.tensor_scalar(stat[:, 2 + t:3 + t], stat[:, t:t + 1], 1.0 / D, RMS_EPS,
                                                 ALU.mult, ALU.add), "var_ready")
                dve.wait_ge(s["gain_in"], 16)
                for t in range(NT):
                    dve.wait_ge(s["sd_ready"], t + 1)
                    step(nc.vector.reciprocal(stat[:, 6 + t:7 + t], stat[:, 4 + t:5 + t]))
                    step(nc.vector.scalar_tensor_tensor(out=hm[:, t, :], in0=xs[:, t, :], scalar=stat[:, 6 + t:7 + t],
                                                        in1=fg[:], op0=ALU.mult, op1=ALU.mult), "h_ready")


def shape_constants():
    import numpy as np
    a = np.zeros((P, CONSTS), np.float32)

    def put(name, value):
        lo, hi = _off[name]
        a[:, lo:hi] = np.asarray(value, np.float32).reshape(P, hi - lo)

    i = np.arange(P)
    row, col = i[:, None], i[None, :]
    put("ident", row == col)
    same = row // C == col // C
    strict, upto = same & (row < col), same & (row <= col)
    put("amask", np.stack([strict, upto, strict, upto], 1))
    lower = []
    for lev in range(LEVELS):
        b = 1 << lev
        lower.append((row // (2 * b) == col // (2 * b)) & (row // b % 2 == 1) & (col // b % 2 == 0))
    put("xmask", np.stack(lower, 1))
    put("xtmask", np.stack([m.T for m in lower], 1))
    put("pairones", row // HD == col // HD)
    put("headsel", row // HD == np.arange(2)[None, :])
    tok = np.arange(S)[None, :]
    put("cumsel", np.stack([row + P * t <= tok for t in range(NT)], 1))
    put("reset", np.broadcast_to(np.arange(NPAIR * S) % C != 0, (P, NPAIR * S)))
    put("causal", np.concatenate([np.zeros((P, P)), np.where(col > row, BIG, 0.0)], 1))
    fs = np.zeros((P, FOX_H, P))
    for h in range(FOX_H):
        fs[h, h, :] = -1.0 / FOX_SCALE
    put("foxsel", fs)
    put("iota", np.broadcast_to(np.arange(TOPK), (P, TOPK)))
    lam = np.array([0.8 - 0.6 * math.exp(-0.3 * d) for d in range(DEPTH)])
    return a, np.stack([lam, 1.0 - lam], 1).astype(np.float32)


_INS = ["x", "c", "norm_mix_g", "norm_ffn_g", "final_norm_g", "ada_w", "ada_b", "w_in", "w_out", "dif_lam",
        "dif_subln_g", "rw_mu", "rw_w0", "rw_w2", "rw_a0", "rw_a2", "rw_g2", "rw_kk", "rw_ka", "rw_rk", "rw_ln_g",
        "rw_ln_b", "fox_bf", "peer_wq", "peer_subkeys", "peer_u", "peer_v"]


def kernel(**inputs):
    import numpy as _np
    import concourse.bacc as _bacc
    from concourse import mybir as _mybir
    from concourse.bass_utils import run_bass_kernel_spmd as _run

    nc = _bacc.Bacc("TRN2", target_bir_lowering=False, num_devices=1)
    arrays, args = {}, []
    consts, lam_consts = shape_constants()
    for name, a in [(n, _np.ascontiguousarray(inputs[n])) for n in _INS] + [("consts", consts), ("lam_consts", lam_consts)]:
        arrays[f"in_{name}_dram"] = a
        args.append(nc.dram_tensor(f"in_{name}_dram", a.shape, _mybir.dt.from_np(a.dtype), kind="ExternalInput").ap())
    args.append(nc.dram_tensor("out_0_dram", (1, S, D), _mybir.dt.float32, kind="ExternalOutput").ap())
    trunk(nc, *args)
    r = _run(nc, [arrays], core_ids=[0])
    return r.results[0]["out_0_dram"]
```

```python
import math
from contextlib import ExitStack

import concourse.bass as bass
from concourse import mybir

ALU = mybir.AluOpType
ACT = mybir.ActivationFunctionType
F32 = mybir.dt.float32
I32 = mybir.dt.int32
U32 = mybir.dt.uint32
AX_X = mybir.AxisListType.X

P = 128
D = 1024
S = 256
NT = S // P
KD = D // P
DEPTH = 2
HD = 64
DIFF_H, RW_H, FOX_H = 6, 6, 4
W6 = DIFF_H * HD
WF = FOX_H * HD
NPAIR = RW_H // 2
C = 64
NC = S // C
LEVELS = int(math.log2(C))
IN_COLS = 3 * W6 + (3 * W6 + 256) + (3 * WF + FOX_H)
RMS_EPS = 1e-6
LN_EPS = 64e-5
DIFF_SCALE = 32 ** -0.5
FOX_SCALE = 64 ** -0.5
PH, NK, TOPK = 8, 128, 16
EXPERTS = NK * NK
SEL = PH * TOPK
RING = 16
PE_ROWS = (1, 4, 6, 9, 12, 14)
DVE_ROWS = tuple(j for j in range(RING) if j not in PE_ROWS)
WS = 4
BIG = -1e30

_off = {}
_n = 0
for _name, _w in (("ident", P), ("amask", 4 * P), ("xmask", LEVELS * P), ("xtmask", LEVELS * P), ("pairones", P),
                  ("headsel", 2), ("cumsel", NT * S), ("reset", NPAIR * S), ("causal", S), ("foxsel", FOX_H * P),
                  ("iota", TOPK)):
    _off[_name] = (_n, _n + _w)
    _n += _w
CONSTS = _n

DIFF0, RW0, FOX0 = 0, 3 * W6, 6 * W6 + 256
GROUPS = [("r", RW0, W6, "f"), ("k", RW0 + W6, W6, "f"), ("v", RW0 + 2 * W6, W6, "f"), ("x", RW0 + 3 * W6, 256, "f"),
          ("dq", DIFF0, W6, "f"), ("dk", DIFF0 + W6, W6, "f"), ("dv", DIFF0 + 2 * W6, W6, "t"),
          ("fqk", FOX0, 2 * WF, "f"), ("fv", FOX0 + 2 * WF, WF + FOX_H, "t")]
OUTS_OF = [(w // P if kind == "f" else NT) for _, _, w, kind in GROUPS]
COLS = {g[0]: sum(OUTS_OF[:n + 1]) for n, g in enumerate(GROUPS)}


MU, PW0, PA0, PKK, PKA, PRK = 0, 11, 14, 17, 20, 23
PCOLS = 26
LNG, LNB, SUBG, LAM, LAMC, BF, PROWS = 0, W6, 2 * W6, 2 * W6 + HD, 2 * W6 + HD + 128, 2 * W6 + HD + 130, 2 * W6 + HD + 134
MOD_ORDER = (2, 3, 0, 1, 4, 5)


def trunk(nc, x, c_cols, norm_mix_g, norm_ffn_g, final_norm_g, ada_w, ada_b, w_in, w_out, param_cols, param_rows,
          lora_w, peer_wq, subkeys_t, peer_u, peer_v, consts, out):
    gelu, exp, sig = ACT.Gelu, ACT.Exp, ACT.Sigmoid

    with ExitStack() as ctx:
        def sb(name, shape, dt=F32, where=ctx):
            return where.enter_context(nc.sbuf_tensor(name, shape, dt))

        def sem(name):
            return ctx.enter_context(nc.semaphore(name))

        bank = [ctx.enter_context(nc.psum_tensor(f"bank{i}", [P, 512], F32)) for i in range(8)]

        row_landed = [sem(f"row_landed{i}") for i in range(RING)]
        names = ("zero_diag", "gf_out", "gf_taken", "pe_sum_taken", "diag_ready", "coef_ready", "act_pass",
                 "const_in", "params_in", "bias_in", "gate_bias_in", "gain_in", "wout_in0", "wout_in1", "small_in",
                 "w_in0", "w_in1", "w_in2", "w_in3", "next_w0", "next_w1", "next_w2", "next_w3", "c_ready", "crep",
                 "pe_out", "mod_ready", "cols_ready", "dve_step", "act_step", "h_ready", "h_turned", "hT_ready",
                 "ss_ready", "var_ready", "sd_ready", "acc_zero", "lora_in", "lora_out", "lora_act", "kk_sq",
                 "kk_sum", "kk_var", "kk_sd", "decay", "decay_exp", "rw_ops", "bonus_out", "tm_turned", "tm_ready",
                 "apair", "apair_sb", "z_out", "z_sb", "xz_out", "x_sb", "av_out", "av_sb", "uw_out", "uw_sb",
                 "sa_out", "sa_sb", "st_out", "st_sb", "y_out", "y_taken", "y_copied", "gate_out", "gate_sb",
                 "s_out", "s_masked", "s_exp", "p_ready", "p_turned", "pT_ready", "pv_out", "o_taken", "f_exp",
                 "f_in", "f_ln", "cum_in", "cum_out", "cum_sb", "lam_in", "lam_exp", "o_var", "o_sd", "y_var",
                 "y_sd", "mix_ready", "mix_turned", "mixT_ready", "mix_out", "x_done", "reset_free", "rpad",
                 "stored", "q_out", "q_ready", "score_out", "score_taken", "gate_max", "gate_exp", "idx_ready",
                 "idx_step", "pool_pass", "act_in", "gelu_out")
        s = {n: sem(n) for n in names}
        slot_free = [sem(f"slot_free{i}") for i in range(RING)]
        clearable = range(min(q.num for q in s.values()), max(q.num for q in slot_free) + 1)
        assert RING == TOPK and len(clearable) == len(names) + RING and all(q.num not in clearable for q in row_landed)

        class Steps:

            def __init__(self, eng, own):
                self.eng, self.own, self.count = eng, own, {}

            def __call__(self, ins, tell=None):
                q = self.own if tell is None else tell
                self.count[q] = self.count.get(q, 0) + 1
                ins.then_inc(s[q], 1)
                self.eng.wait_ge(s[q], self.count[q])

        K = sb("K", [P, CONSTS])
        const = {n: K[:, a:b] for n, (a, b) in _off.items()}
        ident, pairones = const["ident"], const["pairones"]
        xs = sb("xs", [P, NT, D])
        hm = sb("hm", [P, NT, D])
        hT = sb("hT", [P, KD, S])
        mod = sb("mod", [P, 3, D])
        crep = sb("crep", [P, KD, P])
        ringmem = sb("ringmem", [P, RING, D])
        ringf = ringmem[:].rearrange("p a b -> p (a b)")
        wslot = [ringf[:, i * 4096:(i + 1) * 4096].rearrange("p (k n) -> p k n", k=KD) for i in range(WS)]
        stat = sb("stat", [P, 16])
        ones_c = sb("ones_c", [P, P])
        ebase = sb("ebase", [P, 1])

        def weight_landed(pe, n):
            pe.wait_ge(s[f"w_in{n % WS}"], 16 * (n // WS + 1))

        with ExitStack() as setup, nc.Block() as block:
            cin = sb("cin", [P, KD], where=setup)
            cT = sb("cT", [P, KD], where=setup)

            @block.sync
            def _(sp):
                sp.dma_start(cin[:], c_cols).then_inc(s["small_in"], 16)
                sp.dma_start(K[:], consts).then_inc(s["const_in"], 16)
                sp.dma_start(xs[:], x.rearrange("o (t p) d -> p (o t) d", p=P)).then_inc(s["params_in"], 16)
                sp.wait_ge(s["params_in"], 16)
                sp.wait_ge(s["const_in"], 16)

            @block.scalar
            def _(act):
                act.wait_ge(s["small_in"], 16)
                nc.scalar.activation(cT[:], cin[:], ACT.Silu).then_inc(s["c_ready"], 1)

            @block.vector
            def _(dve):
                step = Steps(dve, "dve_step")
                step(nc.vector.memset(ones_c[:], 1.0))
                step(nc.vector.memset(ebase[:], 0.0))
                dve.wait_ge(s["c_ready"], 1)
                for k in range(KD):
                    nc.vector.tensor_scalar(crep[:, k, :], ones_c[:], cT[:, k:k + 1], None,
                                            ALU.mult).then_inc(s["crep"], 1)

        nc.all_engine_barrier(sems_to_clear=clearable)

        def ada_plan(l, half):
            view = ada_w[bass.ds(l, 1)].rearrange("o (k p) n -> p (o k) n", p=P)
            return [view[:, :, half * 3 * D + 512 * n:half * 3 * D + 512 * (n + 1)] for n in MOD_ORDER]

        def load_bias(sp, l, half, rows, told="bias_in"):
            b = ada_b[bass.ds(l, 1), (half * 3 + rows.start) * D:(half * 3 + rows.stop) * D]
            sp.dma_start(mod[:, rows, :].rearrange("p a d -> p (a d)"),
                         b.broadcast_to([P, (rows.stop - rows.start) * D])).then_inc(s[told], 16)

        def load_gain(sp, l, gain, gains):
            sp.dma_start(gain, gains[bass.ds(l, 1), :].broadcast_to([P, D])).then_inc(s["gain_in"], 16)

        def ada_pe(pe):
            for n in range(6):
                weight_landed(pe, n)
                if n >= 2:
                    pe.wait_ge(s["mod_ready"], n - 1)
                for k in range(KD):
                    mm = nc.tensor.matmul(bank[n % 2][:, :], crep[:, k, :], wslot[n % WS][:, k, :],
                                          start=(k == 0), stop=(k == KD - 1))
                mm.then_inc(s["pe_out"], 1)

        def take_mod(dve, step, n, out_n, bk):
            dve.wait_ge(s["pe_out"], out_n)
            part = mod[:].rearrange("p a d -> p (a d)")[:, 512 * n:512 * (n + 1)]
            step(nc.vector.tensor_tensor(part, bank[bk][:, :], part, ALU.add), "mod_ready")

        def norm_variance(dve, step, t, nth=0):
            dve.wait_ge(s["ss_ready"], NT * nth + t + 1)
            step(nc.vector.tensor_scalar(stat[:, 2 + t:3 + t], stat[:, t:t + 1], 1.0 / D, RMS_EPS,
                                         ALU.mult, ALU.add), "var_ready")

        def norm_gain(step, gain):
            step(nc.vector.scalar_tensor_tensor(out=mod[:, 1, :], in0=mod[:, 1, :], scalar=1.0, in1=gain,
                                                op0=ALU.add, op1=ALU.mult))

        def norm_scaled(dve, step, t, nth=0):
            dve.wait_ge(s["sd_ready"], NT * nth + t + 1)
            step(nc.vector.reciprocal(stat[:, 6 + t:7 + t], stat[:, 4 + t:5 + t]))
            step(nc.vector.scalar_tensor_tensor(out=hm[:, t, :], in0=xs[:, t, :], scalar=stat[:, 6 + t:7 + t],
                                                in1=mod[:, 1, :], op0=ALU.mult, op1=ALU.mult))

        def norm_act(act, junk, nth=0):
            for t in range(NT):
                if nth:
                    act.wait_ge(s["x_done"], t + 1)
                nc.scalar.activation(junk, xs[:, t, :], ACT.Square,
                                     accum_out=stat[:, t:t + 1]).then_inc(s["ss_ready"], 1)
                act.wait_ge(s["ss_ready"], NT * nth + t + 1)
            for t in range(NT):
                act.wait_ge(s["var_ready"], NT * nth + t + 1)
                nc.scalar.activation(stat[:, 4 + t:5 + t], stat[:, 2 + t:3 + t], ACT.Sqrt).then_inc(s["sd_ready"], 1)

        def turn_pe(pe, src, ready, turned, taken, banks, tiles=range(NT)):
            for t in tiles:
                if ready is not None:
                    pe.wait_ge(s[ready], t + 1)
                for b in range(2):
                    n = 2 * t + b
                    if n >= 2:
                        pe.wait_ge(s[taken], n - 1)
                    for j in range(4):
                        k = 4 * b + j
                        tr = nc.tensor.transpose(bank[banks + n % 2][:, j * P:(j + 1) * P],
                                                 src[:, t, k * P:(k + 1) * P], ident)
                    tr.then_inc(s[turned], 1)

        def turn_act(act, turned, taken, banks):
            for t in range(NT):
                for b in range(2):
                    n = 2 * t + b
                    act.wait_ge(s[turned], n + 1)
                    nc.scalar.activation(hT[:, 4 * b:4 * b + 4, t * P:(t + 1) * P],
                                         bank[banks + n % 2][:, :].rearrange("p (j c) -> p j c", j=4),
                                         ACT.Copy).then_inc(s[taken], 1)

        with nc.Fori(0, DEPTH) as l:
            with ExitStack() as mix, nc.Block() as block:
                gain = hm[:, 0, :]
                pcol = sb("pcol", [P, PCOLS], where=mix)
                colsT = sb("colsT", [P, 11, S + 1], where=mix)
                mixed = sb("mixed", [P, 11, S], where=mix)
                lora = sb("lora", [P, 2 * W6], where=mix)
                w2a2, g2 = lora[:, 0:W6], lora[:, W6:]
                prow = sb("prow", [P, PROWS], where=mix)
                subg, lamc, bfb = prow[:, SUBG:SUBG + HD], prow[:, LAMC:LAMC + 2], prow[:, BF:BF + FOX_H]
                lamp = prow[:, LAM:LAM + 128].rearrange("p (a b) -> p a b", a=4)
                small = sb("small", [P, 24], where=mix)
                sgx = sb("sgx", [P, S], where=mix)
                thx = sb("thx", [HD, S], where=mix)
                AL = sb("AL", [P, 2, NPAIR, S], where=mix)
                asig, lw = AL[:, 0], AL[:, 1]
                T12 = sb("T12", [P, 2, NPAIR, S], where=mix)
                T1, T2 = T12[:, 0], T12[:, 1]
                cold = colsT[:].rearrange("p a b -> p (a b)")

                def old(n):
                    return cold[:, 1 + n * NPAIR * S:1 + (n + 1) * NPAIR * S].rearrange("p (a b) -> p a b", a=NPAIR)

                E1, E2, E3 = (old(n) for n in range(3))
                bt, kt = asig, lw
                gainf = cold[:, 1 + 2 * NPAIR * S:1 + 2 * NPAIR * S + D]
                ar = sb("ar", [P, NPAIR, NT, 2, P], where=mix)
                rpad = sb("rpad_sb", [P, NPAIR, NT, 2, P], where=mix)
                bon = sb("bon", [P, NT, RW_H], where=mix)
                gate = sb("gate", [P, NT, W6], where=mix)
                ST = sb("ST", [P, NC, NPAIR, P], where=mix)
                bv = mixed[:, 0:3, :].rearrange("p a c -> p (a c)").rearrange("p (t c) -> p t c", t=NT)
                alf, t12f = (a[:].rearrange("p a g c -> p (a g c)") for a in (AL, T12))
                stmp = alf[:, 896:1280].rearrange("p (g c) -> p g c", g=NPAIR)
                SA = sb("SA", [P, NT, NPAIR, P], where=mix)
                dq = sb("dq", [P, 3, S], where=mix)
                dk = sb("dk", [P, 3, S], where=mix)
                dv = sb("dv", [P, NT, W6], where=mix)
                fqk = sb("fqk", [P, 4, S], where=mix)
                fv = sb("fv", [P, NT, WF + FOX_H], where=mix)
                fl = sb("fl", [P, 4, NT, FOX_H], where=mix)
                cumT = sb("cumT", [FOX_H, S], where=mix)
                sc = t12f[:, 0:1024].rearrange("p (a b) -> p a b", a=2)
                pn = t12f[:, 1024:1536].rearrange("p (a b) -> p a b", a=2)
                pT = alf[:, 0:512].rearrange("p (a b) -> p a b", a=2)
                ast = sb("ast", [P, 2, 8], where=mix)
                ov = alf[:, 512:896]
                AT = [ringf[:, n * 512:(n + 1) * 512] for n in range(12)]
                X, XT, Z = (ringf[:, 6144 + n * 1536:6144 + (n + 1) * 1536].rearrange("p (g c) -> p g c", g=NPAIR)
                            for n in range(3))
                tm = ringf[:, 10752:10752 + 3072].rearrange("p (g t k c) -> p g t k c", g=NPAIR, t=NT, k=4)
                AV, U, WT = (ringf[:, 13824 + n * 768:13824 + (n + 1) * 768].rearrange("p (t g c) -> p t g c", t=NT, g=NPAIR)
                             for n in range(3))
                wout = [ringf[:, o:o + 4096].rearrange("p (k n) -> p k n", k=KD) for o in (6144, 12288)]

                def fourk(a):
                    return a.rearrange("p (k n) -> p k n", k=KD // 2)

                x_place = (fourk(ringf[:, 6144:8192]), fourk(ringf[:, 8192:10240]))
                next_w = [(fourk(hT[:].rearrange("p a b -> p (a b)")), fourk(mixed[:, 3:11, :].rearrange("p a b -> p (a b)"))),
                          x_place, (fourk(ringf[:, 0:2048]), fourk(ringf[:, 2048:4096])),
                          (fourk(ringf[:, 4096:6144]), fourk(ringf[:, 10240:12288]))]
                NEXT_BANK = (3, 1, 1, 0)
                BTK, KTK, ATK, VTK = range(4)
                proj0 = 6
                nproj = COLS["fv"]

                units = [("d", h, t) for t in range(NT) for h in range(DIFF_H)] + \
                        [("f", h, t) for t in range(NT) for h in range(FOX_H)]
                assert len(units) == 2 * LEVELS + 2 * NC

                @block.sync
                def _(sp):
                    for n, view in enumerate(ada_plan(l, 0)):
                        if n >= WS:
                            sp.wait_ge(s["pe_out"], n - WS + 1)
                        sp.dma_start(wslot[n % WS], view).then_inc(s[f"w_in{n % WS}"], 16)
                        if n == 1:
                            load_bias(sp, l, 0, slice(0, 2))
                            load_gain(sp, l, gain, norm_mix_g)
                        if n == 3:
                            load_bias(sp, l, 0, slice(2, 3), "gate_bias_in")
                            sp.dma_start(prow[:], param_rows[bass.ds(l, 1), :].broadcast_to([P, PROWS])).then_inc(s["small_in"], 16)
                            sp.dma_start(pcol[:], param_cols[bass.ds(l, 1)].rearrange("o p n -> (o p) n")).then_inc(s["params_in"], 16)
                            sp.dma_start(lora[:], lora_w[bass.ds(l, 1)].rearrange("o p n -> (o p) n")).then_inc(s["lora_in"], 16)
                    win = w_in[bass.ds(l, 1)].rearrange("o (k p) n -> p (o k) n", p=P)
                    last_out = [n + 1 for n in range(6)] + [proj0 + COLS[g[0]] for g in GROUPS]
                    for g, (_, c0, w, _) in enumerate(GROUPS):
                        n = 6 + g
                        sp.wait_ge(s["pe_out"], last_out[n - WS])
                        sp.dma_start(wslot[n % WS][:, :, 0:w], win[:, :, c0:c0 + w]).then_inc(s[f"w_in{n % WS}"], 16)
                    sp.wait_ge(s["h_ready"], NT)
                    load_bias(sp, l, 1, slice(0, 2))

                    def load_next(n):
                        view = ada_plan(l, 1)[n]
                        for i in range(2):
                            sp.dma_start(next_w[n][i], view[:, 4 * i:4 * i + 4, :]).then_inc(s[f"next_w{n}"], 16)

                    sp.wait_ge(s["pe_out"], proj0 + nproj)
                    sp.wait_ge(s["tm_turned"], 6)
                    load_next(0)
                    load_gain(sp, l, gainf, norm_ffn_g)
                    sp.wait_ge(s["uw_out"], NT)
                    load_next(1)

                    def load_wout(b):
                        sp.dma_start(wout[b], w_out[bass.ds(l, 1)].rearrange("o (k p) n -> p (o k) n", p=P)
                                     [:, :, b * 512:(b + 1) * 512]).then_inc(s[f"wout_in{b}"], 16)

                    sp.wait_ge(s["pe_out"], proj0 + nproj + 2)
                    load_wout(0)
                    sp.wait_ge(s["y_out"], NT)
                    load_wout(1)
                    load_next(2)
                    load_next(3)

                @block.gpsimd
                def _(pool):
                    nc.gpsimd.memset(rpad[:], 0.0).then_inc(s["reset_free"], 1)
                    nc.gpsimd.memset(colsT[:, :, 0:1], 0.0).then_inc(s["reset_free"], 1)
                    nc.gpsimd.memset(ST[:, 0], 0.0).then_inc(s["reset_free"], 1)
                    pool.wait_ge(s["rw_ops"], 2)
                    pool.wait_ge(s["reset_free"], 1)
                    for cc in range(2):
                        nc.gpsimd.tensor_copy(rpad[:, :, :, cc, cc * C:(cc + 1) * C].rearrange("p g t c -> p (g t) c"),
                                              ar[:, :, :, 1, cc * C:(cc + 1) * C].rearrange("p g t c -> p (g t) c")
                                              ).then_inc(s["rpad"], 1)
                    for a, used in ((X, "fqk"), (XT, "fv")):
                        pool.wait_ge(s["pe_out"], proj0 + COLS[used])
                        nc.gpsimd.tensor_copy(a.rearrange("p g (i c) -> p (g i) c", c=P),
                                              ident.rearrange("p (o c) -> p o c", o=1).broadcast_to([P, 12, P])).then_inc(s["reset_free"], 1)

                @block.tensor
                def _(pe):
                    def blocks_z(u):
                        p = u % NPAIR
                        if u >= NPAIR + 2:
                            pe.wait_ge(s["z_sb"], u - NPAIR - 1)
                        pe.wait_ge(s["x_sb"], 2 * (u - NPAIR) + 2)
                        for j in range(4):
                            mm = nc.tensor.matmul(bank[u % 2][:, j * P:(j + 1) * P], AT[4 * p + j][:, 0:P],
                                                  X[:, p, j * P:(j + 1) * P], start=True, stop=True)
                        mm.then_inc(s["z_out"], 1)

                    def blocks_first(u):
                        if u:
                            pe.wait_ge(s["x_sb"], 2 * u)
                        for j in range(4):
                            tr = nc.tensor.transpose(bank[2][:, j * P:(j + 1) * P], AT[4 * u + j][:, 0:P], ident)
                        tr.then_inc(s["xz_out"], 1)

                    def blocks_x(u):
                        p = u % NPAIR
                        pe.wait_ge(s["z_sb"], u - NPAIR + 1)
                        pe.wait_ge(s["x_sb"], 2 * u)
                        if u < (LEVELS - 1) * NPAIR:
                            for j in range(4):
                                nc.tensor.matmul(bank[2][:, j * P:(j + 1) * P], XT[:, p, j * P:(j + 1) * P],
                                                 Z[:, p, j * P:(j + 1) * P], start=True, stop=True)
                        for j in range(4):
                            mm = nc.tensor.matmul(bank[3][:, j * P:(j + 1) * P], Z[:, p, j * P:(j + 1) * P],
                                                  XT[:, p, j * P:(j + 1) * P], start=True, stop=True)
                        mm.then_inc(s["xz_out"], 1)

                    def att_scores(n):
                        kind, h, t = units[n]
                        nk = (t + 1) * P
                        if n:
                            pe.wait_ge(s["s_masked"], n)
                        o = 64 * (h % 2)
                        if kind == "d":
                            for a in range(2):
                                q = slice(o + 32 * a, o + 32 * a + 32)
                                mm = nc.tensor.matmul(bank[4 + a][:, 0:nk], dq[q, h // 2, t * P:(t + 1) * P],
                                                      dk[q, h // 2, 0:nk], start=True, stop=True)
                        else:
                            q = slice(o, o + 64)
                            nc.tensor.matmul(bank[4][:, 0:nk], fqk[q, h // 2, t * P:(t + 1) * P], fqk[q, 2 + h // 2, 0:nk],
                                             start=True, stop=False)
                            mm = nc.tensor.matmul(bank[4][:, 0:nk], const["foxsel"][0:FOX_H, h * P:(h + 1) * P],
                                                  cumT[:, 0:nk], start=False, stop=True)
                        mm.then_inc(s["s_out"], 1)

                    def att_turn(n):
                        kind, h, t = units[n]
                        pe.wait_ge(s["p_ready"], n + 1)
                        if n:
                            pe.wait_ge(s["pT_ready"], n)
                        for j in range(t + 1):
                            tr = nc.tensor.transpose(bank[6][:, j * P:(j + 1) * P], pn[:, n % 2, j * P:(j + 1) * P], ident)
                        tr.then_inc(s["p_turned"], 1)

                    def att_values(n):
                        kind, h, t = units[n]
                        pe.wait_ge(s["pT_ready"], n + 1)
                        if n:
                            pe.wait_ge(s["o_taken"], n)
                        for j in range(t + 1):
                            vals = (dv if kind == "d" else fv)[:, j, h * HD:(h + 1) * HD]
                            mm = nc.tensor.matmul(bank[7][:, 0:HD], pT[:, n % 2, j * P:(j + 1) * P], vals,
                                                  start=(j == 0), stop=(j == t))
                        mm.then_inc(s["pv_out"], 1)

                    def attention(n):
                        if n < len(units):
                            att_scores(n)
                        att_outputs(n)

                    def att_outputs(n):
                        if 1 <= n <= len(units):
                            att_turn(n - 1)
                        if n >= 2:
                            att_values(n - 2)

                    ada_pe(pe)
                    turn_pe(pe, hm, "h_ready", "h_turned", "hT_ready", 2)
                    pe.wait_ge(s["hT_ready"], 4)
                    m = 0
                    for g, (name, c0, w, kind) in enumerate(GROUPS):
                        n = 6 + g
                        weight_landed(pe, n)
                        wt = wslot[n % WS]
                        for j in range(w // P if kind == "f" else NT):
                            if m >= 2:
                                pe.wait_ge(s["cols_ready"], m - 1)
                            else:
                                pe.wait_ge(s["mod_ready"], 5 + m)
                            for k in range(KD):
                                if kind == "f":
                                    mm = nc.tensor.matmul(bank[m % 2][:, 0:S], wt[:, k, j * P:(j + 1) * P], hT[:, k, :],
                                                          start=(k == 0), stop=(k == KD - 1))
                                else:
                                    mm = nc.tensor.matmul(bank[m % 2][:, 0:w], hT[:, k, j * P:(j + 1) * P], wt[:, k, 0:w],
                                                          start=(k == 0), stop=(k == KD - 1))
                            mm.then_inc(s["pe_out"], 1)
                            m += 1
                        if name != "dk":
                            continue
                        pe.wait_ge(s["lora_in"], 16)
                        pe.wait_ge(s["act_step"], 2)
                        pe.wait_ge(s["rw_ops"], 1)
                        for j in range(6):
                            r0 = 0 if j < 3 else 64
                            rhs = thx[:, :] if j < 3 else mixed[64:128, 9, :]
                            if j >= 2:
                                pe.wait_ge(s["lora_act"], j - 1)
                            nc.tensor.matmul(bank[2 + j % 2][:, 0:S], w2a2[r0:r0 + 64, (j % 3) * P:(j % 3 + 1) * P], rhs,
                                             start=True, stop=True).then_inc(s["lora_out"], 1)
                        for t in range(NT):
                            nc.tensor.matmul(bank[4 + t][:, 0:W6], sgx[:, t * P:(t + 1) * P], g2[:, :],
                                             start=True, stop=True).then_inc(s["gate_out"], 1)
                        pe.wait_ge(s["kk_sq"], 1)
                        for p in range(NPAIR):
                            mm = nc.tensor.matmul(bank[6 + p // 2][:, (p % 2) * S:(p % 2 + 1) * S], pairones, T1[:, p, :],
                                                  start=True, stop=True)
                        mm.then_inc(s["kk_sum"], 1)
                    pe.wait_ge(s["rw_ops"], 3)
                    pe.wait_ge(s["lora_act"], 6)
                    pe.wait_ge(s["kk_var"], 1)
                    for n in range(6):
                        p, t = n // 2, n % 2
                        if n >= 2:
                            pe.wait_ge(s["tm_ready"], n - 1)
                        for kind, src in ((BTK, bt[:, p, t * P:(t + 1) * P]), (KTK, kt[:, p, t * P:(t + 1) * P]),
                                          (ATK, ar[:, p, t, 0, :]), (VTK, mixed[:, 6 + p, t * P:(t + 1) * P])):
                            tr = nc.tensor.transpose(bank[2 + n % 2][:, kind * P:(kind + 1) * P], src, ident)
                        tr.then_inc(s["tm_turned"], 1)
                    pe.wait_ge(s["gate_sb"], NT)
                    for n in range(12):
                        p, t, par = n // 4, (n // 2) % 2, n % 2
                        if n >= 2:
                            pe.wait_ge(s["apair_sb"], n - 1)
                        q = slice(64 * par, 64 * par + 64)
                        rhs = ar[q, p, t, :, :].rearrange("p a c -> p (a c)")
                        for o, left in ((0, bt), (256, kt)):
                            mm = nc.tensor.matmul(bank[4 + n % 2][:, o:o + 256], left[q, p, t * P:(t + 1) * P], rhs,
                                                  start=True, stop=True)
                        mm.then_inc(s["apair"], 1)
                    pe.wait_ge(s["rw_ops"], 4)
                    for t in range(NT):
                        for p in range(NPAIR):
                            mm = nc.tensor.matmul(bank[6][:, t * 8 + 2 * p:t * 8 + 2 * p + 2], T2[:, p, t * P:(t + 1) * P],
                                                  const["headsel"], start=True, stop=True)
                    mm.then_inc(s["bonus_out"], 1)

                    pe.wait_ge(s["cum_in"], 1)
                    for t in range(NT):
                        mm = nc.tensor.matmul(bank[0][0:FOX_H, 0:S], fl[:, 3, t, :],
                                              const["cumsel"][:, t * S:(t + 1) * S], start=(t == 0), stop=(t == NT - 1))
                    mm.then_inc(s["cum_out"], 1)

                    pe.wait_ge(s["apair_sb"], 12)
                    pe.wait_ge(s["reset_free"], 5)
                    pe.wait_ge(s["tm_ready"], 6)
                    pe.wait_ge(s["y_taken"], 1)
                    pe.wait_ge(s["cum_sb"], 1)
                    blocks_first(0)
                    attention(0)
                    blocks_first(1)
                    attention(1)
                    blocks_first(2)
                    for lev in range(1, LEVELS):
                        first = lev * NPAIR
                        blocks_z(first)
                        blocks_z(first + 1)
                        attention(2 * lev)
                        blocks_x(first)
                        blocks_z(first + 2)
                        blocks_x(first + 1)
                        att_scores(2 * lev + 1)
                        blocks_x(first + 2)
                        att_outputs(2 * lev + 1)
                    pe.wait_ge(s["x_sb"], LEVELS * 6)
                    for t in range(NT):
                        for p in range(NPAIR):
                            for par in range(2):
                                mm = nc.tensor.matmul(bank[t][:, p * P + par * 64:p * P + par * 64 + 64],
                                                      AT[4 * p + 2 * t + par][:, 256:384],
                                                      tm[:, p, t, VTK, par * 64:par * 64 + 64], start=True, stop=True)
                        mm.then_inc(s["av_out"], 1)
                    def next_mod(n, ks):
                        if ks[0] == 0:
                            pe.wait_ge(s[f"next_w{n}"], 32)
                            if n == 3:
                                pe.wait_ge(s["y_copied"], NT)
                            elif n == 2:
                                pe.wait_ge(s["mod_ready"], 6 + n)
                        for k in ks:
                            mm = nc.tensor.matmul(bank[NEXT_BANK[n]][:, :], crep[:, k, :], next_w[n][k // 4][:, k % 4, :],
                                                  start=(k == 0), stop=(k == KD - 1))
                        if ks[-1] == KD - 1:
                            mm.then_inc(s["pe_out"], 1)

                    def outputs(t):
                        if t:
                            pe.wait_ge(s["y_copied"], t)
                        for p in range(NPAIR):
                            whole = bank[0][:, p * P:(p + 1) * P]
                            for cc in range(2):
                                nc.tensor.matmul(whole, rpad[:, p, t, cc, :], ST[:, 2 * t + cc, p, :],
                                                 start=(cc == 0), stop=False, skip_group_check=True)
                            for par in range(2):
                                half = bank[0][:, p * P + 64 * par:p * P + 64 * par + 64]
                                a = AT[4 * p + 2 * t + par]
                                nc.tensor.matmul(half, a[:, 128:256], SA[:, t, p, 64 * par:64 * par + 64],
                                                 start=False, stop=False, skip_group_check=True)
                                mm = nc.tensor.matmul(half, a[:, 384:512], tm[:, p, t, VTK, 64 * par:64 * par + 64],
                                                      start=False, stop=True, skip_group_check=True)
                        mm.then_inc(s["y_out"], 1)

                    next_mod(0, [0, 1])
                    pe.wait_ge(s["av_sb"], NT)
                    for t in range(NT):
                        if t:
                            next_mod(0, [4, 5])
                            pe.wait_ge(s["uw_sb"], 1)
                        for p in range(NPAIR):
                            for par in range(2):
                                xt = XT[:, p, (2 * t + par) * P:(2 * t + par + 1) * P]
                                nc.tensor.matmul(bank[2][:, p * P + par * 64:p * P + par * 64 + 64], xt,
                                                 AV[:, t, p, par * 64:par * 64 + 64], start=True, stop=True)
                                mm = nc.tensor.matmul(bank[par][:, p * P:(p + 1) * P], tm[:, p, t, ATK, :], xt,
                                                      start=True, stop=True)
                        mm.then_inc(s["uw_out"], 1)
                        next_mod(0, [4 * t + 2, 4 * t + 3])
                    pe.wait_ge(s["uw_sb"], NT)
                    pe.wait_ge(s["rpad"], 2)
                    for cc in range(NC):
                        t, o = cc // 2, slice(64 * (cc % 2), 64 * (cc % 2) + 64)
                        if cc:
                            pe.wait_ge(s["st_sb"], cc)
                        for p in range(NPAIR):
                            mm = nc.tensor.matmul(bank[2][:, p * P:(p + 1) * P], WT[:, t, p, :], ST[:, cc, p, :],
                                                  start=True, stop=True)
                        mm.then_inc(s["sa_out"], 1)
                        att_scores(2 * LEVELS + 2 * cc)
                        if cc:
                            next_mod(1, [2 * cc, 2 * cc + 1])
                        pe.wait_ge(s["sa_sb"], cc + 1)
                        if cc < NC - 1:
                            if cc == 0:
                                pe.wait_ge(s["mod_ready"], 7)
                            for p in range(NPAIR):
                                nc.tensor.matmul(bank[3][:, p * P:(p + 1) * P], tm[o, p, t, KTK, :], tm[o, p, t, VTK, :],
                                                 start=True, stop=False)
                                mm = nc.tensor.matmul(bank[3][:, p * P:(p + 1) * P], tm[o, p, t, BTK, :],
                                                      SA[o, t, p, :], start=False, stop=True)
                            mm.then_inc(s["st_out"], 1)
                        att_outputs(2 * LEVELS + 2 * cc)
                        if cc == NC - 1:
                            outputs(1)
                        attention(2 * LEVELS + 2 * cc + 1)
                        if cc == 0:
                            next_mod(1, [0, 1])
                        if cc == 1:
                            outputs(0)
                    attention(len(units))
                    attention(len(units) + 1)
                    pe.wait_ge(s["o_taken"], len(units))
                    for t in range(NT):
                        turn_pe(pe, hm, "mix_ready", "mix_turned", "mixT_ready", 2, (t,))
                        pe.wait_ge(s["mixT_ready"], 2 * t + 2)
                        for b in range(2):
                            pe.wait_ge(s[f"wout_in{b}"], 16)
                            for k in range(KD):
                                mm = nc.tensor.matmul(bank[4 + 2 * t + b][:, :], hT[:, k, t * P:(t + 1) * P],
                                                      wout[b][:, k, :], start=(k == 0), stop=(k == KD - 1))
                            mm.then_inc(s["mix_out"], 1)
                    next_mod(2, list(range(KD)))
                    next_mod(3, list(range(KD)))

                @block.scalar
                def _(act):
                    junk = t12f[:, 0:1024]
                    norm_act(act, junk)
                    turn_act(act, "h_turned", "hT_ready", 2)
                    dest = {"r": colsT[:, 0:3, 1:], "k": colsT[:, 3:6, 1:], "v": colsT[:, 6:9, 1:], "x": colsT[:, 9:11, 1:],
                            "dq": dq, "dk": dk, "dv": dv, "fqk": fqk, "fv": fv}

                    def take(name):
                        g = [q[0] for q in GROUPS].index(name)
                        w, kind = GROUPS[g][2], GROUPS[g][3]
                        first = COLS[name] - OUTS_OF[g]
                        for j in range(OUTS_OF[g]):
                            m = first + j
                            act.wait_ge(s["pe_out"], proj0 + m + 1)
                            nc.scalar.activation(dest[name][:, j, 0:(S if kind == "f" else w)],
                                                 bank[m % 2][:, 0:(S if kind == "f" else w)],
                                                 ACT.Copy).then_inc(s["cols_ready"], 1)

                    for name in ("r", "k", "v", "x", "dq"):
                        take(name)
                    act.wait_ge(s["rw_ops"], 1)
                    nc.scalar.activation(thx[:], mixed[0:64, 9, :], ACT.Tanh).then_inc(s["act_step"], 1)
                    nc.scalar.activation(sgx[:], mixed[:, 10, :], sig).then_inc(s["act_step"], 1)
                    take("dk")
                    act.wait_ge(s["kk_sq"], 1)
                    act.wait_ge(s["params_in"], 16)
                    for j in range(6):
                        act.wait_ge(s["lora_out"], j + 1)
                        dst = lw[:, j, :] if j < 3 else asig[:, j - 3, :]
                        nc.scalar.activation(dst, bank[2 + j % 2][:, 0:S], sig, bias=pcol[:, PW0 + j:PW0 + j + 1]
                                             ).then_inc(s["lora_act"], 1)
                    for t in range(NT):
                        act.wait_ge(s["gate_out"], t + 1)
                        nc.scalar.activation(gate[:, t, :], bank[4 + t][:, 0:W6], ACT.Copy).then_inc(s["gate_sb"], 1)
                    take("dv")
                    act.wait_ge(s["decay"], 1)
                    nc.scalar.activation(E2, E1, exp).then_inc(s["decay_exp"], 1)
                    nc.scalar.activation(E3, E1, exp, scale=-1.0).then_inc(s["decay_exp"], 1)
                    act.wait_ge(s["decay"], 2)
                    nc.scalar.activation(lw, lw, exp).then_inc(s["decay_exp"], 1)
                    act.wait_ge(s["kk_var"], 1)
                    nc.scalar.activation(T1, T1, ACT.Sqrt).then_inc(s["kk_sd"], 1)
                    take("fqk")
                    take("fv")
                    for n in range(6):
                        act.wait_ge(s["tm_turned"], n + 1)
                        nc.scalar.activation(tm[:, n // 2, n % 2].rearrange("p k c -> p (k c)"), bank[2 + n % 2][:, :],
                                             ACT.Copy).then_inc(s["tm_ready"], 1)
                    act.wait_ge(s["f_in"], 1)
                    nc.scalar.activation(fl[:, 2], fl[:, 1], exp, scale=-1.0).then_inc(s["f_exp"], 1)
                    act.wait_ge(s["lam_in"], 1)
                    nc.scalar.activation(small[:, 2:4], small[:, 0:2], exp).then_inc(s["lam_exp"], 1)
                    act.wait_ge(s["f_exp"], 1)
                    nc.scalar.activation(fl[:, 1], fl[:, 2], ACT.Ln, bias=1.0).then_inc(s["f_ln"], 1)
                    act.wait_ge(s["cum_out"], 1)
                    nc.scalar.activation(cumT[:], bank[0][0:FOX_H, 0:S], ACT.Copy).then_inc(s["cum_sb"], 1)
                    def take_z(u):
                        act.wait_ge(s["z_out"], u - NPAIR + 1)
                        nc.scalar.activation(Z[:, u % NPAIR, :], bank[u % 2][:, :], ACT.Copy).then_inc(s["z_sb"], 1)

                    def attention(n):
                        if n < len(units):
                            kind, h, t = units[n]
                            nk = (t + 1) * P
                            act.wait_ge(s["s_masked"], n + 1)
                            for a in range(2 if kind == "d" else 1):
                                ins = nc.scalar.activation(sc[:, n % 2, a * S:a * S + nk], sc[:, n % 2, a * S:a * S + nk],
                                                           exp, bias=ast[:, n % 2, a:a + 1],
                                                           scale=DIFF_SCALE if kind == "d" else FOX_SCALE,
                                                           accum_out=ast[:, n % 2, 2 + a:3 + a])
                            ins.then_inc(s["s_exp"], 1)
                        if 1 <= n <= len(units):
                            m = n - 1
                            nk = (units[m][2] + 1) * P
                            act.wait_ge(s["p_turned"], m + 1)
                            nc.scalar.activation(pT[:, m % 2, 0:nk], bank[6][:, 0:nk], ACT.Copy).then_inc(s["pT_ready"], 1)
                        if n >= 2:
                            kind, h, t = units[n - 2]
                            c0 = h * HD + (0 if kind == "d" else 2 * W6)
                            act.wait_ge(s["pv_out"], n - 1)
                            nc.scalar.activation(hm[:, t, c0:c0 + HD], bank[7][:, 0:HD], ACT.Copy).then_inc(s["o_taken"], 1)

                    attention(0)
                    attention(1)
                    for lev in range(1, LEVELS):
                        take_z(lev * NPAIR)
                        take_z(lev * NPAIR + 1)
                        attention(2 * lev)
                        take_z(lev * NPAIR + 2)
                        attention(2 * lev + 1)

                    def deviation(t, told_by, tell):
                        act.wait_ge(s[told_by], t + 1)
                        nc.scalar.activation(small[:, 12:18] if t == 0 else small[:, 18:24], small[:, 6:12], ACT.Sqrt
                                             ).then_inc(s[tell], 1)

                    for n in range(2 * LEVELS, len(units) + 2):
                        attention(n)
                        if n == 2 * LEVELS + 3:
                            deviation(0, "o_var", "o_sd")
                        if n == 2 * LEVELS + 5:
                            deviation(1, "o_var", "o_sd")
                        if n == 2 * LEVELS + 6:
                            deviation(0, "y_var", "y_sd")
                    deviation(1, "y_var", "y_sd")
                    turn_act(act, "mix_turned", "mixT_ready", 2)
                    norm_act(act, junk, nth=1)

                @block.vector
                def _(dve):
                    v = nc.vector
                    step = Steps(dve, "dve_step")
                    for t in range(NT):
                        norm_variance(dve, step, t)
                    dve.wait_ge(s["bias_in"], 16)
                    for n in range(6):
                        if n == 4:
                            dve.wait_ge(s["gate_bias_in"], 16)
                        take_mod(dve, step, MOD_ORDER[n], n + 1, n % 2)
                        if n == 1:
                            dve.wait_ge(s["gain_in"], 16)
                            norm_gain(step, gain)
                            for t in range(NT):
                                norm_scaled(dve, step, t)
                        if n == 3:
                            for t in range(NT):
                                step(v.tensor_tensor(hm[:, t, :], hm[:, t, :], mod[:, 0, :], ALU.add), "h_ready")
                    dve.wait_ge(s["small_in"], 16)
                    lprod = ov[:, 0:64].rearrange("p (a b) -> p a b", a=2)
                    step(v.tensor_tensor(lprod, lamp[:, 0:4:2, :], lamp[:, 1:4:2, :], ALU.mult))
                    step(v.tensor_reduce(small[:, 0:2], lprod, AX_X, ALU.add), "lam_in")

                    dve.wait_ge(s["reset_free"], 3)
                    dve.wait_ge(s["params_in"], 16)
                    for name, a, b in (("r", 0, 3), ("k", 3, 6), ("v", 6, 9), ("x", 9, 11)):
                        dve.wait_ge(s["cols_ready"], COLS[name])
                        step(v.tensor_tensor(mixed[:, a:b, :], colsT[:, a:b, 0:S], colsT[:, a:b, 1:S + 1], ALU.subtract))
                        for q in range(a, b):
                            ins = v.scalar_tensor_tensor(out=mixed[:, q, :], in0=mixed[:, q, :],
                                                         scalar=pcol[:, MU + q:MU + q + 1], in1=colsT[:, q, 1:S + 1],
                                                         op0=ALU.mult, op1=ALU.add)
                            if q == 10:
                                step(ins, "rw_ops")
                            else:
                                step(ins)

                    def bc(o):
                        return pcol[:, o:o + 3].rearrange("p (a b) -> p a b", b=1).broadcast_to([P, NPAIR, S])

                    r_, k_, v_ = mixed[:, 0:3, :], mixed[:, 3:6, :], mixed[:, 6:9, :]
                    step(v.tensor_tensor(T2, k_, bc(PKK), ALU.mult))
                    step(v.tensor_tensor(T1, T2, T2, ALU.mult), "kk_sq")
                    dve.wait_ge(s["kk_sum"], 1)
                    step(v.tensor_scalar(T1[:, 0:2, :].rearrange("p a b -> p (a b)"), bank[6][:, :], 1e-24, None, ALU.max))
                    step(v.tensor_scalar(T1[:, 2, :], bank[7][:, 0:S], 1e-24, None, ALU.max), "kk_var")
                    dve.wait_ge(s["lora_act"], 6)
                    step(v.tensor_scalar(lw, lw, -math.exp(-0.5), None, ALU.mult))
                    step(v.tensor_tensor_scan(E1.rearrange("p a b -> p (a b)"), const["reset"],
                                              lw.rearrange("p a b -> p (a b)"), 0.0, ALU.mult, ALU.add), "decay")
                    step(v.tensor_tensor(lw, E1, lw, ALU.subtract), "decay")
                    dve.wait_ge(s["decay_exp"], 3)
                    step(v.tensor_tensor(ar[:, :, :, 1, :], r_.rearrange("p g (t c) -> p g t c", t=NT),
                                         E2.rearrange("p g (t c) -> p g t c", t=NT), ALU.mult), "rw_ops")
                    step(v.scalar_tensor_tensor(out=E1, in0=asig, scalar=-1.0, in1=bc(PKA), op0=ALU.add, op1=ALU.mult))
                    step(v.scalar_tensor_tensor(out=E1, in0=E1, scalar=1.0, in1=k_, op0=ALU.add, op1=ALU.mult))
                    dve.wait_ge(s["kk_sd"], 1)
                    step(v.reciprocal(T1, T1))
                    step(v.scalar_tensor_tensor(out=T2, in0=T2, scalar=-1.0, in1=T1, op0=ALU.mult, op1=ALU.mult))
                    step(v.tensor_tensor(ar[:, :, :, 0, :], T2.rearrange("p g (t c) -> p g t c", t=NT),
                                         lw.rearrange("p g (t c) -> p g t c", t=NT), ALU.mult))
                    step(v.tensor_tensor(kt, E1, E3, ALU.mult))
                    step(v.scalar_tensor_tensor(out=asig, in0=T2, scalar=-1.0, in1=asig, op0=ALU.mult, op1=ALU.mult))
                    step(v.tensor_tensor(bt, asig, E3, ALU.mult), "rw_ops")
                    step(v.tensor_tensor(T2, r_, E1, ALU.mult))
                    step(v.tensor_tensor(T2, T2, bc(PRK), ALU.mult), "rw_ops")
                    dve.wait_ge(s["cols_ready"], nproj)
                    z = fl[:, 0]
                    step(v.tensor_tensor(z, fv[:, :, WF:], bfb.rearrange("p (a b) -> p a b", a=1).broadcast_to([P, NT, FOX_H]), ALU.add))
                    step(v.tensor_scalar(fl[:, 1], z, -1.0, None, ALU.mult))
                    step(v.tensor_tensor(fl[:, 1], fl[:, 1], z, ALU.max), "f_in")
                    for n in range(12):
                        dve.wait_ge(s["apair"], n + 1)
                        step(v.tensor_tensor(AT[n], bank[4 + n % 2][:, :], const["amask"], ALU.mult), "apair_sb")
                    dve.wait_ge(s["f_ln"], 1)
                    step(v.scalar_tensor_tensor(out=fl[:, 3], in0=z, scalar=0.0, in1=fl[:, 1],
                                                op0=ALU.min, op1=ALU.subtract), "cum_in")
                    dve.wait_ge(s["bonus_out"], 1)
                    dve.wait_ge(s["tm_ready"], 6)
                    step(v.tensor_copy(bon[:], bank[6][:, 0:16].rearrange("p (t h) -> p t h", t=NT)[:, :, 0:RW_H]), "y_taken")
                    for t in range(NT):
                        step(v.tensor_tensor(bv[:, t, :].rearrange("p (g a d) -> p g a d", g=NPAIR, a=2),
                                             tm[:, :, t, VTK, :].rearrange("p g (a d) -> p g a d", a=2),
                                             bon[:, t, :].rearrange("p (g a o) -> p g a o", g=NPAIR, o=1).broadcast_to([P, NPAIR, 2, HD]),
                                             ALU.mult), "y_taken")
                    dve.wait_ge(s["lam_exp"], 1)
                    step(v.tensor_tensor(small[:, 4:5], small[:, 3:4], small[:, 2:3], ALU.subtract))
                    step(v.tensor_tensor(small[:, 4:5], small[:, 4:5], lamc[:, 0:1], ALU.subtract))
                    step(v.tensor_scalar(subg, subg, lamc[:, 1:2], None, ALU.mult))

                    def mask4(name, lev):
                        a = const[name][:, lev * P:(lev + 1) * P].rearrange("p (o c) -> p o c", o=1)
                        return a.broadcast_to([P, 4, P]).bitcast(I32)

                    def four(a):
                        return a.rearrange("p (j c) -> p j c", j=4)

                    def take_x(u):
                        lev, p = u // NPAIR, u % NPAIR
                        dve.wait_ge(s["xz_out"], u + 1)
                        if lev < LEVELS - 1:
                            step(v.copy_predicated(four(X[:, p, :]), mask4("xmask", lev), four(bank[2][:, :])), "x_sb")
                        else:
                            step(v.tensor_copy(stat[:, 8:9], stat[:, 6:7]), "x_sb")
                        new = four(bank[3][:, :]) if lev else \
                            ringf[:, p * 2048:(p + 1) * 2048].rearrange("p (j c) -> p j c", j=4)[:, :, 0:P]
                        step(v.copy_predicated(four(XT[:, p, :]), mask4("xtmask", lev), new), "x_sb")

                    def attention(n):
                        divide(n)
                        mask(n)

                    def divide(n):
                        if 1 <= n <= len(units):
                            m = n - 1
                            kind, h, t = units[m]
                            nk = (t + 1) * P
                            st = ast[:, m % 2, :]
                            na = 2 if kind == "d" else 1
                            dve.wait_ge(s["s_exp"], m + 1)
                            step(v.reciprocal(st[:, 4:4 + na], st[:, 2:2 + na]))
                            if kind == "d":
                                step(v.tensor_tensor(st[:, 5:6], st[:, 5:6], small[:, 4:5], ALU.mult))
                                step(v.tensor_scalar(sc[:, m % 2, 0:nk], sc[:, m % 2, 0:nk], st[:, 4:5], None, ALU.mult))
                                step(v.scalar_tensor_tensor(out=pn[:, m % 2, 0:nk], in0=sc[:, m % 2, S:S + nk],
                                                            scalar=st[:, 5:6], in1=sc[:, m % 2, 0:nk],
                                                            op0=ALU.mult, op1=ALU.add), "p_ready")
                            else:
                                step(v.tensor_scalar(pn[:, m % 2, 0:nk], sc[:, m % 2, 0:nk], st[:, 4:5], None, ALU.mult),
                                     "p_ready")

                    def mask(n):
                        if n < len(units):
                            kind, h, t = units[n]
                            nk = (t + 1) * P
                            na = 2 if kind == "d" else 1
                            a_ = sc[:, n % 2, :].rearrange("p (a c) -> p a c", a=2)[:, 0:na, 0:nk]
                            st = ast[:, n % 2, :]
                            dve.wait_ge(s["s_out"], n + 1)
                            for a in range(na):
                                step(v.tensor_tensor(a_[:, a, :], bank[4 + a][:, 0:nk], const["causal"][:, S - nk:S], ALU.add))
                            step(v.tensor_reduce(st[:, 0:na], a_, AX_X, ALU.max))
                            step(v.tensor_scalar(st[:, 0:na], st[:, 0:na], -(DIFF_SCALE if kind == "d" else FOX_SCALE), None,
                                                 ALU.mult), "s_masked")

                    take_x(0)
                    attention(0)
                    take_x(1)
                    attention(1)
                    take_x(2)
                    for lev in range(1, LEVELS):
                        attention(2 * lev)
                        take_x(lev * NPAIR)
                        divide(2 * lev + 1)
                        take_x(lev * NPAIR + 1)
                        mask(2 * lev + 1)
                        take_x(lev * NPAIR + 2)
                    for t in range(NT):
                        dve.wait_ge(s["av_out"], t + 1)
                        step(v.tensor_copy(AV[:, t].rearrange("p g c -> p (g c)"), bank[t][:, 0:W6]), "av_sb")
                    for t in range(NT):
                        dve.wait_ge(s["uw_out"], t + 1)
                        step(v.tensor_copy(U[:, t].rearrange("p g c -> p (g c)"), bank[2][:, 0:W6]))
                        for par in range(2):
                            q = slice(64 * par, 64 * par + 64)
                            ins = v.tensor_copy(WT[q, t].rearrange("p g c -> p (g c)"), bank[par][q, 0:W6])
                            step(ins, "uw_sb") if par else step(ins)

                    def head6(a):
                        return a.rearrange("p (h d) -> p h d", h=6)

                    def col6(a):
                        return a.rearrange("p (h o) -> p h o", o=1).broadcast_to([P, 6, HD])

                    def diff_norm(t):
                        dve.wait_ge(s["o_taken"], 2 * DIFF_H)
                        o = hm[:, t, 0:W6]
                        step(v.tensor_tensor(ov, o, o, ALU.mult))
                        step(v.tensor_reduce(small[:, 6:12], head6(ov), AX_X, ALU.add))
                        step(v.tensor_scalar(small[:, 6:12], small[:, 6:12], 1.0 / HD, RMS_EPS, ALU.mult, ALU.add), "o_var")
                        dve.wait_ge(s["o_sd"], t + 1)
                        sd = small[:, 12:18] if t == 0 else small[:, 18:24]
                        step(v.reciprocal(sd, sd))
                        step(v.tensor_tensor(head6(o), head6(o), col6(sd), ALU.mult))
                        step(v.tensor_tensor(head6(o), head6(o), subg.rearrange("p (o d) -> p o d", o=1)
                                             .broadcast_to([P, 6, HD]), ALU.mult))

                    def copy_y(t):
                        dve.wait_ge(s["y_out"], t + 1)
                        step(v.tensor_copy(hm[:, t, W6:2 * W6], bank[0][:, 0:W6]), "y_copied")

                    def y_variance(t):
                        y = hm[:, t, W6:2 * W6]
                        step(v.tensor_reduce(small[:, 6:12], head6(y), AX_X, ALU.add))
                        step(v.tensor_scalar(small[:, 6:12], small[:, 6:12], 1.0 / HD, None, ALU.mult))
                        step(v.tensor_tensor(head6(y), head6(y), col6(small[:, 6:12]), ALU.subtract))
                        step(v.tensor_tensor(ov, y, y, ALU.mult))
                        step(v.tensor_reduce(small[:, 6:12], head6(ov), AX_X, ALU.add))
                        step(v.tensor_scalar(small[:, 6:12], small[:, 6:12], 1.0 / HD, LN_EPS, ALU.mult, ALU.add), "y_var")

                    def y_norm(t):
                        y = hm[:, t, W6:2 * W6]
                        dve.wait_ge(s["y_sd"], t + 1)
                        sd = small[:, 12:18] if t == 0 else small[:, 18:24]
                        step(v.reciprocal(sd, sd))
                        step(v.tensor_tensor(head6(y), head6(y), col6(sd), ALU.mult))
                        step(v.tensor_tensor(y, y, prow[:, LNG:LNG + W6], ALU.mult))
                        step(v.tensor_tensor(y, y, prow[:, LNB:LNB + W6], ALU.add))
                        step(v.tensor_tensor(y, y, bv[:, t, :], ALU.add))
                        step(v.tensor_tensor(y, y, gate[:, t, :], ALU.mult), "mix_ready")

                    def take_next(n):
                        take_mod(dve, step, MOD_ORDER[n], proj0 + nproj + n + 1, NEXT_BANK[n])

                    dve.wait_ge(s["gate_sb"], NT)
                    dve.wait_ge(s["bias_in"], 32)
                    take_next(0)
                    for cc in range(NC):
                        t, o = cc // 2, slice(64 * (cc % 2), 64 * (cc % 2) + 64)
                        dve.wait_ge(s["sa_out"], cc + 1)
                        step(v.tensor_tensor(SA[o, t].rearrange("p g c -> p (g c)"), bank[2][o, 0:W6],
                                             U[o, t].rearrange("p g c -> p (g c)"), ALU.add), "sa_sb")
                        if cc == 2:
                            copy_y(0)
                        divide(2 * LEVELS + 2 * cc)
                        if cc < NC - 1:
                            dve.wait_ge(s["st_out"], cc + 1)
                            step(v.tensor_tensor(stmp, bank[3][:, 0:W6].rearrange("p (g c) -> p g c", g=NPAIR),
                                                 ST[:, cc], ALU.add))
                            last = E2[:, :, cc * C + C - 1:cc * C + C]
                            step(v.tensor_tensor(stmp, stmp, last.broadcast_to([P, NPAIR, P]), ALU.mult))
                            step(v.tensor_tensor(ST[:, cc + 1], stmp, pairones.rearrange("p (o c) -> p o c", o=1)
                                                 .broadcast_to([P, NPAIR, P]), ALU.mult), "st_sb")
                        mask(2 * LEVELS + 2 * cc)
                        if cc == NC - 1:
                            y_variance(0)
                        attention(2 * LEVELS + 2 * cc + 1)
                        if cc in (1, 2):
                            diff_norm(cc - 1)
                    copy_y(1)
                    attention(len(units))
                    y_norm(0)
                    take_next(1)
                    y_variance(1)
                    y_norm(1)
                    dve.wait_ge(s["gain_in"], 32)
                    norm_gain(step, gainf)
                    for t in range(NT):
                        for b in range(2):
                            dve.wait_ge(s["mix_out"], 2 * t + b + 1)
                            q = slice(b * 512, (b + 1) * 512)
                            step(v.tensor_tensor(hm[:, t, q], bank[4 + 2 * t + b][:, :], mod[:, 2, q], ALU.mult))
                            ins = v.tensor_tensor(xs[:, t, q], xs[:, t, q], hm[:, t, q], ALU.add)
                            step(ins, "x_done") if b else step(ins)
                    for t in range(NT):
                        norm_variance(dve, step, t, nth=1)
                    for t in range(NT):
                        norm_scaled(dve, step, t, nth=1)
                    for n in (2, 3):
                        take_next(n)
                        q = slice((n - 2) * 512, (n - 1) * 512)
                        for t in range(NT):
                            step(v.tensor_tensor(hm[:, t, q], hm[:, t, q], mod[:, 0, q], ALU.add))

            nc.all_engine_barrier(sems_to_clear=clearable)

            with ExitStack() as peer, nc.Block() as block:
                whead = sb("whead", [P, 2, KD, 256], where=peer)
                qh = sb("qh", [P, 2, 2, S], where=peer)
                diag = sb("diag", [P, len(PE_ROWS), P], where=peer)
                skT = sb("skT", [P, 2 * PH, P], where=peer)
                score = sb("score", [P, NT, 2 * PH, NK], where=peer)
                top = sb("top", [P, 2 * PH, TOPK], where=peer)
                topi = sb("topi", [P, 2 * PH, TOPK], U32, where=peer)
                topf = sb("topf", [P, 2 * PH, TOPK], where=peer)
                cand = sb("cand", [P, 3, TOPK * TOPK], where=peer)
                fval = sb("fval", [P, NT, PH, TOPK], where=peer)
                fpos = sb("fpos", [P, TOPK], U32, where=peer)
                fhi = sb("fhi", [P, 2, TOPK], U32, where=peer)
                ff = sb("ff", [P, 2, TOPK], where=peer)
                eid = sb("eid", [P, 3, TOPK], where=peer)
                eidx = sb("eidx", [P, NT, SEL], I32, where=peer)
                zidx = sb("zidx", [P, RING], I32, where=peer)
                islot = sb("islot", [P, 2, RING], I32, where=peer)
                gsum = sb("gsum", [P, NT, 2, PH], where=peer)
                dots = sb("dots", [P, NT, SEL], where=peer)
                coef = sb("coef", [P, NT, SEL], where=peer)
                accv = sb("accv", [P, NT, D], where=peer)
                zdiag = sb("zdiag", [P, P], where=peer)
                ROUNDS = SEL // RING

                @block.sync
                def _(sp):
                    wq = peer_wq[bass.ds(l, 1)].rearrange("o (k p) n -> p (o k) n", p=P)
                    ada = ada_w[bass.ds(l, 1)].rearrange("o (k p) n -> p (o k) n", p=P)
                    for n in range(PH + 4):
                        if 2 <= n < PH + 2:
                            sp.wait_ge(s["q_out"], 2 * (n - 1))
                        elif n >= PH + 2:
                            sp.wait_ge(s["gf_out"], n - PH - 1)
                        src = wq[:, :, n * 256:(n + 1) * 256] if n < PH else \
                            ada[:, :, 5 * D + (n - PH) * 256:5 * D + (n - PH + 1) * 256]
                        sp.dma_start(whead[:, n % 2], src).then_inc(s[f"w_in{n % 2}"], 16)
                        if n == 0:
                            sp.dma_start(skT[:].rearrange("p a b -> p (a b)"), subkeys_t[bass.ds(l, 1)].rearrange(
                                "o p n -> (o p) n")).then_inc(s["small_in"], 16)
                        if n == 1:
                            load_bias(sp, l, 1, slice(2, 3))

                @block.tensor
                def _(pe):
                    turn_pe(pe, hm, None, "h_turned", "hT_ready", 2)
                    pe.wait_ge(s["hT_ready"], 4)
                    for h in range(PH):
                        pe.wait_ge(s[f"w_in{h % 2}"], 16 * (h // 2 + 1))
                        for cc in range(2):
                            m = 2 * h + cc
                            if m >= 2:
                                pe.wait_ge(s["q_ready"], m - 1)
                            for k in range(KD):
                                mm = nc.tensor.matmul(bank[cc][:, 0:S], whead[:, h % 2, k, cc * P:(cc + 1) * P], hT[:, k, :],
                                                      start=(k == 0), stop=(k == KD - 1))
                            mm.then_inc(s["q_out"], 1)
                        pe.wait_ge(s["q_ready"], 2 * h + 2)
                        if h == 0:
                            pe.wait_ge(s["small_in"], 16)
                        if h >= 2:
                            pe.wait_ge(s["score_taken"], h - 1)
                        for t in range(NT):
                            for cc in range(2):
                                mm = nc.tensor.matmul(bank[4 + h % 2][:, (2 * t + cc) * P:(2 * t + cc + 1) * P],
                                                      qh[:, h % 2, cc, t * P:(t + 1) * P], skT[:, 2 * h + cc, :],
                                                      start=True, stop=True)
                        mm.then_inc(s["score_out"], 1)
                    for n in range(4):
                        pe.wait_ge(s[f"w_in{n % 2}"], 16 * (PH // 2 + n // 2 + 1))
                        if n >= 2:
                            pe.wait_ge(s["gf_taken"], n - 1)
                        for k in range(KD):
                            mm = nc.tensor.matmul(bank[2 + n % 2][:, 0:256], crep[:, k, :], whead[:, n % 2, k, :],
                                                  start=(k == 0), stop=(k == KD - 1))
                        mm.then_inc(s["gf_out"], 1)
                    pe.wait_ge(s["zero_diag"], 1)
                    for t in range(NT):
                        if t:
                            pe.wait_ge(s["pe_sum_taken"], t)
                        for b in range(2):
                            nc.tensor.matmul(bank[6 + b][:, :], zdiag[:], hT[:, 0:2, :].rearrange("p a c -> p (a c)"),
                                             start=True, stop=False, skip_group_check=True)
                        with pe.Fori(0, ROUNDS) as r:
                            pe.wait_ge(s["diag_ready"], r + (t * ROUNDS + 1))
                            for i, j in enumerate(PE_ROWS):
                                pe.wait_ge(row_landed[j], l * (2 * NT * ROUNDS * 16) + r * 16 + ((2 * t + 1) * ROUNDS * 16 + 16))
                                for b in range(2):
                                    mm = nc.tensor.matmul(bank[6 + b][:, :], diag[:, i, :], ringmem[:, j, b * 512:(b + 1) * 512],
                                                          start=False, stop=False, skip_group_check=True)
                                mm.then_inc(slot_free[j], 1)

                @block.scalar
                def _(act):
                    turn_act(act, "h_turned", "hT_ready", 2)
                    for m in range(2 * PH):
                        act.wait_ge(s["q_out"], m + 1)
                        if m >= 4:
                            act.wait_ge(s["score_out"], m // 2 - 1)
                        nc.scalar.activation(qh[:, m // 2 % 2, m % 2, :], bank[m % 2][:, 0:S], ACT.Copy).then_inc(s["q_ready"], 1)
                    for t in range(NT):
                        act.wait_ge(s["gate_max"], t + 1)
                        nc.scalar.activation(coef[:, t, :], coef[:, t, :], exp).then_inc(s["gate_exp"], 1)
                        act.wait_ge(s["act_in"], t + 1)
                        nc.scalar.activation(dots[:, t, :], dots[:, t, :], gelu).then_inc(s["gelu_out"], 1)
                        act.wait_ge(s["coef_ready"], t + 1)
                        with act.Fori(0, ROUNDS) as r:
                            for j in PE_ROWS[-1:]:
                                act.wait_ge(slot_free[j], r + ((2 * t + 1) * ROUNDS + 1))
                                act.sem_inc(s["act_pass"], 1)
                            for i, j in enumerate(PE_ROWS):
                                ins = nc.scalar.activation(diag[:, i, :], ident, ACT.Copy,
                                                           scale=coef[:, t, bass.ds(r * RING + j, 1)])
                            ins.then_inc(s["diag_ready"], 1)

                @block.gpsimd
                def _(pool):
                    nc.gpsimd.memset(accv[:], 0.0).then_inc(s["acc_zero"], 1)
                    for ph in range(2 * NT):
                        t, table = ph // 2, (peer_u, peer_v)[ph % 2]
                        rows = table.rearrange("a e d -> (a e) d")
                        with pool.Fori(0, ROUNDS // 2) as rr:
                            for half in range(2):
                                rnd = rr * 2 + (half + ph * ROUNDS)
                                if ph % 2 == 0:
                                    pool.wait_ge(s["idx_ready"], rr * 2 + (half + t * PH + 1))
                                    pool.sem_inc(s["pool_pass"], 1)
                                pool.wait_ge(slot_free[0], rnd + 1)
                                nc.gpsimd.tensor_tensor(islot[:, half, :], eidx[:, t, bass.ds(rr * (2 * RING) + half * RING, RING)],
                                                        zidx[:], ALU.add).then_inc(s["idx_step"], 1)
                                pool.wait_ge(s["idx_step"], rr * 2 + (half + ph * ROUNDS + 1))
                                pool.sem_inc(s["pool_pass"], 1)
                                for j in range(RING):
                                    if j:
                                        pool.wait_ge(slot_free[j], rnd + 1)
                                        pool.sem_inc(s["pool_pass"], 1)
                                    nc.gpsimd.indirect_dma_start(ringmem[:, j, :], None, rows,
                                                                 bass.IndirectOffsetOnAxis(ap=islot[:, half, j:j + 1], axis=0)
                                                                 ).then_inc(row_landed[j], 16)

                @block.vector
                def _(dve):
                    v = nc.vector
                    step = Steps(dve, "dve_step")
                    step(v.memset(zidx[:], 0))
                    step(v.memset(zdiag[:], 0.0), "zero_diag")

                    def top16(vals, idxs, src):
                        step(v.max(vals[:, 0:8], src))
                        step(v.max_index(idxs[:, 0:8], vals[:, 0:8], src))
                        step(v.match_replace(src, vals[:, 0:8], src, BIG * 1e8))
                        step(v.max(vals[:, 8:16], src))
                        step(v.max_index(idxs[:, 8:16], vals[:, 8:16], src))

                    def take_scores(h):
                        dve.wait_ge(s["score_out"], h + 1)
                        step(v.tensor_copy(score[:, :, 2 * h:2 * h + 2, :],
                                           bank[4 + h % 2][:, :].rearrange("p (t a n) -> p t a n", t=NT, a=2)), "score_taken")

                    def retrieve(t, h):
                        for hc in (2 * h, 2 * h + 1):
                            top16(top[:, hc, :], topi[:, hc, :], score[:, t, hc, :])
                        step(v.tensor_copy(topf[:, 2 * h:2 * h + 2, :], topi[:, 2 * h:2 * h + 2, :]))
                        a = top[:, 2 * h, :].rearrange("p (i o) -> p i o", o=1).broadcast_to([P, TOPK, TOPK])
                        b = top[:, 2 * h + 1, :].rearrange("p (o j) -> p o j", o=1).broadcast_to([P, TOPK, TOPK])
                        step(v.tensor_tensor(cand[:, 0, :].rearrange("p (i j) -> p i j", i=TOPK), a, b, ALU.add))
                        top16(fval[:, t, h, :], fpos[:], cand[:, 0, :])
                        step(v.tensor_scalar(fhi[:, 0, :], fpos[:], 4, None, ALU.logical_shift_right))
                        step(v.tensor_scalar(fhi[:, 1, :], fpos[:], 15, None, ALU.bitwise_and))
                        step(v.tensor_copy(ff[:], fhi[:]))
                        oh = cand[:, 1:3, :].rearrange("p a (k i) -> p a k i", k=TOPK)
                        f4 = ff[:].rearrange("p a (k o) -> p a k o", o=1).broadcast_to([P, 2, TOPK, TOPK])
                        io = const["iota"].rearrange("p (a b i) -> p a b i", a=1, b=1).broadcast_to([P, 2, TOPK, TOPK])
                        step(v.tensor_tensor(oh, f4, io, ALU.is_equal))
                        ix = topf[:, 2 * h:2 * h + 2, :].rearrange("p a (o i) -> p a o i", o=1).broadcast_to([P, 2, TOPK, TOPK])
                        step(v.tensor_tensor(oh, oh, ix, ALU.mult))
                        step(v.tensor_reduce(eid[:, 0:2, :], oh, AX_X, ALU.add))
                        step(v.scalar_tensor_tensor(out=eid[:, 2, :], in0=eid[:, 0, :], scalar=float(NK), in1=eid[:, 1, :],
                                                    op0=ALU.mult, op1=ALU.add))
                        step(v.tensor_scalar(eidx[:, t, h * TOPK:(h + 1) * TOPK], eid[:, 2, :], ebase[:, 0:1], None,
                                             ALU.add), "idx_ready")

                    def gates(t):
                        c3 = coef[:, t, :].rearrange("p (h k) -> p h k", h=PH)
                        step(v.tensor_tensor(c3, fval[:, t], fval[:, t, :, 0:1].broadcast_to([P, PH, TOPK]),
                                             ALU.subtract), "gate_max")
                        dve.wait_ge(s["gate_exp"], t + 1)
                        step(v.tensor_reduce(gsum[:, t, 0, :], c3, AX_X, ALU.add))
                        step(v.reciprocal(gsum[:, t, 1, :], gsum[:, t, 0, :]))
                        step(v.tensor_tensor(c3, c3, gsum[:, t, 1, :].rearrange("p (h o) -> p h o", o=1)
                                             .broadcast_to([P, PH, TOPK]), ALU.mult))

                    def row(ph, r, j):
                        t = ph // 2
                        if ph % 2 and j in PE_ROWS:
                            return
                        dve.wait_ge(row_landed[j], l * (2 * NT * ROUNDS * 16) + r * 16 + (ph * ROUNDS * 16 + 16))
                        k = r * RING + j
                        col = slice(k, k + 1) if isinstance(r, int) else bass.ds(k, 1)
                        if ph % 2 == 0:
                            ins = v.scalar_tensor_tensor(out=ringmem[:, j, :], in0=ringmem[:, j, :], scalar=1.0,
                                                         in1=hm[:, t, :], op0=ALU.mult, op1=ALU.mult,
                                                         accum_out=dots[:, t, col])
                            ins.then_inc(slot_free[j], 1)
                            return
                        at = DVE_ROWS.index(j)
                        dve.wait_ge(slot_free[DVE_ROWS[at - 1]], r + (ph * ROUNDS + (2 if at else 1)))
                        ins = v.scalar_tensor_tensor(out=accv[:, t, :], in0=ringmem[:, j, :], scalar=coef[:, t, col],
                                                     in1=accv[:, t, :], op0=ALU.mult, op1=ALU.add)
                        ins.then_inc(slot_free[j], 1)

                    def rows(ph):
                        with dve.Fori(0, ROUNDS) as r:
                            for j in range(RING):
                                row(ph, r, j)

                    def coefficients(t):
                        for j in range(RING):
                            dve.wait_ge(slot_free[j], (2 * t + 1) * ROUNDS + 1)
                        step(v.memset(stat[:, 9:10], 0.0), "act_in")
                        dve.wait_ge(s["gelu_out"], t + 1)
                        step(v.tensor_tensor(coef[:, t, :], coef[:, t, :], dots[:, t, :], ALU.mult), "coef_ready")

                    def take_pe_sum(t):
                        for j in range(RING):
                            dve.wait_ge(slot_free[j], (2 * t + 2) * ROUNDS + 1)
                        for b in range(2):
                            q = slice(512 * b, 512 * (b + 1))
                            ins = v.tensor_tensor(accv[:, t, q], accv[:, t, q], bank[6 + b][:, :], ALU.add)
                            step(ins, "pe_sum_taken") if b else step(ins)

                    def take_gate_mod(n):
                        dve.wait_ge(s["gf_out"], n + 1)
                        part = mod[:, 2, 256 * n:256 * (n + 1)]
                        step(v.tensor_tensor(part, bank[2 + n % 2][:, 0:256], part, ALU.add), "gf_taken")

                    def add_sum(t):
                        step(v.tensor_tensor(accv[:, t, :], accv[:, t, :], mod[:, 2, :], ALU.mult))
                        step(v.tensor_tensor(xs[:, t, :], xs[:, t, :], accv[:, t, :], ALU.add))

                    for j in range(RING):
                        dve.sem_inc(slot_free[j], 1)
                    dve.wait_ge(s["bias_in"], 16)
                    take_scores(0)
                    retrieve(0, 0)
                    for h in range(PH):
                        if h + 1 < PH:
                            take_scores(h + 1)
                            retrieve(0, h + 1)
                        else:
                            gates(0)
                        for j in range(TOPK):
                            row(0, h, j)
                        if h >= PH - 2:
                            take_gate_mod(2 * (h - PH + 2))
                            take_gate_mod(2 * (h - PH + 2) + 1)
                    coefficients(0)
                    dve.wait_ge(s["acc_zero"], 1)
                    for h in range(PH):
                        for j in range(TOPK):
                            row(1, h, j)
                        retrieve(1, h)
                    gates(1)
                    take_pe_sum(0)
                    rows(2)
                    coefficients(1)
                    add_sum(0)
                    rows(3)
                    take_pe_sum(1)
                    add_sum(1)
                    step(v.tensor_scalar(ebase[:], ebase[:], float(EXPERTS), None, ALU.add))

            nc.all_engine_barrier(sems_to_clear=clearable)

        with ExitStack() as end, nc.Block() as block:
            fg = sb("fg", [P, D], where=end)

            @block.sync
            def _(sp):
                sp.dma_start(fg[:], final_norm_g.rearrange("(o d) -> o d", o=1).broadcast_to([P, D])).then_inc(s["gain_in"], 16)
                for t in range(NT):
                    sp.wait_ge(s["h_ready"], t + 1)
                    sp.dma_start(out.rearrange("o (t p) d -> p (o t) d", p=P)[:, t, :], hm[:, t, :]).then_inc(s["stored"], 16)
                sp.wait_ge(s["stored"], 16 * NT)

            @block.scalar
            def _(act):
                norm_act(act, hm[:, 0, :])

            @block.vector
            def _(dve):
                step = Steps(dve, "dve_step")
                for t in range(NT):
                    dve.wait_ge(s["ss_ready"], t + 1)
                    step(nc.vector.tensor_scalar(stat[:, 2 + t:3 + t], stat[:, t:t + 1], 1.0 / D, RMS_EPS,
                                                 ALU.mult, ALU.add), "var_ready")
                dve.wait_ge(s["gain_in"], 16)
                for t in range(NT):
                    dve.wait_ge(s["sd_ready"], t + 1)
                    step(nc.vector.reciprocal(stat[:, 6 + t:7 + t], stat[:, 4 + t:5 + t]))
                    step(nc.vector.scalar_tensor_tensor(out=hm[:, t, :], in0=xs[:, t, :], scalar=stat[:, 6 + t:7 + t],
                                                        in1=fg[:], op0=ALU.mult, op1=ALU.mult), "h_ready")


def shape_constants():
    import numpy as np
    a = np.zeros((P, CONSTS), np.float32)

    def put(name, value):
        lo, hi = _off[name]
        a[:, lo:hi] = np.asarray(value, np.float32).reshape(P, hi - lo)

    i = np.arange(P)
    row, col = i[:, None], i[None, :]
    put("ident", row == col)
    same = row // C == col // C
    strict, upto = same & (row < col), same & (row <= col)
    put("amask", np.stack([strict, upto, strict, upto], 1))
    lower = []
    for lev in range(LEVELS):
        b = 1 << lev
        lower.append((row // (2 * b) == col // (2 * b)) & (row // b % 2 == 1) & (col // b % 2 == 0))
    put("xmask", np.stack(lower, 1))
    put("xtmask", np.stack([m.T for m in lower], 1))
    put("pairones", row // HD == col // HD)
    put("headsel", row // HD == np.arange(2)[None, :])
    tok = np.arange(S)[None, :]
    put("cumsel", np.stack([row + P * t <= tok for t in range(NT)], 1))
    put("reset", np.broadcast_to(np.arange(NPAIR * S) % C != 0, (P, NPAIR * S)))
    put("causal", np.concatenate([np.zeros((P, P)), np.where(col > row, BIG, 0.0)], 1))
    fs = np.zeros((P, FOX_H, P))
    for h in range(FOX_H):
        fs[h, h, :] = -1.0 / FOX_SCALE
    put("foxsel", fs)
    put("iota", np.broadcast_to(np.arange(TOPK), (P, TOPK)))
    lam = np.array([0.8 - 0.6 * math.exp(-0.3 * d) for d in range(DEPTH)])
    return a, np.stack([lam, 1.0 - lam], 1).astype(np.float32)


def laid_out(a, lam_consts):
    import numpy as np
    cols = [a[n].reshape(DEPTH, -1, P) for n in ("rw_mu", "rw_w0", "rw_a0", "rw_kk", "rw_ka", "rw_rk")]
    rows = [a[n].reshape(DEPTH, -1) for n in ("rw_ln_g", "rw_ln_b", "dif_subln_g", "dif_lam")]
    return {
        "c_cols": a["c"].reshape(KD, P).T,
        "param_cols": np.concatenate(cols, 1).transpose(0, 2, 1),
        "param_rows": np.concatenate(rows + [lam_consts, a["fox_bf"].reshape(DEPTH, -1)], 1),
        "lora_w": np.concatenate([np.concatenate([a["rw_w2"], a["rw_a2"]], 1), a["rw_g2"]], 2),
        "subkeys_t": a["peer_subkeys"].reshape(DEPTH, 2 * PH, NK, P).transpose(0, 3, 1, 2).reshape(DEPTH, P, -1),
    }


_INS = ["x", "c_cols", "norm_mix_g", "norm_ffn_g", "final_norm_g", "ada_w", "ada_b", "w_in", "w_out", "param_cols",
        "param_rows", "lora_w", "peer_wq", "subkeys_t", "peer_u", "peer_v", "consts"]


def kernel(**inputs):
    import numpy as _np
    import concourse.bacc as _bacc
    from concourse import mybir as _mybir
    from concourse.bass_utils import run_bass_kernel_spmd as _run

    nc = _bacc.Bacc("TRN2", target_bir_lowering=False, num_devices=1)
    arrays, args = {}, []
    consts, lam_consts = shape_constants()
    data = dict(inputs, consts=consts, **laid_out(inputs, lam_consts))
    for name in _INS:
        a = _np.ascontiguousarray(data[name])
        arrays[f"in_{name}_dram"] = a
        args.append(nc.dram_tensor(f"in_{name}_dram", a.shape, _mybir.dt.from_np(a.dtype), kind="ExternalInput").ap())
    args.append(nc.dram_tensor("out_0_dram", (1, S, D), _mybir.dt.float32, kind="ExternalOutput").ap())
    trunk(nc, *args)
    r = _run(nc, [arrays], core_ids=[0])
    return r.results[0]["out_0_dram"]
```
